# Optimizing a Trainium2 kernel written in Bass

```python
import jax, jax.numpy as jnp
from jax import lax
import numpy as np
import math

D_MODEL = 2048
BATCH = 1
SEQ = 256
DEPTH = 1

A_HEADS = 8
A_HEAD_DIM = 128
A_WIDTH = A_HEADS * A_HEAD_DIM
MOBA_BLOCK = 256
MOBA_TOPK = 3
MOBA_QBLOCK = 64
R_HEADS = 4
R_QK_DIM = 256
R_V_DIM = 512
R_QK_WIDTH = R_HEADS * R_QK_DIM
R_V_WIDTH = R_HEADS * R_V_DIM
R_CHUNK = 256
_FF_RAW = -(-8 * D_MODEL // 3)
D_FF = -(-_FF_RAW // 256) * 256
EPS = 1e-6
SEQ_ALIGN = 256


def _split_points():
    sizes = [A_WIDTH] * 3 + [R_QK_WIDTH] * 2 + [R_V_WIDTH] * 2 + [D_MODEL] * 2
    pts, acc = [], 0
    for s in sizes[:-1]:
        acc += s
        pts.append(acc)
    return pts, acc + sizes[-1]

def rms_norm(x, g):
    xf = x.astype(jnp.float32)
    y = xf * lax.rsqrt(jnp.mean(xf * xf, axis=-1, keepdims=True) + EPS)
    return (y * g.astype(jnp.float32)).astype(x.dtype)

def head_group_norm(y):
    yf = y.astype(jnp.float32)
    mu = jnp.mean(yf, axis=-1, keepdims=True)
    var = jnp.mean(jnp.square(yf - mu), axis=-1, keepdims=True)
    return ((yf - mu) * lax.rsqrt(var + EPS)).astype(y.dtype)

def alibi_slopes(n):
    start = 2.0 ** (-8.0 / n)
    return jnp.array([start ** (i + 1) for i in range(n)], dtype=jnp.float32)

def moba_attention(q, k, v):
    B, H, S, d = q.shape
    nb = S // MOBA_BLOCK
    topk = min(MOBA_TOPK, nb)
    kb = k.reshape(B, H, nb, MOBA_BLOCK, d)
    vb = v.reshape(B, H, nb, MOBA_BLOCK, d)
    kmean = jnp.mean(kb.astype(jnp.float32), axis=3).astype(k.dtype)
    slopes = alibi_slopes(H)[None, :, None, None]
    scale = d ** -0.5
    blk_ids = jnp.arange(nb)
    offs = jnp.arange(MOBA_BLOCK)
    gather = jax.vmap(jax.vmap(lambda blocks, idx: blocks[idx]))

    def one_qblock(c):
        start = c * MOBA_QBLOCK
        qc = lax.dynamic_slice_in_dim(q, start, MOBA_QBLOCK, axis=2)
        t = start + jnp.arange(MOBA_QBLOCK)
        cur = start // MOBA_BLOCK
        gate = jnp.einsum('bhqd,bhnd->bhqn', qc, kmean).astype(jnp.float32)
        gate = jnp.where(blk_ids < cur, gate, -jnp.inf)
        _, sel = lax.top_k(gate, topk)
        valid = sel < cur
        kg = gather(kb, sel)
        vg = gather(vb, sel)
        s_past = jnp.einsum('bhqd,bhqjsd->bhqjs', qc, kg).astype(jnp.float32) * scale
        kpos_past = sel[..., None] * MOBA_BLOCK + offs
        s_past = s_past - slopes[..., None] * (t[:, None, None] - kpos_past).astype(jnp.float32)
        s_past = jnp.where(valid[..., None], s_past, -jnp.inf).reshape(B, H, MOBA_QBLOCK, topk * MOBA_BLOCK)
        k_own = lax.dynamic_slice_in_dim(kb, cur, 1, axis=2)[:, :, 0]
        v_own = lax.dynamic_slice_in_dim(vb, cur, 1, axis=2)[:, :, 0]
        kpos_own = cur * MOBA_BLOCK + offs
        rel = (t[:, None] - kpos_own[None, :])
        s_own = jnp.einsum('bhqd,bhsd->bhqs', qc, k_own).astype(jnp.float32) * scale
        s_own = s_own - slopes * rel.astype(jnp.float32)
        s_own = jnp.where(rel >= 0, s_own, -jnp.inf)
        p = jax.nn.softmax(jnp.concatenate([s_past, s_own], axis=-1), axis=-1).astype(v.dtype)
        p_past = p[..., :topk * MOBA_BLOCK].reshape(B, H, MOBA_QBLOCK, topk, MOBA_BLOCK)
        p_own = p[..., topk * MOBA_BLOCK:]
        return (jnp.einsum('bhqjs,bhqjsd->bhqd', p_past, vg)
                + jnp.einsum('bhqs,bhsd->bhqd', p_own, v_own))

    out = lax.map(one_qblock, jnp.arange(S // MOBA_QBLOCK))
    return out.transpose(1, 2, 0, 3, 4).reshape(B, H, S, d)

def retention(q, k, v):
    B, H, S, dk = q.shape
    dv = v.shape[-1]
    C = R_CHUNK
    n = S // C
    dt = v.dtype
    log_g = jnp.log(1.0 - jnp.exp2(-5.0 - jnp.arange(H, dtype=jnp.float32)))
    i = jnp.arange(C, dtype=jnp.float32)
    diff = i[:, None] - i[None, :]
    decay_mask = jnp.where(diff >= 0, jnp.exp(log_g[:, None, None] * jnp.maximum(diff, 0.0)), 0.0).astype(dt)
    qc = q.reshape(B, H, n, C, dk)
    kc = (k * (dk ** -0.5)).reshape(B, H, n, C, dk)
    vc = v.reshape(B, H, n, C, dv)
    inner = jnp.einsum('bhnid,bhnjd->bhnij', qc, kc) * decay_mask[:, None]
    inner_out = jnp.einsum('bhnij,bhnje->bhnie', inner, vc)
    k_dec = jnp.exp(log_g[:, None] * (C - 1.0 - i)).astype(dt)
    chunk_kv = jnp.einsum('bhnjd,bhnje->nbhde', kc * k_dec[:, None, :, None], vc)
    chunk_decay = jnp.exp(log_g * C).astype(dt)[None, :, None, None]

    def step(state, kv):
        return state * chunk_decay + kv, state

    _, states = lax.scan(step, jnp.zeros((B, H, dk, dv), dt), chunk_kv)
    q_dec = jnp.exp(log_g[:, None] * (i + 1.0)).astype(dt)
    cross = jnp.einsum('bhnid,nbhde->bhnie', qc * q_dec[:, None, :, None], states)
    return (inner_out + cross).reshape(B, H, S, dv)

def hybrid_layer(x, w_in, w_o_attn, w_o_ret, w_out, q_gain, k_gain, g_mix, g_ffn, w_ffn_in, w_ffn_out):
    B, S, _ = x.shape
    pts, _ = _split_points()
    h = rms_norm(x, g_mix)
    proj = h @ w_in
    qa, ka, va, qr, kr, vr, gr, gate_a, gate_r = jnp.split(proj, pts, axis=-1)

    def heads(t, nh):
        return t.reshape(B, S, nh, -1).transpose(0, 2, 1, 3)

    oa = moba_attention(rms_norm(heads(qa, A_HEADS), q_gain),
                        rms_norm(heads(ka, A_HEADS), k_gain),
                        heads(va, A_HEADS))
    oa = oa.transpose(0, 2, 1, 3).reshape(B, S, A_WIDTH)
    orr = retention(heads(qr, R_HEADS), heads(kr, R_HEADS), heads(vr, R_HEADS))
    orr = head_group_norm(orr).transpose(0, 2, 1, 3).reshape(B, S, R_V_WIDTH) * jax.nn.silu(gr)
    merged = jax.nn.sigmoid(gate_a) * (oa @ w_o_attn) + jax.nn.sigmoid(gate_r) * (orr @ w_o_ret)
    x = x + merged @ w_out
    h2 = rms_norm(x, g_ffn)
    g, u = jnp.split(h2 @ w_ffn_in, 2, axis=-1)
    return x + (jax.nn.silu(g) * u) @ w_ffn_out

def first_inputs(seed: int = 0) -> dict:
    key = jax.random.key(seed)
    ks = jax.random.split(key, 12)
    _, in_cols = _split_points()
    f32 = jnp.float32

    def w(k, shape, fan_in):
        return jax.random.normal(k, shape, f32) * (fan_in ** -0.5)

    def gain(k, shape):
        return 1.0 + 0.02 * jax.random.normal(k, shape, f32)

    return {
        "x": jax.random.normal(ks[0], (BATCH, SEQ, D_MODEL), f32),
        "w_in": w(ks[1], (DEPTH, D_MODEL, in_cols), D_MODEL),
        "w_o_attn": w(ks[2], (DEPTH, A_WIDTH, D_MODEL), A_WIDTH),
        "w_o_ret": w(ks[3], (DEPTH, R_V_WIDTH, D_MODEL), R_V_WIDTH),
        "w_out": w(ks[4], (DEPTH, D_MODEL, D_MODEL), D_MODEL),
        "q_norm": gain(ks[5], (DEPTH, A_HEAD_DIM)),
        "k_norm": gain(ks[6], (DEPTH, A_HEAD_DIM)),
        "norm_mix": gain(ks[7], (DEPTH, D_MODEL)),
        "norm_ffn": gain(ks[8], (DEPTH, D_MODEL)),
        "w_ffn_in": w(ks[9], (DEPTH, D_MODEL, 2 * D_FF), D_MODEL),
        "w_ffn_out": w(ks[10], (DEPTH, D_FF, D_MODEL), D_FF),
    }

def first_block(x, w_in, w_o_attn, w_o_ret, w_out, q_norm, k_norm, norm_mix, norm_ffn, w_ffn_in, w_ffn_out):
    S = x.shape[1]
    s_pad = -(-S // SEQ_ALIGN) * SEQ_ALIGN
    h = jnp.pad(x, ((0, 0), (0, s_pad - S), (0, 0)))
    for l in range(DEPTH):
        h = hybrid_layer(h, w_in[l], w_o_attn[l], w_o_ret[l], w_out[l], q_norm[l], k_norm[l],
                         norm_mix[l], norm_ffn[l], w_ffn_in[l], w_ffn_out[l])
    return h[:, :S]


GLA_HEADS = 4
GLA_DK = 128
GLA_DV = 256
GLA_RANK = 16
GLA_TAU = 16.0
GLA_CHUNK = 64
DIFF_HEADS = 4
DIFF_DQK = 128
DIFF_DV = 2 * DIFF_DQK
Q_BLOCK = 128
D_FF_2 = 5632
CONV_W = 3

GLA_QK = GLA_HEADS * GLA_DK
GLA_V = GLA_HEADS * GLA_DV
DIFF_QK = DIFF_HEADS * 2 * DIFF_DQK
DIFF_V = DIFF_HEADS * DIFF_DV
MIX_WIDTH = GLA_V + DIFF_V
IN_SPLITS = (GLA_QK, GLA_QK, GLA_V, GLA_V, GLA_RANK, DIFF_QK, DIFF_QK, DIFF_V)
IN_COLS = sum(IN_SPLITS)


def rmsnorm(x, g):
    xf = x.astype(jnp.float32)
    y = xf * lax.rsqrt(jnp.mean(xf * xf, axis=-1, keepdims=True) + EPS)
    return (y * g.astype(jnp.float32)).astype(x.dtype)

def gla_chunked(q, k, v, log_a):
    B, S = q.shape[0], q.shape[1]
    n = S // GLA_CHUNK

    def to_chunks(t):
        t = t.astype(jnp.float32).reshape(B, n, GLA_CHUNK, GLA_HEADS, t.shape[-1])
        return jnp.transpose(t, (1, 0, 3, 2, 4))

    qc = to_chunks(q * (GLA_DK ** -0.5))
    kc, vc, ac = to_chunks(k), to_chunks(v), to_chunks(log_a)
    causal = jnp.tril(jnp.ones((GLA_CHUNK, GLA_CHUNK), dtype=bool))

    def step(state, inp):
        qi, ki, vi, ai = inp
        b = jnp.cumsum(ai, axis=2)
        o_inter = jnp.einsum('bhcd,bhde->bhce', qi * jnp.exp(b), state)
        diff = b[:, :, :, None, :] - b[:, :, None, :, :]
        decay = jnp.exp(jnp.where(causal[:, :, None], diff, -jnp.inf))
        scores = jnp.einsum('bhid,bhjd,bhijd->bhij', qi, ki, decay)
        o_intra = jnp.einsum('bhij,bhje->bhie', scores, vi)
        b_last = b[:, :, -1:, :]
        state = (jnp.exp(b_last[:, :, 0, :])[..., None] * state
                 + jnp.einsum('bhcd,bhce->bhde', ki * jnp.exp(b_last - b), vi))
        return state, o_inter + o_intra

    s0 = jnp.zeros((B, GLA_HEADS, GLA_DK, GLA_DV), jnp.float32)
    _, o = lax.scan(step, s0, (qc, kc, vc, ac))
    return jnp.transpose(o, (1, 0, 3, 2, 4)).reshape(B, S, GLA_HEADS, GLA_DV)

def diff_attention(q, k, v, lam):
    B, S = q.shape[0], q.shape[1]
    nb = S // Q_BLOCK
    slopes = jnp.asarray(2.0 ** (-8.0 * np.arange(1, DIFF_HEADS + 1) / DIFF_HEADS), jnp.float32)
    qb = jnp.transpose(q.reshape(B, nb, Q_BLOCK, DIFF_HEADS, 2, DIFF_DQK), (1, 0, 2, 3, 4, 5))
    k_pos = jnp.arange(S, dtype=jnp.int32)
    scale = DIFF_DQK ** -0.5

    def block(args):
        qi, bi = args
        q_pos = bi * Q_BLOCK + jnp.arange(Q_BLOCK, dtype=jnp.int32)
        dist = q_pos[:, None] - k_pos[None, :]
        bias = -slopes[:, None, None] * dist.astype(jnp.float32)
        s = jnp.einsum('bqhcd,bkhcd->bhcqk', qi, k,
                       preferred_element_type=jnp.float32) * scale + bias[None, :, None]
        s = jnp.where(dist >= 0, s, -jnp.inf)
        p = jax.nn.softmax(s, axis=-1)
        a = p[:, :, 0] - lam * p[:, :, 1]
        return jnp.einsum('bhqk,bkhe->bqhe', a, v.astype(jnp.float32))

    o = lax.map(block, (qb, jnp.arange(nb, dtype=jnp.int32)))
    return jnp.transpose(o, (1, 0, 2, 3, 4)).reshape(B, S, DIFF_HEADS, DIFF_DV)

def token_mixer(h, w_in, w_alpha_up, b_alpha, gla_norm, lambda_q1, lambda_k1,
                lambda_q2, lambda_k2, diff_norm, w_o, lambda_init):
    B, S, _ = h.shape
    proj = h @ w_in
    offs = np.cumsum((0,) + IN_SPLITS)
    gq, gk, gv, gg, ga, dq, dk, dv = [proj[..., int(offs[i]):int(offs[i + 1])]
                                      for i in range(len(IN_SPLITS))]
    log_a = jax.nn.log_sigmoid((ga @ w_alpha_up + b_alpha).astype(jnp.float32)) / GLA_TAU
    o_a = gla_chunked(gq.reshape(B, S, GLA_HEADS, GLA_DK), gk.reshape(B, S, GLA_HEADS, GLA_DK),
                      gv.reshape(B, S, GLA_HEADS, GLA_DV), log_a.reshape(B, S, GLA_HEADS, GLA_DK))
    gate = jax.nn.silu(gg.astype(jnp.float32)).reshape(B, S, GLA_HEADS, GLA_DV)
    o_a = (rmsnorm(o_a, gla_norm) * gate).reshape(B, S, GLA_V)
    f32 = jnp.float32
    lam = (jnp.exp(jnp.sum(lambda_q1.astype(f32) * lambda_k1.astype(f32)))
           - jnp.exp(jnp.sum(lambda_q2.astype(f32) * lambda_k2.astype(f32))) + lambda_init)
    o_b = diff_attention(dq.reshape(B, S, DIFF_HEADS, 2, DIFF_DQK),
                         dk.reshape(B, S, DIFF_HEADS, 2, DIFF_DQK),
                         dv.reshape(B, S, DIFF_HEADS, DIFF_DV), lam)
    o_b = (rmsnorm(o_b, diff_norm) * (1.0 - lambda_init)).reshape(B, S, DIFF_V)
    o = jnp.concatenate([o_a, o_b], axis=-1).astype(h.dtype)
    return o @ w_o

def conv_ffn(h, w_ffn_in, conv_w, conv_b, w_ffn_out):
    S = h.shape[1]
    up = h @ w_ffn_in
    a, b = up[..., :D_FF_2], up[..., D_FF_2:]
    a_pad = jnp.pad(a, ((0, 0), (CONV_W - 1, 0), (0, 0)))
    a = (conv_w[0] * a_pad[:, 0:S] + conv_w[1] * a_pad[:, 1:S + 1]
         + conv_w[2] * a_pad[:, 2:S + 2] + conv_b)
    return (jax.nn.gelu(a, approximate=True) * b) @ w_ffn_out

def second_inputs(seed: int = 0) -> dict:
    key = jax.random.key(seed)
    ks = jax.random.split(key, 20)
    nrm = lambda k, shape: jax.random.normal(k, shape, jnp.float32)
    gain = lambda k, n: 1.0 + 0.1 * nrm(k, (DEPTH, n))
    return {
        'x': nrm(ks[0], (BATCH, SEQ, D_MODEL)),
        'attn_pre_norm': gain(ks[1], D_MODEL),
        'w_in': nrm(ks[2], (DEPTH, D_MODEL, IN_COLS)) * D_MODEL ** -0.5,
        'w_alpha_up': nrm(ks[3], (DEPTH, GLA_RANK, GLA_QK)) * GLA_RANK ** -0.5,
        'b_alpha': 0.1 * nrm(ks[4], (DEPTH, GLA_QK)),
        'gla_norm': gain(ks[5], GLA_DV),
        'lambda_q1': 0.1 * nrm(ks[6], (DEPTH, DIFF_DQK)),
        'lambda_k1': 0.1 * nrm(ks[7], (DEPTH, DIFF_DQK)),
        'lambda_q2': 0.1 * nrm(ks[8], (DEPTH, DIFF_DQK)),
        'lambda_k2': 0.1 * nrm(ks[9], (DEPTH, DIFF_DQK)),
        'diff_norm': gain(ks[10], DIFF_DV),
        'w_o': nrm(ks[11], (DEPTH, MIX_WIDTH, D_MODEL)) * MIX_WIDTH ** -0.5,
        'attn_post_norm': gain(ks[12], D_MODEL),
        'ffn_pre_norm': gain(ks[13], D_MODEL),
        'w_ffn_in': nrm(ks[14], (DEPTH, D_MODEL, 2 * D_FF_2)) * D_MODEL ** -0.5,
        'conv_w': nrm(ks[15], (DEPTH, CONV_W, D_FF_2)) * CONV_W ** -0.5,
        'conv_b': 0.02 * nrm(ks[16], (DEPTH, D_FF_2)),
        'w_ffn_out': nrm(ks[17], (DEPTH, D_FF_2, D_MODEL)) * D_FF_2 ** -0.5,
        'ffn_post_norm': gain(ks[18], D_MODEL),
    }

def second_block(x, attn_pre_norm, w_in, w_alpha_up, b_alpha, gla_norm, lambda_q1, lambda_k1,
              lambda_q2, lambda_k2, diff_norm, w_o, attn_post_norm, ffn_pre_norm, w_ffn_in,
              conv_w, conv_b, w_ffn_out, ffn_post_norm):
    for l in range(DEPTH):
        lambda_init = 0.8 - 0.6 * math.exp(-0.3 * l)
        h = rmsnorm(x, attn_pre_norm[l])
        m = token_mixer(h, w_in[l], w_alpha_up[l], b_alpha[l], gla_norm[l], lambda_q1[l],
                        lambda_k1[l], lambda_q2[l], lambda_k2[l], diff_norm[l], w_o[l], lambda_init)
        x = x + rmsnorm(m, attn_post_norm[l])
        h = rmsnorm(x, ffn_pre_norm[l])
        f = conv_ffn(h, w_ffn_in[l], conv_w[l], conv_b[l], w_ffn_out[l])
        x = x + rmsnorm(f, ffn_post_norm[l])
    return x


def setup_inputs(seed=0):
    out = dict(first_inputs(seed))
    for name, value in second_inputs(seed + 1).items():
        if name != "x":
            out[name + "_2"] = value
    return out


def reference(
    x, w_in, w_o_attn, w_o_ret, w_out, q_norm, k_norm, norm_mix, norm_ffn, w_ffn_in, w_ffn_out,
    attn_pre_norm_2, w_in_2, w_alpha_up_2, b_alpha_2, gla_norm_2, lambda_q1_2, lambda_k1_2,
    lambda_q2_2, lambda_k2_2, diff_norm_2, w_o_2, attn_post_norm_2, ffn_pre_norm_2, w_ffn_in_2,
    conv_w_2, conv_b_2, w_ffn_out_2, ffn_post_norm_2,
):
    x = first_block(
        x, w_in, w_o_attn, w_o_ret, w_out, q_norm, k_norm, norm_mix, norm_ffn, w_ffn_in,
        w_ffn_out,
    )
    return second_block(
        x, attn_pre_norm_2, w_in_2, w_alpha_up_2, b_alpha_2, gla_norm_2, lambda_q1_2,
        lambda_k1_2, lambda_q2_2, lambda_k2_2, diff_norm_2, w_o_2, attn_post_norm_2,
        ffn_pre_norm_2, w_ffn_in_2, conv_w_2, conv_b_2, w_ffn_out_2, ffn_post_norm_2,
    )


_drawn_inputs = setup_inputs


def setup_inputs(seed=0):
    import zlib

    import numpy as np

    out = dict(_drawn_inputs(seed))
    spreads = {}
    factors = {'q_norm': 8.0, 'k_norm': 8.0, 'b_alpha_2': 3.052, 'lambda_q1_2': 8.0, 'conv_b_2': 5.383}
    for name, (base, spread) in spreads.items():
        noise = np.random.default_rng([zlib.crc32(name.encode()), seed]).standard_normal(out[name].shape)
        drawn = base * np.exp(spread * noise) if base else spread * noise
        out[name] = __import__('jax').numpy.asarray(drawn.astype(out[name].dtype))
    for name, factor in factors.items():
        out[name] = (out[name] * factor).astype(out[name].dtype)
    return out
```

```python
from contextlib import ExitStack

import numpy as np
import concourse.bass as bass
from concourse import mybir

F32 = mybir.dt.float32
F32R = mybir.dt.float32r
ALU = mybir.AluOpType
ACT = mybir.ActivationFunctionType
AX = mybir.AxisListType

P = 128
SEQ = 256
NT = SEQ // P
DM = 2048
KT = DM // P
EPS = 1e-6
CHUNK = 1024
CPB = 8
SLOTS = 4
FF = 5632
FT = FF // P
FBLK = FF // 512
A_HEADS = 8
R_HEADS = 4
G_HEADS = 4
D_HEADS = 4
A_SCALE = 128 ** -0.5
LAMBDA_INIT = 0.2
MASKED = 1e30
LEVELS = 8
LW = LEVELS * P

GAIN = {"mix": 0, "ffn": 16, "pre2": 32, "ffn2": 48, "q": 64, "k": 65, "lq1": 66, "lk1": 67, "lq2": 68, "lk2": 69}
GAIN_ROWS = 70
CONV_ROWS = 4 * FT


def shape_constants():
    i = np.arange(P)
    ident = np.eye(P)
    ones = np.ones((P, P))
    q = np.arange(SEQ).reshape(NT, P).T[:, :, None]
    rel = q - np.arange(SEQ)[None, None, :]
    dist = np.where(rel >= 0, rel, MASKED).reshape(P, NT * SEQ)
    log_g = np.log(1.0 - 2.0 ** (-5.0 - np.arange(R_HEADS)))
    j = np.arange(SEQ).reshape(NT, P).T[:, None, :, None]
    gap = np.arange(SEQ)[None, None, None, :] - j
    decay = np.where(gap >= 0, np.exp(log_g[None, :, None, None] * np.maximum(gap, 0)), 0.0) * 256 ** -0.5
    sums, masks = [], []
    for s in (64, 32, 16, 8, 4, 2, 1):
        t, u = i[None, :], i[:, None]
        right = (t // s) % 2 == 1
        seam = np.where(right, t // s * s, (t // s + 1) * s)
        sums.append(np.where(right, (u >= seam) & (u <= t), (u > t) & (u < seam)))
        masks.append((u // (2 * s) == t // (2 * s)) & ((u // s) % 2 == 0) & right)
    sums.append(np.zeros((P, P)))
    masks.append(np.eye(P))
    sums.append(i[:, None] > i[None, :])
    sums.append(i[:, None] <= i[None, :])
    first = np.concatenate([ident, ones, dist], 1)
    second = np.concatenate([m.astype(np.float64) for m in sums + masks], 1)
    return (first.astype(np.float32), decay.reshape(P, -1).astype(np.float32), second.astype(np.float32))


class Chain:

    def __init__(self, eng, sem):
        self.eng, self.sem, self.base, self.k, self.at = eng, sem, 0, 0, None

    def __call__(self, ins):
        self.k += 1
        ins.then_inc(self.sem, 1)
        value = self.base + self.k
        if self.at is not None:
            i, per = self.at
            value = i * per + value
        self.eng.wait_ge(self.sem, value)

    def straight(self):
        self.base, self.k, self.at = self.base + self.k, 0, None

    def begin(self, i, per):
        self.straight()
        self.at = (i, per)

    def end(self, n):
        assert self.k == self.at[1], (self.k, self.at)
        self.base, self.k, self.at = self.base + n * self.k, 0, None


def two_blocks(nc, a, out, c_first, c_decay, c_second):
    with ExitStack() as ctx:
        def sb(name, shape, dt=F32):
            return ctx.enter_context(nc.sbuf_tensor(name, shape, dt))

        sems = {}

        def S(name):
            if name not in sems:
                sems[name] = ctx.enter_context(nc.semaphore(name))
            return sems[name]

        raw = sb("raw", [P, SLOTS, CHUNK])
        whi = sb("whi", [P, SLOTS, CHUNK], F32R)
        wlo = sb("wlo", [P, SLOTS, CHUNK], F32R)
        hT = sb("hT", [P, KT, 2, SEQ], F32R)
        big = sb("big", [P, 48 * SEQ])
        area_d = sb("area_d", [P, NT * DM])
        split_e = sb("split_e", [P, 16, SEQ], F32R)
        resid = sb("resid", [P, NT, DM])
        area_g = sb("area_g", [P, 2048])
        temp = sb("temp", [P, 2048])
        first = sb("first", [P, 2 * P + NT * SEQ])
        masks = sb("masks", [P, 10 * P + LW])
        gains = sb("gains", [P, GAIN_ROWS])
        conv = sb("conv", [P, CONV_ROWS])
        small = sb("small", [P, 64])

        ident, ones = first[:, 0:P], first[:, P:2 * P]
        dist = first[:, 2 * P:]
        decay = masks[:, 0:R_HEADS * NT * SEQ]
        sums_m, masks_m = masks[:, 0:10 * P], masks[:, 10 * P:]

        area = [big[:, n * 16 * SEQ:(n + 1) * 16 * SEQ] for n in range(3)]
        tiles_a = area[0].rearrange("p (n t) -> p n t", t=SEQ)
        rows_a = area[0].rearrange("p (t n) -> p t n", t=NT)
        tiles_b = area[1].rearrange("p (n t) -> p n t", t=SEQ)
        gv = area[1][:, 2048:].rearrange("p (t n) -> p t n", t=NT)
        rows_c = area[2].rearrange("p (t n) -> p t n", t=NT)
        dv = area[2][:, 0:2048].rearrange("p (t n) -> p t n", t=NT)
        free_c = area[2][:, 2048:]
        hidden = big[:, 0:FT * SEQ].rearrange("p (n t) -> p n t", t=SEQ)
        rows_d = area_d[:, :].rearrange("p (t n) -> p t n", t=NT)
        va = area_g[:, :].rearrange("p (t n) -> p t n", t=NT)
        lo_sum = area_d[:, 0:1024]
        gate_t = area_d[:, 1024:2048]
        up_t = area_d[:, 2048:3072]
        conv_in = temp[:, 0:4 * (2 + SEQ)].rearrange("p (f t) -> p f t", f=4)
        oaT = split_e[:, :, :].rearrange("p (h s) t -> p h s t", s=2)
        staged = split_e[:, :, :].rearrange("p (b k s) t -> p b k s t", b=2, s=2)

        ps = ctx.enter_context(nc.psum_tensor("ps", [P, 8, 512], F32))

        col = {}

        def keep(name, n):
            at = sum(w for _, w in col.values())
            col[name] = (at, n)
            return small[:, at:at + n]

        sumsq = keep("sumsq", 2)
        rstd = keep("rstd", 2)
        slopes1 = keep("slopes1", A_HEADS)
        slopes2 = keep("slopes2", D_HEADS)
        top = keep("top", 2)
        negtop = keep("negtop", 2)
        total = keep("total", 2)
        recip = keep("recip", 2)
        recip2 = keep("recip2", 2)
        bn = keep("bn", 12)
        mv = keep("mv", 4)
        lam = keep("lam", 2)
        neglam = keep("neglam", 1)
        lamprod = keep("lamprod", 2)
        unit = keep("unit", 1)
        osum = keep("osum", 2)
        orstd = keep("orstd", 2)
        spare = keep("spare", 1)
        eps = {n: keep(f"eps_{n}", 1) for n in ("head", "model", "one", "gla", "diff")}

        order = [("qk", 4), ("qkr", 4), ("va", 2), ("vr", 4), ("gr", 4), ("ga", 4), ("gb", 4), ("oa", 2), ("or", 4),
                 ("out", 4), ("ff", 2 * FBLK), ("fo", FBLK),
                 ("gqk", 2), ("dqk", 4), ("al", 1), ("gv", 2), ("dv", 2), ("gg", 2), ("o2", 4),
                 ("ff2", 2 * FBLK), ("fo2", FBLK)]
        base, n_blocks = {}, 0
        for name, n in order:
            base[name] = n_blocks
            n_blocks += n

        loaded = [S(f"loaded{s}") for s in range(SLOTS)]
        hi_ready, lo_ready, split_used = S("hi_ready"), S("lo_ready"), S("split_used")
        acc_ready, acc_freed, lo_copied = S("acc_ready"), S("acc_freed"), S("lo_copied")

        def wcols(w):
            return a[w].rearrange("l (k p) n -> p (l k) n", p=P)

        block = ctx.enter_context(nc.Block())

        @block.sync
        def _(sp):
            sp.dma_start(resid[:, :, :], a["x"].rearrange("b (t p) n -> p (b t) n", p=P)).then_inc(S("x_in"), 16)
            sp.dma_start(first[:, :], c_first).then_inc(S("first_in"), 16)

            def chunk_in(blk, c, src):
                if not (isinstance(blk, int) and blk * CPB + c < SLOTS):
                    sp.wait_ge(lo_ready, blk * CPB + c - SLOTS + 1)
                dst = raw[:, c % SLOTS, :]
                if len(src.shape) == 3:
                    dst = dst.rearrange("p (k n) -> p k n", k=2)[:, :, 0:src.shape[2]]
                sp.dma_start(dst, src).then_inc(loaded[c % SLOTS], 16)

            def wide(blk, w, col0, n=512):
                for c in range(CPB):
                    chunk_in(blk, c, wcols(w)[:, 2 * c:2 * c + 2, bass.ds(col0, n)])

            def run(name, n, w, col0):
                with sp.Fori(0, n) as i:
                    wide(base[name] + i, w, col0 + i * 512)

            def feed_in(name, w):
                with sp.Fori(0, FBLK) as i:
                    wide(base[name] + 2 * i, w, i * 512)
                    wide(base[name] + 2 * i + 1, w, FF + i * 512)

            def feed_out(name, w):
                with sp.Fori(0, FBLK) as i:
                    for c in range(CPB):
                        rows = a[w].rearrange("l k n -> (l k) n")[bass.ds(i * 512 + c // 2 * P, P), :]
                        chunk_in(base[name] + i, c, rows[:, c % 2 * CHUNK:(c % 2 + 1) * CHUNK])

            wide(0, "w_in", 0)
            with sp.Fori(1, 4) as i:
                wide(i, "w_in", i * 512)
            run("qkr", 4, "w_in", 3072)
            run("va", 2, "w_in", 2048)
            run("vr", 4, "w_in", 5120)
            with sp.Fori(0, 12) as i:
                wide(base["gr"] + i, "w_in", 7168 + i * 512)
            for j in range(2):
                for c in range(CPB):
                    chunk_in(base["oa"] + j, c, wcols("w_o_attn")[:, c, j * CHUNK:(j + 1) * CHUNK])
            run("or", 4, "w_o_ret", 0)
            run("out", 4, "w_out", 0)
            feed_in("ff", "w_ffn_in")
            feed_out("fo", "w_ffn_out")
            run("gqk", 2, "w_in_2", 0)
            run("dqk", 4, "w_in_2", 3088)
            wide(base["al"], "w_in_2", 3072, P)
            run("gv", 2, "w_in_2", 1024)
            run("dv", 2, "w_in_2", 5136)
            run("gg", 2, "w_in_2", 2048)
            run("o2", 4, "w_o_2", 0)
            feed_in("ff2", "w_ffn_in_2")
            feed_out("fo2", "w_ffn_out_2")
            sp.wait_ge(S("y_ready"), 1)
            sp.dma_start(out.rearrange("b (t p) n -> p (b t) n", p=P), resid[:, :, :]).then_inc(S("stored"), 16)
            sp.wait_ge(S("stored"), 16)

        @block.tensor
        def _(pe):
            def ready(blk, c):
                pe.wait_ge(lo_ready, blk * CPB + c + 1)

            def acc_free(blk, all_of_them):
                if isinstance(blk, int) and blk < (1 if all_of_them else 2):
                    return
                pe.wait_ge(acc_freed, blk if all_of_them else blk - 1)

            def cols_block(blk, par, after_rows=False, turned=None, tiles=4):
                acc_free(blk, after_rows)
                for c in range(CPB):
                    if turned is not None:
                        pe.wait_ge(turned, c + 1)
                    ready(blk, c)
                    for k2 in range(2):
                        kt = 2 * c + k2
                        for ft in range(tiles):
                            acc = ps[:, 4 * par + ft, :]
                            f = slice(k2 * 512 + ft * P, k2 * 512 + ft * P + P)
                            pe.matmul(acc, whi[:, c % SLOTS, f], hT[:, kt, :, :], start=(kt == 0), stop=False)
                            mm = pe.matmul(acc[:, 0:SEQ], wlo[:, c % SLOTS, f], hT[:, kt, 0, :], start=False,
                                           stop=(kt == KT - 1))
                    mm.then_inc(split_used, 1)

            def rows_mm(acc, x, t, c, f, start, stop):
                hi, lo = x[:, 0, t * P:t * P + P], x[:, 1, t * P:t * P + P]
                pe.matmul(acc, hi, whi[:, c % SLOTS, f], start=start, stop=False)
                pe.matmul(acc, hi, wlo[:, c % SLOTS, f], start=False, stop=False)
                return pe.matmul(acc, lo, whi[:, c % SLOTS, f], start=False, stop=stop)

            def rows_block(blk, par, turned=None):
                acc_free(blk, False)
                for c in range(CPB):
                    if turned is not None:
                        pe.wait_ge(turned, c + 1)
                    ready(blk, c)
                    for k2 in range(2):
                        kt = 2 * c + k2
                        for t in range(NT):
                            mm = rows_mm(ps[:, 2 * par + t, :], hT[:, kt, :, :], t, c,
                                         slice(k2 * 512, k2 * 512 + 512), kt == 0, kt == KT - 1)
                    mm.then_inc(split_used, 1)

            def done(blk):
                pe.wait_ge(split_used, (blk + 1) * CPB)
                pe.sem_inc(acc_ready, 1)

            def pairs(name, n, form, turned=None, after_rows=False):
                b = base[name]
                form(b, 0, turned=turned, **({"after_rows": True} if after_rows else {}))
                done(b)
                form(b + 1, 1)
                done(b + 1)
                if n > 2:
                    with pe.Fori(1, n // 2) as i:
                        for par in range(2):
                            form(b + 2 * i + par, par)
                            done(b + 2 * i + par)

            def turn(u, src):
                pe.wait_ge(S(f"rows{u}"), 1)
                for j in range(KT // 2):
                    if j >= 4:
                        pe.wait_ge(S(f"turned{u}"), j - 3)
                    for k2 in range(2):
                        for t in range(NT):
                            mm = pe.transpose(ps[:, 4 + j % 4, k2 * SEQ + t * P:k2 * SEQ + t * P + P],
                                              src[:, t, (2 * j + k2) * P:(2 * j + k2 + 1) * P], ident)
                    mm.then_inc(S(f"turn{u}"), 1)

            pe.wait_ge(S("first_in"), 16)
            pe.wait_ge(S("gains_in"), 16 * 13)
            g_rows = area_g[:, 0:3 * P].rearrange("p (n d) -> p n d", d=P)
            pe.transpose(ps[:, 0, 0:GAIN_ROWS], g_rows[0:GAIN_ROWS, 0, :], ident[0:GAIN_ROWS, 0:GAIN_ROWS])
            half = CONV_ROWS // 2
            for n in range(2):
                mm = pe.transpose(ps[:, 1 + n, 0:half], g_rows[0:half, 1 + n, :], ident[0:half, 0:half])
            mm.then_inc(S("gain_t"), 1)
            pe.wait_ge(S("lam_prod"), 1)
            pe.matmul(ps[:, 3, 0:2], ones, lamprod, start=True, stop=True).then_inc(S("lam_sum"), 1)

            turn(0, resid)
            pe.wait_ge(S("lam_read"), 1)
            pairs("qk", 4, cols_block, S("turned0"))
            pairs("qkr", 4, cols_block)
            pairs("va", 2, rows_block)
            pairs("vr", 4, rows_block)
            pe.wait_ge(acc_freed, base["gr"])

            s1, qst, pT, on = temp[:, 0:512], temp[:, 512:768], temp[:, 1024:1536], temp[:, 1536:1792]
            with pe.Fori(0, A_HEADS) as h:
                pe.wait_ge(S("a_sq"), h + 1)
                pe.matmul(ps[:, 4, :], ones, s1, start=True, stop=True).then_inc(S("a_ss"), 1)
                pe.wait_ge(S("a_root"), h + 1)
            with pe.Fori(0, A_HEADS) as h:
                pe.wait_ge(S("a_q"), h + 1)
                for t in range(NT):
                    mm = pe.matmul(ps[:, 5, t * SEQ:t * SEQ + SEQ], qst[:, t * P:t * P + P], tiles_a[:, bass.ds(8 + h, 1), :],
                                   start=True, stop=True)
                mm.then_inc(S("a_score"), 1)
                pe.wait_ge(S("a_exp"), h + 1)
                for kt, t in ((0, 0), (0, 1), (1, 1)):
                    mm = pe.transpose(ps[:, 6, kt * SEQ + t * P:kt * SEQ + t * P + P],
                                      s1[:, t * SEQ + kt * P:t * SEQ + kt * P + P], ident)
                mm.then_inc(S("a_turn"), 1)
                pe.wait_ge(S("a_pT"), h + 1)
                v = [va[:, kt, bass.ds(h * P, P)] for kt in range(NT)]
                pe.matmul(ps[:, 7, 0:P], pT[:, 0:P], v[0], start=True, stop=True)
                pe.matmul(ps[:, 7, P:2 * P], pT[:, P:2 * P], v[0], start=True, stop=False)
                pe.matmul(ps[:, 7, P:2 * P], pT[:, SEQ + P:2 * SEQ], v[1], start=False, stop=True)\
                    .then_inc(S("a_o"), 1)
                pe.wait_ge(S("a_on"), h + 1)
                for t in range(NT):
                    mm = pe.transpose(ps[:, 4, t * P:t * P + P], on[:, t * P:t * P + P], ident)
                mm.then_inc(S("a_oT"), 1)
                pe.wait_ge(S("a_done"), h + 1)

            kst, aT = temp[:, 0:512], temp[:, 512:1024]
            with pe.Fori(0, R_HEADS) as h:
                pe.wait_ge(S("r_k"), h + 1)
                for jt in range(NT):
                    for d in range(2):
                        mm = pe.matmul(ps[:, 4, jt * SEQ:jt * SEQ + SEQ], kst[:, d * SEQ + jt * P:d * SEQ + jt * P + P],
                                       tiles_b[:, bass.ds(2 * h + d, 1), :], start=(d == 0), stop=(d == 1))
                mm.then_inc(S("r_score"), 1)
                pe.wait_ge(S("r_a"), h + 1)
                v = [rows_c[:, jt, bass.ds(h * 512, 512)] for jt in range(NT)]
                pe.matmul(ps[:, 6, :], aT[:, 0:P], v[0], start=True, stop=True)
                pe.matmul(ps[:, 7, :], aT[:, P:SEQ], v[0], start=True, stop=False)
                pe.matmul(ps[:, 7, :], aT[:, SEQ + P:2 * SEQ], v[1], start=False, stop=True).then_inc(S("r_o"), 1)
                pe.wait_ge(S("r_done"), h + 1)

            pairs("gr", 4, rows_block)
            pairs("ga", 4, rows_block)
            pairs("gb", 4, rows_block)

            for j in range(2):
                blk = base["oa"] + j
                acc_free(blk, j == 0)
                for c in range(CPB):
                    ready(blk, c)
                    for half_c in range(2):
                        for t in range(NT):
                            mm = rows_mm(ps[:, 4 * j + 2 * half_c + t, :], oaT[:, c, :, :], t, c,
                                         slice(half_c * 512, half_c * 512 + 512), c == 0, c == CPB - 1)
                    mm.then_inc(split_used, 1)
                done(blk)
            pe.wait_ge(acc_freed, base["or"])
            turn(1, resid)
            pairs("or", 4, rows_block, S("turned1"))
            turn(2, rows_d)
            pairs("out", 4, rows_block, S("turned2"))

            def feed_out(name, u):
                b = base[name]

                def one(i, blk, buf, start, stop):
                    pe.wait_ge(S(f"staged{u}"), i + 1)
                    for c in range(CPB):
                        ready(blk, c)
                        k = c // 2
                        for half_c in range(2):
                            for t in range(NT):
                                mm = rows_mm(ps[:, 4 * t + 2 * (c % 2) + half_c, :], staged[:, buf, k, :, :], t, c,
                                             slice(half_c * 512, half_c * 512 + 512), start and k == 0, stop and k == 3)
                        mm.then_inc(split_used, 1)

                acc_free(b, True)
                one(0, b, 0, True, False)
                with pe.Fori(0, (FBLK - 3) // 2) as i:
                    one(2 * i + 1, b + 2 * i + 1, 1, False, False)
                    one(2 * i + 2, b + 2 * i + 2, 0, False, False)
                one(FBLK - 2, b + FBLK - 2, 1, False, False)
                one(FBLK - 1, b + FBLK - 1, 0, False, True)
                pe.wait_ge(split_used, (b + FBLK) * CPB)
                pe.sem_inc(acc_ready, FBLK)

            turn(3, rows_d)
            pairs("ff", 2 * FBLK, cols_block, S("turned3"), after_rows=True)
            feed_out("fo", 0)

            turn(4, rows_d)
            pairs("gqk", 2, cols_block, S("turned4"), after_rows=True)
            pairs("dqk", 4, cols_block)
            cols_block(base["al"], 0, tiles=1)
            done(base["al"])
            gaT = temp[0:16, 0:SEQ]
            pe.wait_ge(S("g_ga"), 1)
            pe.wait_ge(S("alpha_in"), 32)
            for t in range(NT):
                pe.matmul(ps[:, 6 + t, :], gaT[:, t * P:t * P + P], area_g[0:16, 0:512], start=True, stop=False)
                mm = pe.matmul(ps[:, 6 + t, :], ones[0:1, :], area_g[0:1, 512:1024], start=False, stop=True)
            mm.then_inc(S("g_z"), 1)
            pairs("gv", 2, rows_block)
            pairs("dv", 2, rows_block)

            ke, qe = area_g[:, 0:LW], area_g[:, LW:2 * LW]
            sT, cross, la_h = temp[:, 0:512], temp[:, 512:768], temp[:, 768:1024]
            pe.wait_ge(S("second_in"), 16)
            with pe.Fori(0, G_HEADS) as h:
                for t in range(NT):
                    pe.wait_ge(S("g_la"), h + 1)
                    if t == 0:
                        pe.wait_ge(S("g_done"), h)
                    else:
                        pe.wait_ge(S("g_sT"), 3 * h + 1)
                    la = la_h[:, t * P:t * P + P]
                    for n in range(2):
                        pe.matmul(ps[:, 4 + n, :], la, sums_m[:, n * 512:n * 512 + 512], start=True, stop=True)
                    pe.matmul(ps[:, 6, 0:P], la, sums_m[:, LW + t * P:LW + t * P + P], start=True, stop=True)\
                        .then_inc(S("g_sum"), 1)
                    pe.wait_ge(S("g_qk"), 2 * h + t + 1)
                    for n in range(LEVELS):
                        mm = pe.matmul(ps[:, 4 + n // 4, n % 4 * P:n % 4 * P + P], ke[:, n * P:n * P + P],
                                       qe[:, n * P:n * P + P], start=True, stop=True)
                    mm.then_inc(S("g_score"), 1)
                pe.matmul(ps[:, 6, P:2 * P], cross[:, 0:P], cross[:, P:2 * P], start=True, stop=True)\
                    .then_inc(S("g_cross"), 1)
                pe.wait_ge(S("g_sT"), 3 * h + 3)
                v = [gv[:, jt, bass.ds(h * SEQ, SEQ)] for jt in range(NT)]
                pe.matmul(ps[:, 7, 0:SEQ], sT[:, 0:P], v[0], start=True, stop=True)
                pe.matmul(ps[:, 7, SEQ:], sT[:, P:SEQ], v[0], start=True, stop=False)
                pe.matmul(ps[:, 7, SEQ:], sT[:, SEQ + P:], v[1], start=False, stop=True).then_inc(S("g_o"), 1)

            s1, dT, q_h = temp[:, 512:1024], temp[:, 1024:1536], temp[:, 1536:1792]
            diff = temp[:, 0:512]
            with pe.Fori(0, D_HEADS) as h:
                for c in range(2):
                    pe.wait_ge(S("d_q"), 2 * h + c + 1)
                    pe.wait_ge(S("d_top"), 2 * h + c)
                    for t in range(NT):
                        mm = pe.matmul(ps[:, 4, t * SEQ:t * SEQ + SEQ], q_h[:, t * P:t * P + P],
                                       tiles_a[:, bass.ds(8 + 2 * h + c, 1), :], start=True, stop=True)
                    mm.then_inc(S("d_score"), 1)
                pe.wait_ge(S("d_p"), h + 1)
                for kt, t in ((0, 0), (0, 1), (1, 1)):
                    mm = pe.transpose(ps[:, 5, kt * SEQ + t * P:kt * SEQ + t * P + P],
                                      diff[:, t * SEQ + kt * P:t * SEQ + kt * P + P], ident)
                mm.then_inc(S("d_turn"), 1)
                pe.wait_ge(S("d_pT"), h + 1)
                v = [dv[:, kt, bass.ds(h * SEQ, SEQ)] for kt in range(NT)]
                pe.matmul(ps[:, 6, 0:SEQ], dT[:, 0:P], v[0], start=True, stop=True)
                pe.matmul(ps[:, 6, SEQ:], dT[:, P:SEQ], v[0], start=True, stop=False)
                pe.matmul(ps[:, 6, SEQ:], dT[:, SEQ + P:], v[1], start=False, stop=True).then_inc(S("d_o"), 1)
                pe.wait_ge(S("d_done"), h + 1)

            pairs("gg", 2, rows_block)
            turn(5, rows_d)
            pairs("o2", 4, rows_block, S("turned5"))
            turn(6, rows_d)
            pairs("ff2", 2 * FBLK, cols_block, S("turned6"), after_rows=True)
            feed_out("fo2", 1)

        @block.scalar
        def _(act):
            def split(blk, cs):
                for c in cs:
                    act.wait_ge(loaded[c % SLOTS], 16 * (2 * blk + c // SLOTS + 1))
                    if not (isinstance(blk, int) and blk * CPB + c < SLOTS):
                        act.wait_ge(split_used, blk * CPB + c - SLOTS + 1)
                    act.activation(whi[:, c % SLOTS, :], raw[:, c % SLOTS, :], ACT.Copy).then_inc(hi_ready, 1)

            def ahead(blk, more=True):
                split(blk, range(SLOTS, CPB))
                if more:
                    split(blk + 1, range(SLOTS))

            def low_sums(blk, par):
                act.wait_ge(acc_ready, blk + 1)
                if not (isinstance(blk, int) and blk == 0):
                    act.wait_ge(acc_freed, blk)
                act.activation(lo_sum.rearrange("p (f t) -> p f t", f=4), ps[:, 4 * par:4 * par + 4, SEQ:], ACT.Copy)\
                    .then_inc(lo_copied, 1)

            def pairs(name, n, epilogue):
                b = base[name]
                with act.Fori(0, n // 2) as i:
                    for par in range(2):
                        ahead(b + 2 * i + par)
                        epilogue(b + 2 * i + par, par, 2 * i + par)

            def turn(u, col0=None):
                for j in range(KT // 2):
                    act.wait_ge(S(f"turn{u}"), j + 1)
                    for k2 in range(2):
                        kt = 2 * j + k2
                        src = ps[:, 4 + j % 4, k2 * SEQ:k2 * SEQ + SEQ]
                        if col0 is None:
                            ins = act.activation(hT[:, kt, 0, :], src, ACT.Copy)
                        else:
                            ins = act.activation(hT[:, kt, 0, :], src, ACT.Copy, scale=gains[:, col0 + kt:col0 + kt + 1])
                    ins.then_inc(S(f"turn_hi{u}"), 1)

            def squares(u, src):
                if u:
                    act.wait_ge(S(f"norm_in{u}"), 1)
                for t in range(NT):
                    ins = act.activation(rows_d[:, t, :], src[:, t, :], ACT.Square, accum_out=sumsq[:, t:t + 1])
                own(ins)
                act.activation(sumsq, sumsq, ACT.Sqrt, bias=eps["model"]).then_inc(S(f"norm_sq{u}"), 1)

            own = Chain(act, S("act_own"))
            split(0, range(SLOTS))
            act.wait_ge(S("unit_ok"), 1)
            act.wait_ge(S("x_in"), 16)
            squares(0, resid)
            act.wait_ge(S("lam_sum"), 1)
            act.activation(lam, ps[:, 3, 0:2], ACT.Exp).then_inc(S("lam_read"), 1)
            act.wait_ge(S("gain_ok"), 1)
            turn(0, GAIN["mix"])

            pairs("qk", 4, lambda blk, par, i: low_sums(blk, par))
            pairs("qkr", 4, lambda blk, par, i: low_sums(blk, par))

            def keep_rows(dst):
                def epilogue(blk, par, i):
                    act.wait_ge(acc_ready, blk + 1)
                    act.activation(dst[:, :, bass.ds(i * 512, 512)], ps[:, 2 * par:2 * par + 2, :], ACT.Copy)\
                        .then_inc(acc_freed, 1)
                return epilogue

            pairs("va", 2, keep_rows(va))
            pairs("vr", 4, keep_rows(rows_c))

            s1, qn, pT = temp[:, 0:512], temp[:, 512:1024], temp[:, 1024:1536]
            with act.Fori(0, A_HEADS) as h:
                act.wait_ge(S("a_ss"), h + 1)
                act.wait_ge(S("a_qn"), h)
                act.activation(qn, ps[:, 4, :], ACT.Sqrt, bias=eps["head"]).then_inc(S("a_root"), 1)
            with act.Fori(0, A_HEADS) as h:
                act.wait_ge(S("a_top"), h + 1)
                for t in range(NT):
                    ins = act.activation(s1[:, t * SEQ:t * SEQ + SEQ], s1[:, t * SEQ:t * SEQ + SEQ], ACT.Exp,
                                         bias=negtop[:, t:t + 1], scale=A_SCALE, accum_out=total[:, t:t + 1])
                ins.then_inc(S("a_exp"), 1)
                act.wait_ge(S("a_turn"), h + 1)
                act.activation(pT[:, 0:SEQ], ps[:, 6, 0:SEQ], ACT.Copy)
                act.activation(pT[:, SEQ + P:], ps[:, 6, SEQ + P:], ACT.Copy).then_inc(S("a_pT"), 1)
                act.wait_ge(S("a_oT"), h + 1)
                act.activation(oaT[:, bass.ds(h, 1), 0, :], ps[:, 4, 0:SEQ], ACT.Copy).then_inc(S("a_hi"), 1)

            with act.Fori(0, R_HEADS) as h:
                act.wait_ge(S("r_var"), h + 1)
                act.activation(rstd, mv.rearrange("p (t s) -> p t s", s=2)[:, :, 1], ACT.Sqrt, bias=eps["one"]).then_inc(S("r_root"), 1)

            def gate_silu(blk, par, i):
                act.wait_ge(acc_ready, blk + 1)
                act.wait_ge(acc_freed, blk)
                act.activation(lo_sum.rearrange("p (t n) -> p t n", t=NT), ps[:, 2 * par:2 * par + 2, :], ACT.Silu)\
                    .then_inc(S("silu"), 1)

            pairs("gr", 4, gate_silu)

            def gate_sigmoid(dst):
                def epilogue(blk, par, i):
                    act.wait_ge(acc_ready, blk + 1)
                    act.wait_ge(acc_freed, blk)
                    act.activation(dst[:, :, bass.ds(i * 512, 512)], ps[:, 2 * par:2 * par + 2, :], ACT.Sigmoid)\
                        .then_inc(acc_freed, 1)
                return epilogue

            pairs("ga", 4, gate_sigmoid(rows_d))
            pairs("gb", 4, gate_sigmoid(rows_a))
            for j in range(2):
                ahead(base["oa"] + j)
            turn(1)
            pairs("or", 4, lambda blk, par, i: None)
            turn(2)
            pairs("out", 4, lambda blk, par, i: None)
            squares(3, resid)
            turn(3, GAIN["ffn"])

            def feed_in(name, gate):
                b = base[name]
                with act.Fori(0, FBLK) as i:
                    ahead(b + 2 * i)
                    low_sums(b + 2 * i, 0)
                    gate(i, b + 2 * i)
                    ahead(b + 2 * i + 1)
                    low_sums(b + 2 * i + 1, 1)

            def silu_gate(i, blk):
                act.wait_ge(acc_freed, blk + 1)
                act.wait_ge(S("hidden0"), i)
                act.activation(up_t, gate_t, ACT.Silu).then_inc(S("gate0"), 1)

            def stage(u, i, buf):
                act.activation(staged[:, buf, :, 0, :], hidden[:, bass.ds(4 * i, 4), :], ACT.Copy)\
                    .then_inc(S(f"stage_hi{u}"), 1)

            def feed_out(name, u, last):
                b = base[name]

                def one(i, blk, buf, more=True):
                    split(blk, range(SLOTS, CPB))
                    if more:
                        act.wait_ge(split_used, blk * CPB)
                        stage(u, i + 1, 1 - buf)
                        split(blk + 1, range(SLOTS))

                act.wait_ge(S(f"hidden{u}"), FBLK)
                stage(u, 0, 0)
                one(0, b, 0)
                with act.Fori(0, (FBLK - 3) // 2) as i:
                    one(2 * i + 1, b + 2 * i + 1, 1)
                    one(2 * i + 2, b + 2 * i + 2, 0)
                one(FBLK - 2, b + FBLK - 2, 1)
                one(FBLK - 1, b + FBLK - 1, 0, False)
                if not last:
                    split(b + FBLK, range(SLOTS))

            feed_in("ff", silu_gate)
            feed_out("fo", 0, False)
            squares(4, resid)
            turn(4, GAIN["pre2"])

            pairs("gqk", 2, lambda blk, par, i: low_sums(blk, par))
            pairs("dqk", 4, lambda blk, par, i: low_sums(blk, par))
            blk = base["al"]
            ahead(blk)
            act.wait_ge(acc_ready, blk + 1)
            act.wait_ge(acc_freed, blk)
            act.activation(lo_sum[0:16, 0:SEQ], ps[0:16, 0, SEQ:], ACT.Copy).then_inc(lo_copied, 1)

            z_abs = free_c[:, 0:1024]
            act.wait_ge(S("g_z"), 1)
            own(act.activation(z_abs.rearrange("p (t n) -> p t n", t=NT), ps[:, 6:8, :], ACT.Abs))
            own(act.activation(z_abs, z_abs, ACT.Exp, scale=-1.0))
            act.activation(z_abs, z_abs, ACT.Ln, bias=unit).then_inc(S("g_ln"), 1)
            pairs("gv", 2, keep_rows(gv))
            pairs("dv", 2, keep_rows(dv))

            decays = free_c[:, 0:9 * P]
            with act.Fori(0, G_HEADS) as h:
                own.begin(h, 1)
                for t in range(NT):
                    act.wait_ge(S("g_sum"), 2 * h + t + 1)
                    act.activation(decays[:, 0:LW].rearrange("p (n c) -> p n c", n=2), ps[:, 4:6, :], ACT.Exp, scale=1.0 / 16)
                    act.activation(decays[:, LW:], ps[:, 6, 0:P], ACT.Exp, scale=1.0 / 16).then_inc(S("g_exp"), 1)
                act.wait_ge(S("g_o"), h + 1)
                for t in range(NT):
                    ins = act.activation(area_g[:, t * SEQ:t * SEQ + SEQ], ps[:, 7, t * SEQ:t * SEQ + SEQ], ACT.Square,
                                         accum_out=osum[:, t:t + 1])
                own(ins)
                act.activation(osum, osum, ACT.Sqrt, bias=eps["gla"]).then_inc(S("g_sq"), 1)
            own.end(G_HEADS)

            s1, dT = temp[:, 512:1024], temp[:, 1024:1536]
            with act.Fori(0, D_HEADS) as h:
                own.begin(h, 1)
                for c in range(2):
                    act.wait_ge(S("d_top"), 2 * h + c + 1)
                    for t in range(NT):
                        ins = act.activation(s1[:, t * SEQ:t * SEQ + SEQ], s1[:, t * SEQ:t * SEQ + SEQ], ACT.Exp,
                                             bias=negtop[:, t:t + 1], scale=A_SCALE, accum_out=total[:, t:t + 1])
                    ins.then_inc(S("d_exp"), 1)
                act.wait_ge(S("d_turn"), h + 1)
                act.activation(dT[:, 0:SEQ], ps[:, 5, 0:SEQ], ACT.Copy)
                act.activation(dT[:, SEQ + P:], ps[:, 5, SEQ + P:], ACT.Copy).then_inc(S("d_pT"), 1)
                act.wait_ge(S("d_o"), h + 1)
                for t in range(NT):
                    ins = act.activation(s1[:, t * SEQ:t * SEQ + SEQ], ps[:, 6, t * SEQ:t * SEQ + SEQ], ACT.Square,
                                         accum_out=osum[:, t:t + 1])
                own(ins)
                act.activation(osum, osum, ACT.Sqrt, bias=eps["diff"]).then_inc(S("d_sq"), 1)
            own.end(D_HEADS)

            def gate_silu2(blk, par, i):
                act.wait_ge(acc_ready, blk + 1)
                act.wait_ge(acc_freed, blk)
                act.activation(area_g[:, 0:1024].rearrange("p (t n) -> p t n", t=NT), ps[:, 2 * par:2 * par + 2, :], ACT.Silu)\
                    .then_inc(S("silu2"), 1)

            pairs("gg", 2, gate_silu2)
            turn(5)
            pairs("o2", 4, lambda blk, par, i: None)
            squares(7, rows_a)
            squares(6, resid)
            turn(6, GAIN["ffn2"])

            def gelu_gate(i, blk):
                act.wait_ge(S("conv_done"), i + 1)
                act.wait_ge(S("hidden1"), i)
                for f in range(4):
                    ins = act.activation(up_t[:, f * SEQ:f * SEQ + SEQ], gate_t[:, f * SEQ:f * SEQ + SEQ],
                                         ACT.Gelu_apprx_tanh, bias=conv[:, bass.ds(3 * FT + 4 * i + f, 1)])
                ins.then_inc(S("gate1"), 1)

            feed_in("ff2", gelu_gate)
            feed_out("fo2", 1, True)
            squares(8, rows_a)

        @block.vector
        def _(dve):
            own = Chain(dve, S("dve_own"))

            def split(blk, cs):
                for c in cs:
                    dve.wait_ge(hi_ready, blk * CPB + c + 1)
                    dve.tensor_tensor(wlo[:, c % SLOTS, :], raw[:, c % SLOTS, :], whi[:, c % SLOTS, :].bitcast(F32),
                                      ALU.subtract).then_inc(lo_ready, 1)

            def ahead(blk):
                split(blk, range(SLOTS, CPB))
                split(blk + 1, range(SLOTS))

            def pairs(name, n, epilogue, per=0):
                b = base[name]
                with dve.Fori(0, n // 2) as i:
                    own.begin(i, 2 * per)
                    for par in range(2):
                        ahead(b + 2 * i + par)
                        epilogue(b + 2 * i + par, par, 2 * i + par)
                own.end(n // 2)

            def add_low(blk, par, nth, dst):
                dve.wait_ge(lo_copied, nth + 1)
                return dve.tensor_tensor(dst, ps[:, 4 * par:4 * par + 4, 0:SEQ], lo_sum.rearrange("p (f t) -> p f t", f=4), ALU.add)

            def turn(u, col0=None):
                for j in range(KT // 2):
                    dve.wait_ge(S(f"turn_hi{u}"), j + 1)
                    for k2 in range(2):
                        kt = 2 * j + k2
                        src = ps[:, 4 + j % 4, k2 * SEQ:k2 * SEQ + SEQ]
                        hi = hT[:, kt, 0, :].bitcast(F32)
                        if col0 is None:
                            ins = dve.tensor_tensor(hT[:, kt, 1, :], src, hi, ALU.subtract)
                        else:
                            ins = dve.scalar_tensor_tensor(hT[:, kt, 1, :], src, gains[:, col0 + kt:col0 + kt + 1], hi,
                                                           ALU.mult, ALU.subtract)
                    ins.then_inc(S(f"turned{u}"), 1)

            def row_scale(u):
                dve.wait_ge(S(f"norm_sq{u}"), 1)
                own(dve.reciprocal(rstd, sumsq))

            def norm_rows(u, dst):
                row_scale(u)
                for t in range(NT):
                    ins = dve.tensor_scalar(dst[:, t, :], resid[:, t, :], rstd[:, t:t + 1], DM ** 0.5, ALU.mult, ALU.mult)
                ins.then_inc(S(f"rows{u}"), 1)

            for h in range(A_HEADS):
                dve.memset(slopes1[:, h:h + 1], -(2.0 ** -(h + 1)) / A_SCALE)
            for h in range(D_HEADS):
                dve.memset(slopes2[:, h:h + 1], -(2.0 ** (-8.0 * (h + 1) / D_HEADS)) / A_SCALE)
            for n, width in (("head", P), ("model", DM), ("one", 1), ("diff", SEQ), ("gla", SEQ / A_SCALE ** 2)):
                dve.memset(eps[n], EPS * width)
            dve.memset(unit, 1.0).then_inc(S("unit_ok"), 1)
            dve.wait_ge(S("gain_t"), 1)
            dve.tensor_copy(gains[:, :], ps[:, 0, 0:GAIN_ROWS])
            half = CONV_ROWS // 2
            own(dve.tensor_copy(conv[:, :].rearrange("p (n f) -> p n f", n=2), ps[:, 1:3, 0:half]))
            dve.tensor_tensor(lamprod[:, 0:1], gains[:, GAIN["lq1"]:GAIN["lq1"] + 1], gains[:, GAIN["lk1"]:GAIN["lk1"] + 1], ALU.mult)
            dve.tensor_tensor(lamprod[:, 1:2], gains[:, GAIN["lq2"]:GAIN["lq2"] + 1], gains[:, GAIN["lk2"]:GAIN["lk2"] + 1], ALU.mult)\
                .then_inc(S("lam_prod"), 1)
            dve.tensor_scalar(gains[:, GAIN["q"]:GAIN["k"] + 1], gains[:, GAIN["q"]:GAIN["k"] + 1], P ** 0.5, None, ALU.mult)\
                .then_inc(S("gain_ok"), 1)
            split(0, range(SLOTS))
            norm_rows(0, resid)
            turn(0, GAIN["mix"])
            dve.wait_ge(S("lam_read"), 1)
            own(dve.tensor_tensor(neglam, lam[:, 1:2], lam[:, 0:1], ALU.subtract))
            own(dve.tensor_scalar(neglam, neglam, -LAMBDA_INIT, None, ALU.add))

            n_cols = [0]

            def keep_tiles(dst, first_block):
                def epilogue(blk, par, i):
                    add_low(blk, par, blk - first_block, dst[:, bass.ds(4 * i, 4), :]).then_inc(acc_freed, 1)
                return epilogue

            def nothing(blk, par, i):
                pass

            pairs("qk", 4, keep_tiles(tiles_a, 0))
            pairs("qkr", 4, keep_tiles(tiles_b, 0))
            cols_so_far = 8
            pairs("va", 2, nothing)
            pairs("vr", 4, nothing)

            s1, qn, on = temp[:, 0:512], temp[:, 512:1024], temp[:, 1536:1792]
            both = tiles_a.rearrange("p (s h) t -> p s h t", s=2)

            def scores(src, slope, done_sem):
                own(dve.scalar_tensor_tensor(s_buf, dist, slope, src, ALU.mult, ALU.add))
                own(dve.tensor_reduce(top, s_buf.rearrange("p (t k) -> p t k", t=NT), AX.X, ALU.max))
                dve.tensor_scalar(negtop, top, -A_SCALE, None, ALU.mult).then_inc(done_sem, 1)

            s_buf = s1
            with dve.Fori(0, A_HEADS) as h:
                own.begin(h, 1)
                for n in range(2):
                    ins = dve.tensor_tensor(s1[:, n * SEQ:n * SEQ + SEQ], tiles_a[:, bass.ds(8 * n + h, 1), :],
                                            tiles_a[:, bass.ds(8 * n + h, 1), :], ALU.mult)
                ins.then_inc(S("a_sq"), 1)
                dve.wait_ge(S("a_root"), h + 1)
                own(dve.reciprocal(qn, qn))
                for n in range(2):
                    x = tiles_a[:, bass.ds(8 * n + h, 1), :]
                    ins = dve.scalar_tensor_tensor(x, x, gains[:, GAIN["q"] + n:GAIN["q"] + n + 1],
                                                   qn[:, n * SEQ:n * SEQ + SEQ].rearrange("p (n t) -> p n t", n=1),
                                                   ALU.mult, ALU.mult)
                ins.then_inc(S("a_qn"), 1)
            own.end(A_HEADS)
            with dve.Fori(0, A_HEADS) as h:
                own.begin(h, 4)
                dve.wait_ge(S("a_score"), h + 1)
                scores(ps[:, 5, :], slopes1[:, bass.ds(h, 1)], S("a_top"))
                dve.wait_ge(S("a_exp"), h + 1)
                own(dve.reciprocal(recip, total))
                dve.wait_ge(S("a_o"), h + 1)
                for t in range(NT):
                    ins = dve.tensor_scalar(on[:, t * P:t * P + P], ps[:, 7, t * P:t * P + P], recip[:, t:t + 1], None, ALU.mult)
                ins.then_inc(S("a_on"), 1)
                dve.wait_ge(S("a_hi"), h + 1)
                own(dve.tensor_tensor(oaT[:, bass.ds(h, 1), 1, :], ps[:, 4, 0:SEQ], oaT[:, bass.ds(h, 1), 0, :].bitcast(F32),
                                      ALU.subtract))
                dve.sem_inc(S("a_done"), 1)
            own.end(A_HEADS)

            aT = temp[:, 512:1024]
            with dve.Fori(0, R_HEADS) as h:
                own.begin(h, 3)
                dve.wait_ge(S("r_score"), h + 1)
                dve.tensor_tensor(aT, ps[:, 4, :], decay[:, bass.ds(h * 512, 512)], ALU.mult).then_inc(S("r_a"), 1)
                dve.wait_ge(S("r_o"), h + 1)
                for t in range(NT):
                    ins = dve.bn_stats(bn[:, 6 * t:6 * t + 6], ps[:, 6 + t, :])
                own(ins)
                dve.memset(spare, 0.0)
                for t in range(NT):
                    ins = dve.bn_aggr(mv[:, 2 * t:2 * t + 2], bn[:, 6 * t:6 * t + 6])
                ins.then_inc(S("r_var"), 1)
                dve.wait_ge(S("r_root"), h + 1)
                own(dve.reciprocal(rstd, rstd))
                for t in range(NT):
                    ins = dve.tensor_scalar(resid[:, t, bass.ds(h * 512, 512)], ps[:, 6 + t, :], mv[:, 2 * t:2 * t + 1],
                                            rstd[:, t:t + 1], ALU.subtract, ALU.mult)
                own(ins)
                dve.sem_inc(S("r_done"), 1)
            own.end(R_HEADS)

            def times_silu(blk, par, i):
                dve.wait_ge(S("silu"), i + 1)
                o = resid[:, :, bass.ds(i * 512, 512)]
                dve.tensor_tensor(o, o, lo_sum.rearrange("p (t n) -> p t n", t=NT), ALU.mult).then_inc(acc_freed, 1)

            pairs("gr", 4, times_silu)
            dve.wait_ge(acc_freed, base["ga"])
            dve.sem_inc(S("rows1"), 1)
            pairs("ga", 4, nothing)
            pairs("gb", 4, nothing)
            for j in range(2):
                blk = base["oa"] + j
                ahead(blk)
                dve.wait_ge(acc_ready, blk + 1)
                for t in range(NT):
                    m = rows_d[:, t, j * CHUNK:(j + 1) * CHUNK].rearrange("p (f n) -> p f n", f=2)
                    acc = ps[:, 4 * j:4 * j + 4, :].rearrange("p (f t) n -> p f t n", t=NT)[:, :, t, :]
                    ins = dve.tensor_tensor(m, m, acc, ALU.mult)
                ins.then_inc(acc_freed, 1)
            turn(1)

            def merge(blk, par, i):
                dve.wait_ge(acc_ready, blk + 1)
                cs = bass.ds(i * 512, 512)
                own(dve.tensor_tensor(rows_a[:, :, cs], rows_a[:, :, cs], ps[:, 2 * par:2 * par + 2, :], ALU.mult))
                dve.tensor_tensor(rows_d[:, :, cs], rows_d[:, :, cs], rows_a[:, :, cs], ALU.add).then_inc(acc_freed, 1)

            pairs("or", 4, merge, 1)
            dve.wait_ge(acc_freed, base["out"])
            dve.sem_inc(S("rows2"), 1)
            turn(2)

            def add_resid(blk, par, i):
                dve.wait_ge(acc_ready, blk + 1)
                r = resid[:, :, bass.ds(i * 512, 512)]
                dve.tensor_tensor(r, r, ps[:, 2 * par:2 * par + 2, :], ALU.add).then_inc(acc_freed, 1)

            dve.wait_ge(S("x_again"), 16)
            pairs("out", 4, add_resid)
            dve.wait_ge(acc_freed, base["ff"])
            dve.sem_inc(S("norm_in3"), 1)
            norm_rows(3, rows_d)
            turn(3, GAIN["ffn"])

            gate4 = gate_t.rearrange("p (f t) -> p f t", f=4)
            up4 = up_t.rearrange("p (f t) -> p f t", f=4)
            prod_t = area_d[:, 3072:4096].rearrange("p (f t) -> p f t", f=4)

            with dve.Fori(0, FBLK) as i:
                blk = base["ff"] + 2 * i
                ahead(blk)
                if True:
                    dve.wait_ge(S("gate0"), i)
                add_low(blk, 0, cols_so_far + 2 * i, gate4).then_inc(acc_freed, 1)
                ahead(blk + 1)
                dve.wait_ge(S("hidden0"), i)
                add_low(blk + 1, 1, cols_so_far + 2 * i + 1, prod_t).then_inc(acc_freed, 1)
            cols_so_far += 2 * FBLK

            def feed_out(name, u, last):
                b = base[name]

                def one(i, blk, buf, more=True):
                    split(blk, range(SLOTS, CPB))
                    if more:
                        stage(i + 1, 1 - buf)
                        split(blk + 1, range(SLOTS))

                def stage(i, buf):
                    dve.wait_ge(S(f"stage_hi{u}"), i + 1)
                    dve.tensor_tensor(staged[:, buf, :, 1, :], hidden[:, bass.ds(4 * i, 4), :],
                                      staged[:, buf, :, 0, :].bitcast(F32), ALU.subtract).then_inc(S(f"staged{u}"), 1)

                stage(0, 0)
                one(0, b, 0)
                with dve.Fori(0, (FBLK - 3) // 2) as i:
                    one(2 * i + 1, b + 2 * i + 1, 1)
                    one(2 * i + 2, b + 2 * i + 2, 0)
                one(FBLK - 2, b + FBLK - 2, 1)
                one(FBLK - 1, b + FBLK - 1, 0, False)
                if not last:
                    split(b + FBLK, range(SLOTS))
                dve.wait_ge(acc_ready, b + FBLK)

            feed_out("fo", 0, False)
            for t in range(NT):
                r = resid[:, t, :].rearrange("p (f n) -> p f n", f=4)
                own(dve.tensor_tensor(r, r, ps[:, 4 * t:4 * t + 4, :], ALU.add))
            dve.sem_inc(acc_freed, FBLK)
            dve.sem_inc(S("norm_in4"), 1)
            norm_rows(4, rows_d)
            turn(4, GAIN["pre2"])

            first_col = cols_so_far
            pairs("gqk", 2, lambda blk, par, i: add_low(blk, par, blk - base["gqk"] + first_col,
                                                        tiles_b[:, bass.ds(4 * i, 4), :]).then_inc(acc_freed, 1))
            pairs("dqk", 4, lambda blk, par, i: add_low(blk, par, blk - base["gqk"] + first_col,
                                                        tiles_a[:, bass.ds(4 * i, 4), :]).then_inc(acc_freed, 1))
            blk = base["al"]
            cols_so_far += 6
            ahead(blk)
            dve.wait_ge(lo_copied, cols_so_far + 1)
            own(dve.tensor_tensor(temp[0:16, 0:SEQ], ps[0:16, 0, 0:SEQ], lo_sum[0:16, 0:SEQ], ALU.add))
            dve.sem_inc(acc_freed, 1)
            dve.sem_inc(S("g_ga"), 1)
            cols_so_far += 1
            log_a = temp[:, 1024:2048]
            dve.wait_ge(S("g_ln"), 1)
            dve.scalar_tensor_tensor(log_a.rearrange("p (t n) -> p t n", t=NT), ps[:, 6:8, :], 0.0,
                                     free_c[:, 0:1024].rearrange("p (t n) -> p t n", t=NT),
                                     ALU.min, ALU.subtract).then_inc(S("g_log"), 1)
            pairs("gv", 2, nothing)
            pairs("dv", 2, nothing)

            decays = free_c[:, 0:9 * P]
            ke, qe = area_g[:, 0:LW], area_g[:, LW:2 * LW]
            sT, cross = temp[:, 0:512], temp[:, 512:768]
            lev = decays[:, 0:LW].rearrange("p (n c) -> p n c", c=P)
            gain_g, gain_d = free_c[:, 1280:1536], free_c[:, 1536:1792]
            dve.wait_ge(S("second_in"), 16)
            dve.wait_ge(S("norms_in"), 32)
            dve.wait_ge(S("g_z"), 1)
            for n in (gain_g, gain_d):
                dve.tensor_scalar(n, n, SEQ ** 0.5 * (1.0 - LAMBDA_INIT if n is gain_d else 1.0), None, ALU.mult)
            own(dve.memset(sT, 0.0))
            G_PER = 9
            with dve.Fori(0, G_HEADS) as h:
                own.begin(h, G_PER)
                for t in range(NT):
                    dve.wait_ge(S("g_exp"), 2 * h + t + 1)
                    if t == 0:
                        dve.wait_ge(S("g_sq"), h)
                    k = tiles_b[:, bass.ds(4 + h, 1), t * P:t * P + P]
                    q = tiles_b[:, bass.ds(h, 1), t * P:t * P + P]
                    dve.tensor_tensor(ke.rearrange("p (n c) -> p n c", c=P), lev, k.to_broadcast([P, LEVELS, P]), ALU.mult)
                    dve.tensor_tensor(qe.rearrange("p (n c) -> p n c", c=P), lev, q.to_broadcast([P, LEVELS, P]), ALU.mult)
                    ins = dve.tensor_tensor(cross[:, t * P:t * P + P].rearrange("p (n c) -> p n c", n=1),
                                            decays[:, LW:].rearrange("p (n c) -> p n c", n=1), (k, q)[t], ALU.mult)
                    own(ins)
                    dve.sem_inc(S("g_qk"), 1)
                    dve.wait_ge(S("g_score"), 2 * h + t + 1)
                    own(dve.tensor_tensor(decays[:, 0:LW].rearrange("p (n c) -> p n c", n=2), ps[:, 4:6, :],
                                          masks_m.rearrange("p (n c) -> p n c", n=2), ALU.mult))
                    own(dve.tensor_reduce(sT[:, t * SEQ + t * P:t * SEQ + t * P + P], decays[:, 0:LW].rearrange("p (n c) -> p c n", c=P),
                                          AX.X, ALU.add))
                    dve.sem_inc(S("g_sT"), 1)
                dve.wait_ge(S("g_cross"), h + 1)
                own(dve.tensor_copy(sT[:, P:SEQ], ps[:, 6, P:2 * P]))
                dve.sem_inc(S("g_sT"), 1)
                dve.wait_ge(S("g_sq"), h + 1)
                own(dve.reciprocal(orstd, osum))
                for t in range(NT):
                    ins = dve.scalar_tensor_tensor(rows_d[:, t, bass.ds(h * SEQ, SEQ)], ps[:, 7, t * SEQ:t * SEQ + SEQ],
                                                   orstd[:, t:t + 1], gain_g, ALU.mult, ALU.mult)
                own(ins)
                dve.sem_inc(S("g_done"), 1)
            own.end(G_HEADS)

            diff = temp[:, 0:512]
            s_buf = temp[:, 512:1024]
            with dve.Fori(0, D_HEADS) as h:
                own.begin(h, 11)
                for c in range(2):
                    dve.wait_ge(S("d_score"), 2 * h + c + 1)
                    scores(ps[:, 4, :], slopes2[:, bass.ds(h, 1)], S("d_top"))
                    dve.wait_ge(S("d_exp"), 2 * h + c + 1)
                    own(dve.reciprocal(recip, total))
                    if c == 0:
                        for t in range(NT):
                            ins = dve.tensor_scalar(diff[:, t * SEQ:t * SEQ + SEQ], s_buf[:, t * SEQ:t * SEQ + SEQ],
                                                    recip[:, t:t + 1], None, ALU.mult)
                        own(ins)
                    else:
                        own(dve.tensor_scalar(recip2, recip, neglam, None, ALU.mult))
                        for t in range(NT):
                            ins = dve.scalar_tensor_tensor(diff[:, t * SEQ:t * SEQ + SEQ], s_buf[:, t * SEQ:t * SEQ + SEQ],
                                                           recip2[:, t:t + 1], diff[:, t * SEQ:t * SEQ + SEQ], ALU.mult, ALU.add)
                        own(ins)
                        dve.sem_inc(S("d_p"), 1)
                dve.wait_ge(S("d_sq"), h + 1)
                own(dve.reciprocal(orstd, osum))
                for t in range(NT):
                    ins = dve.scalar_tensor_tensor(rows_d[:, t, bass.ds(1024 + h * SEQ, SEQ)], ps[:, 6, t * SEQ:t * SEQ + SEQ],
                                                   orstd[:, t:t + 1], gain_d, ALU.mult, ALU.mult)
                own(ins)
                dve.sem_inc(S("d_done"), 1)
            own.end(D_HEADS)

            def times_silu2(blk, par, i):
                dve.wait_ge(S("silu2"), i + 1)
                o = rows_d[:, :, bass.ds(i * 512, 512)]
                dve.tensor_tensor(o, o, area_g[:, 0:1024].rearrange("p (t n) -> p t n", t=NT), ALU.mult).then_inc(acc_freed, 1)

            pairs("gg", 2, times_silu2)
            dve.wait_ge(acc_freed, base["o2"])
            dve.sem_inc(S("rows5"), 1)
            turn(5)

            def keep_m(blk, par, i):
                dve.wait_ge(acc_ready, blk + 1)
                dve.tensor_copy(rows_a[:, :, bass.ds(i * 512, 512)], ps[:, 2 * par:2 * par + 2, :]).then_inc(acc_freed, 1)

            def post_norm(u, posted):
                row_scale(u)
                own(dve.tensor_scalar(rstd, rstd, DM ** 0.5, None, ALU.mult))
                dve.wait_ge(posted, 16)
                for t in range(NT):
                    own(dve.scalar_tensor_tensor(rows_a[:, t, :], rows_a[:, t, :], rstd[:, t:t + 1], area_g[:, :], ALU.mult, ALU.mult))
                own(dve.tensor_tensor(resid[:, :, :], resid[:, :, :], rows_a[:, :, :], ALU.add))

            pairs("o2", 4, keep_m)
            dve.wait_ge(acc_freed, base["ff2"])
            dve.sem_inc(S("norm_in7"), 1)
            post_norm(7, S("post_in"))
            dve.sem_inc(S("norm_in6"), 1)
            norm_rows(6, rows_d)
            turn(6, GAIN["ffn2"])

            own(dve.memset(conv_in, 0.0))
            own.straight()
            with dve.Fori(0, FBLK) as i:
                blk = base["ff2"] + 2 * i
                own.begin(i, 3)
                ahead(blk)
                own(add_low(blk, 0, cols_so_far + 2 * i, conv_in[:, :, 2:]))
                dve.sem_inc(acc_freed, 1)
                dve.wait_ge(S("gate1"), i)
                for tap in range(3):
                    for f in range(4):
                        src = conv_in[:, f, tap:tap + SEQ]
                        w = conv[:, bass.ds(tap * FT + 4 * i + f, 1)]
                        dst = gate_t[:, f * SEQ:f * SEQ + SEQ]
                        if tap == 0:
                            ins = dve.tensor_scalar(dst, src, w, None, ALU.mult)
                        else:
                            ins = dve.scalar_tensor_tensor(dst, src, w, dst, ALU.mult, ALU.add)
                    if tap < 2:
                        own(ins)
                ins.then_inc(S("conv_done"), 1)
                ahead(blk + 1)
                dve.wait_ge(S("hidden1"), i)
                add_low(blk + 1, 1, cols_so_far + 2 * i + 1, prod_t).then_inc(acc_freed, 1)
            own.end(FBLK)
            feed_out("fo2", 1, True)
            for t in range(NT):
                ins = dve.tensor_copy(rows_a[:, t, :].rearrange("p (f n) -> p f n", f=4), ps[:, 4 * t:4 * t + 4, :])
            own(ins)
            dve.sem_inc(S("norm_in8"), 1)
            post_norm(8, S("post_in2"))
            dve.sem_inc(S("y_ready"), 1)

        @block.gpsimd
        def _(pool):
            g = area_g[:, 0:3 * P].rearrange("p (n d) -> p n d", d=P)
            for name, at in (("norm_mix", 0), ("norm_ffn", 16), ("attn_pre_norm_2", 32), ("ffn_pre_norm_2", 48)):
                pool.dma_start(g[at:at + 16, 0, :], a[name].rearrange("l (k d) -> (l k) d", d=P)).then_inc(S("gains_in"), 16)
            for n, name in enumerate(("q_norm", "k_norm", "lambda_q1_2", "lambda_k1_2", "lambda_q2_2", "lambda_k2_2")):
                pool.dma_start(g[64 + n:65 + n, 0, :], a[name]).then_inc(S("gains_in"), 16)
            half = CONV_ROWS // 2
            taps = a["conv_w_2"].rearrange("l w (f d) -> (l w f) d", d=P)
            pool.dma_start(g[0:half, 1, :], taps[0:half, :]).then_inc(S("gains_in"), 16)
            pool.dma_start(g[0:half // 2, 2, :], taps[half:, :]).then_inc(S("gains_in"), 16)
            pool.dma_start(g[half // 2:half, 2, :], a["conv_b_2"].rearrange("l (f d) -> (l f) d", d=P)).then_inc(S("gains_in"), 16)
            pool.dma_start(masks[:, 0:R_HEADS * NT * SEQ], c_decay).then_inc(S("decay_in"), 16)

            q_st = temp[:, 512:768].rearrange("p (n t) -> p n t", n=1)
            pool.wait_ge(S("a_qn"), A_HEADS)
            with pool.Fori(0, A_HEADS) as h:
                pool.wait_ge(S("a_score"), h)
                pool.tensor_copy(q_st, tiles_a[:, bass.ds(h, 1), :]).then_inc(S("a_q"), 1)

            kst = temp[:, 0:512].rearrange("p (d t) -> p d t", d=2)
            pool.wait_ge(S("a_done"), A_HEADS)
            pool.wait_ge(S("decay_in"), 16)
            with pool.Fori(0, R_HEADS) as h:
                pool.wait_ge(S("r_done"), h)
                pool.tensor_copy(kst, tiles_b[:, bass.ds(8 + 2 * h, 2), :]).then_inc(S("r_k"), 1)
            pool.wait_ge(S("r_done"), R_HEADS)
            pool.dma_start(masks[:, :], c_second).then_inc(S("second_in"), 16)
            pool.wait_ge(S("turned1"), KT // 2)
            pool.dma_start(resid[:, :, :], a["x"].rearrange("b (t p) n -> p (b t) n", p=P)).then_inc(S("x_again"), 16)

            prod = area_d[:, 3072:4096].rearrange("p (f t) -> p f t", f=4)
            up4 = up_t.rearrange("p (f t) -> p f t", f=4)

            def hidden_of(u, name):
                with pool.Fori(0, FBLK) as i:
                    pool.wait_ge(S(f"gate{u}"), i + 1)
                    pool.wait_ge(acc_freed, base[name] + 2 * i + 2)
                    pool.tensor_tensor(hidden[:, bass.ds(4 * i, 4), :], up4, prod, ALU.mult).then_inc(S(f"hidden{u}"), 1)

            hidden_of(0, "ff")
            pool.dma_start(area_g[0:16, 0:512], a["w_alpha_up_2"].rearrange("l k n -> (l k) n")).then_inc(S("alpha_in"), 16)
            pool.dma_start(area_g[0:1, 512:1024], a["b_alpha_2"]).then_inc(S("alpha_in"), 16)
            pool.wait_ge(S("staged0"), FBLK)
            for n, name in enumerate(("gla_norm_2", "diff_norm_2")):
                pool.dma_start(free_c[:, 1280 + n * SEQ:1280 + (n + 1) * SEQ], a[name].to_broadcast([P, SEQ])).then_inc(S("norms_in"), 16)
            la = temp[:, 1024:2048].rearrange("p (t n) -> p t n", t=NT)
            pool.wait_ge(S("g_log"), 1)
            with pool.Fori(0, G_HEADS) as h:
                pool.wait_ge(S("g_sum"), 2 * h)
                pool.tensor_copy(temp[:, 768:1024].rearrange("p (t n) -> p t n", t=NT), la[:, :, bass.ds(h * P, P)])\
                    .then_inc(S("g_la"), 1)
            pool.wait_ge(S("g_done"), G_HEADS)
            with pool.Fori(0, D_HEADS) as h:
                for c in range(2):
                    pool.wait_ge(S("d_score"), 2 * h + c)
                    pool.tensor_copy(temp[:, 1536:1792].rearrange("p (n t) -> p n t", n=1), tiles_a[:, bass.ds(2 * h + c, 1), :])\
                        .then_inc(S("d_q"), 1)
            pool.wait_ge(acc_freed, base["o2"])
            pool.dma_start(area_g[:, :], a["attn_post_norm_2"].to_broadcast([P, DM])).then_inc(S("post_in"), 16)
            pool.wait_ge(S("norm_in6"), 1)
            pool.dma_start(area_g[:, :], a["ffn_post_norm_2"].to_broadcast([P, DM])).then_inc(S("post_in2"), 16)
            hidden_of(1, "ff2")


_INS = ["x", "w_in", "w_o_attn", "w_o_ret", "w_out", "q_norm", "k_norm", "norm_mix", "norm_ffn", "w_ffn_in", "w_ffn_out",
        "attn_pre_norm_2", "w_in_2", "w_alpha_up_2", "b_alpha_2", "gla_norm_2", "lambda_q1_2", "lambda_k1_2",
        "lambda_q2_2", "lambda_k2_2", "diff_norm_2", "w_o_2", "attn_post_norm_2", "ffn_pre_norm_2", "w_ffn_in_2",
        "conv_w_2", "conv_b_2", "w_ffn_out_2", "ffn_post_norm_2"]


def kernel(**inputs):
    import concourse.bacc as bacc
    from concourse.bass_utils import run_bass_kernel_spmd

    nc = bacc.Bacc("TRN2", target_bir_lowering=False, num_devices=1)
    arrays, aps = {}, {}
    for name in _INS:
        arrays[name] = np.ascontiguousarray(inputs[name])
        aps[name] = nc.dram_tensor(name, arrays[name].shape, F32, kind="ExternalInput").ap()
    consts = []
    for name, value in zip(("shape_first", "shape_decay", "shape_second"), shape_constants()):
        arrays[name] = np.ascontiguousarray(value)
        consts.append(nc.dram_tensor(name, value.shape, F32, kind="ExternalInput").ap())
    out = nc.dram_tensor("y", (1, SEQ, DM), F32, kind="ExternalOutput").ap()
    two_blocks(nc, aps, out, *consts)
    r = run_bass_kernel_spmd(nc, [arrays], core_ids=[0])
    return r.results[0]["y"]
```

```python
from contextlib import ExitStack

import numpy as np
import concourse.bass as bass
from concourse import mybir

F32 = mybir.dt.float32
F32R = mybir.dt.float32r
ALU = mybir.AluOpType
ACT = mybir.ActivationFunctionType
AX = mybir.AxisListType

P = 128
SEQ = 256
NT = SEQ // P
DM = 2048
KT = DM // P
EPS = 1e-6
CHUNK = 1024
CPB = 8
SLOTS = 4
FF = 5632
FT = FF // P
FBLK = FF // 512
A_HEADS = 8
HOSTED = 4
R_HEADS = 4
G_HEADS = 4
D_HEADS = 4
A_SCALE = 128 ** -0.5
LAMBDA_INIT = 0.2
MASKED = 1e30
LEVELS = 8
LW = LEVELS * P

GAIN = {"mix": 0, "ffn": 16, "pre2": 32, "ffn2": 48, "q": 64, "k": 65, "lq1": 66, "lk1": 67, "lq2": 68, "lk2": 69}
GAIN_ROWS = 70
CONV_ROWS = 4 * FT


def shape_constants():
    i = np.arange(P)
    ident = np.eye(P)
    ones = np.ones((P, P))
    q = np.arange(SEQ).reshape(NT, P).T[:, :, None]
    rel = q - np.arange(SEQ)[None, None, :]
    dist = np.where(rel >= 0, rel, MASKED).reshape(P, NT * SEQ)
    log_g = np.log(1.0 - 2.0 ** (-5.0 - np.arange(R_HEADS)))
    j = np.arange(SEQ).reshape(NT, P).T[:, None, :, None]
    gap = np.arange(SEQ)[None, None, None, :] - j
    decay = np.where(gap >= 0, np.exp(log_g[None, :, None, None] * np.maximum(gap, 0)), 0.0) * 256 ** -0.5
    sums, masks = [], []
    for s in (64, 32, 16, 8, 4, 2, 1):
        t, u = i[None, :], i[:, None]
        right = (t // s) % 2 == 1
        seam = np.where(right, t // s * s, (t // s + 1) * s)
        sums.append(np.where(right, (u >= seam) & (u <= t), (u > t) & (u < seam)))
        masks.append((u // (2 * s) == t // (2 * s)) & ((u // s) % 2 == 0) & right)
    sums.append(np.zeros((P, P)))
    masks.append(np.eye(P))
    sums.append(i[:, None] > i[None, :])
    sums.append(i[:, None] <= i[None, :])
    first = np.concatenate([ident, ones, dist], 1)
    second = np.concatenate([m.astype(np.float64) for m in sums + masks], 1)
    return (first.astype(np.float32), decay.reshape(P, -1).astype(np.float32), second.astype(np.float32))


class Chain:

    def __init__(self, eng, sem):
        self.eng, self.sem, self.base, self.k, self.at = eng, sem, 0, 0, None

    def __call__(self, ins):
        self.k += 1
        ins.then_inc(self.sem, 1)
        value = self.base + self.k
        if self.at is not None:
            i, per = self.at
            value = i * per + value
        self.eng.wait_ge(self.sem, value)

    def straight(self):
        self.base, self.k, self.at = self.base + self.k, 0, None

    def begin(self, i, per):
        self.straight()
        self.at = (i, per)

    def end(self, n):
        assert self.k == self.at[1], (self.k, self.at)
        self.base, self.k, self.at = self.base + n * self.k, 0, None


def two_blocks(nc, a, out, c_first, c_decay, c_second):
    with ExitStack() as ctx:
        def sb(name, shape, dt=F32):
            return ctx.enter_context(nc.sbuf_tensor(name, shape, dt))

        sems = {}

        def S(name):
            if name not in sems:
                sems[name] = ctx.enter_context(nc.semaphore(name))
            return sems[name]

        raw = sb("raw", [P, SLOTS, CHUNK])
        whi = sb("whi", [P, SLOTS, CHUNK], F32R)
        wlo = sb("wlo", [P, SLOTS, CHUNK], F32R)
        hT = sb("hT", [P, KT, 2, SEQ], F32R)
        big = sb("big", [P, 48 * SEQ])
        area_d = sb("area_d", [P, NT * DM])
        split_e = sb("split_e", [P, 16, SEQ], F32R)
        resid = sb("resid", [P, NT, DM])
        area_g = sb("area_g", [P, 2048])
        temp = sb("temp", [P, 2048])
        first = sb("first", [P, 2 * P + NT * SEQ])
        masks = sb("masks", [P, 10 * P + LW])
        gains = sb("gains", [P, GAIN_ROWS])
        conv = sb("conv", [P, CONV_ROWS])
        small = sb("small", [P, 96])

        ident, ones = first[:, 0:P], first[:, P:2 * P]
        dist = first[:, 2 * P:]
        decay = masks[:, 0:R_HEADS * NT * SEQ]
        sums_m, masks_m = masks[:, 0:10 * P], masks[:, 10 * P:]

        area = [big[:, n * 16 * SEQ:(n + 1) * 16 * SEQ] for n in range(3)]
        tiles_a = area[0].rearrange("p (n t) -> p n t", t=SEQ)
        rows_a = area[0].rearrange("p (t n) -> p t n", t=NT)
        tiles_b = area[1].rearrange("p (n t) -> p n t", t=SEQ)
        gv = area[1][:, 2048:].rearrange("p (t n) -> p t n", t=NT)
        rows_m = area[1].rearrange("p (t n) -> p t n", t=NT)
        rows_c = area[2].rearrange("p (t n) -> p t n", t=NT)
        dv = area[2][:, 0:2048].rearrange("p (t n) -> p t n", t=NT)
        free_c = area[2][:, 2048:]
        hidden = big[:, 0:FT * SEQ].rearrange("p (n t) -> p n t", t=SEQ)
        rows_d = area_d[:, :].rearrange("p (t n) -> p t n", t=NT)
        va = area_g[:, :].rearrange("p (t n) -> p t n", t=NT)
        head_sq, head_root = area_d[:, 1024:1536], area_d[:, 1536:2048]
        lo_sum = area_d[:, 0:1024]
        gate_t = area_d[:, 1024:2048]
        up_t = area_d[:, 2048:3072]
        conv_in = temp[:, 0:4 * (2 + SEQ)].rearrange("p (f t) -> p f t", f=4)
        oaT = split_e[:, :, :].rearrange("p (h s) t -> p h s t", s=2)
        staged = split_e[:, :, :].rearrange("p (b k s) t -> p b k s t", b=2, s=2)

        ps = ctx.enter_context(nc.psum_tensor("ps", [P, 8, 512], F32))

        col = {}

        def keep(name, n):
            at = sum(w for _, w in col.values())
            col[name] = (at, n)
            return small[:, at:at + n]

        sumsq = keep("sumsq", 2)
        rstd = keep("rstd", 2)
        slopes1 = keep("slopes1", A_HEADS)
        slopes2 = keep("slopes2", D_HEADS)
        top = keep("top", 2)
        negtop = keep("negtop", 2)
        total = keep("total", 2)
        recip = keep("recip", 2)
        bn = keep("bn", 12)
        mv = keep("mv", 4)
        lam = keep("lam", 2)
        neglam = keep("neglam", 1)
        lamprod = keep("lamprod", 2)
        unit = keep("unit", 1)
        parts = keep("parts", 8)
        top4 = keep("top4", 4)
        negtop4 = keep("negtop4", 4)
        total4 = keep("total4", 4)
        recip4 = keep("recip4", 4)
        osum = keep("osum", 2)
        orstd = keep("orstd", 2)
        spare = keep("spare", 1)
        eps = {n: keep(f"eps_{n}", 1) for n in ("head", "model", "one", "gla", "diff")}

        order = [("qk", 4), ("qkr", 4), ("va", 2), ("vr", 4), ("ga", 4), ("gb", 4), ("gr", 4), ("oa", 2), ("or", 4),
                 ("out", 4), ("ff", 2 * FBLK), ("fo", FBLK),
                 ("gqk", 2), ("dqk", 4), ("al", 1), ("gv", 2), ("gg", 2), ("dv", 2), ("o2", 4),
                 ("ff2", 2 * FBLK), ("fo2", FBLK)]
        base, n_blocks = {}, 0
        for name, n in order:
            base[name] = n_blocks
            n_blocks += n

        loaded = [S(f"loaded{s}") for s in range(SLOTS)]
        hi_ready, lo_ready, split_used = S("hi_ready"), S("lo_ready"), S("split_used")
        acc_freed = S("acc_freed")
        lo_copied = S("lo_copied")

        def wcols(w):
            return a[w].rearrange("l (k p) n -> p (l k) n", p=P)

        x_rows = a["x"].rearrange("b (t p) n -> p (b t) n", p=P)
        half_conv = CONV_ROWS // 2
        g_rows = area_g[:, 0:3 * P].rearrange("p (n d) -> p n d", d=P)

        block = ctx.enter_context(nc.Block())

        @block.sync
        def _(sp):
            def chunk_in(blk, c, src):
                if not (isinstance(blk, int) and blk * CPB + c < SLOTS):
                    sp.wait_ge(lo_ready, blk * CPB + c - SLOTS + 1)
                dst = raw[:, c % SLOTS, :]
                if len(src.shape) == 3:
                    dst = dst.rearrange("p (k n) -> p k n", k=2)[:, :, 0:src.shape[2]]
                sp.dma_start(dst, src).then_inc(loaded[c % SLOTS], 16)

            def wide(blk, w, col0, n=512, cs=range(CPB)):
                for c in cs:
                    chunk_in(blk, c, wcols(w)[:, 2 * c:2 * c + 2, bass.ds(col0, n)])

            def run(name, n, w, col0):
                with sp.Fori(0, n) as i:
                    wide(base[name] + i, w, col0 + i * 512)

            def tall(blk, w, kt0, col0):
                for c in range(CPB):
                    chunk_in(blk, c, wcols(w)[:, kt0 + c, col0:col0 + CHUNK])

            def feed_in(name, w):
                with sp.Fori(0, FBLK) as i:
                    wide(base[name] + 2 * i, w, i * 512)
                    wide(base[name] + 2 * i + 1, w, FF + i * 512)

            def feed_out(name, w):
                with sp.Fori(0, FBLK) as i:
                    for c in range(CPB):
                        rows = a[w].rearrange("l k n -> (l k) n")[bass.ds(i * 512 + c % 4 * P, P), :]
                        chunk_in(base[name] + i, c, rows[:, c // 4 * CHUNK:(c // 4 + 1) * CHUNK])

            for t in range(NT):
                sp.dma_start(resid[:, t, :], x_rows[:, t, :]).then_inc(S(f"x_in{t}"), 16)
                if t == 0:
                    sp.dma_start(first[:, :], c_first).then_inc(S("first_in"), 16)
            wide(0, "w_in", 0)
            with sp.Fori(1, 4) as i:
                wide(i, "w_in", i * 512)
            run("qkr", 4, "w_in", 3072)
            run("va", 2, "w_in", 2048)
            run("vr", 4, "w_in", 5120)
            with sp.Fori(0, 8) as i:
                wide(base["ga"] + i, "w_in", 9216 + i * 512)
            run("gr", 4, "w_in", 7168)
            for j in range(2):
                tall(base["oa"] + j, "w_o_attn", 0, j * CHUNK)
            run("or", 4, "w_o_ret", 0)
            run("out", 4, "w_out", 0)
            feed_in("ff", "w_ffn_in")
            feed_out("fo", "w_ffn_out")
            run("gqk", 2, "w_in_2", 0)
            run("dqk", 4, "w_in_2", 3088)
            wide(base["al"], "w_in_2", 3072, P)
            run("gv", 2, "w_in_2", 1024)
            run("gg", 2, "w_in_2", 2048)
            run("dv", 2, "w_in_2", 5136)
            for n in range(4):
                tall(base["o2"] + n, "w_o_2", 8 * (n // 2), n % 2 * CHUNK)
            feed_in("ff2", "w_ffn_in_2")
            feed_out("fo2", "w_ffn_out_2")
            y_rows = out.rearrange("b (t p) n -> p (b t) n", p=P)
            for q in range(4):
                sp.wait_ge(S("y_ready"), q + 1)
                sp.dma_start(y_rows[:, :, q * 512:q * 512 + 512], resid[:, :, q * 512:q * 512 + 512]).then_inc(S("stored"), 16)
            sp.wait_ge(S("stored"), 64)

        @block.tensor
        def _(pe):
            def nothing(c):
                pass

            def acc_free(blk, all_of_them=False):
                if isinstance(blk, int) and blk == 0:
                    return
                pe.wait_ge(acc_freed, blk + 1 if all_of_them else blk)

            def chunk_ready(blk, c, turned, upto):
                if turned is not None:
                    pe.wait_ge(turned, upto)
                pe.wait_ge(lo_ready, blk * CPB + c + 1)

            def cols_block(blk, par, turned=None, side=nothing, whole=False, tiles=4):
                acc_free(blk, whole)
                side(-1)
                for c in range(CPB):
                    chunk_ready(blk, c, turned, c + 1)
                    for k2 in range(2):
                        kt = 2 * c + k2
                        for ft in range(tiles):
                            acc = ps[:, 4 * par + ft, :]
                            f = slice(k2 * 512 + ft * P, k2 * 512 + ft * P + P)
                            pe.matmul(acc, whi[:, c % SLOTS, f], hT[:, kt, :, :], start=(kt == 0), stop=False)
                            mm = pe.matmul(acc[:, 0:SEQ], wlo[:, c % SLOTS, f], hT[:, kt, 0, :], start=False,
                                           stop=(kt == KT - 1))
                    mm.then_inc(split_used, 1)
                    side(c)

            def rows_mm(acc, x, t, c, f, start, stop):
                hi, lo = x[:, 0, t * P:t * P + P], x[:, 1, t * P:t * P + P]
                pe.matmul(acc, hi, whi[:, c % SLOTS, f], start=start, stop=False)
                pe.matmul(acc, hi, wlo[:, c % SLOTS, f], start=False, stop=False)
                return pe.matmul(acc, lo, whi[:, c % SLOTS, f], start=False, stop=stop)

            def rows_block(blk, par, turned=None, side=nothing, whole=False, x=lambda kt: hT[:, kt, :, :]):
                acc_free(blk, whole)
                side(-1)
                for c in range(CPB):
                    chunk_ready(blk, c, turned, c + 1)
                    for k2 in range(2):
                        kt = 2 * c + k2
                        for t in range(NT):
                            mm = rows_mm(ps[:, 2 * par + t, :], x(kt), t, c,
                                         slice(k2 * 512, k2 * 512 + 512), kt == 0, kt == KT - 1)
                    mm.then_inc(split_used, 1)
                    side(c)

            def tall_block(blk, bank, x, side=nothing, turned=None, turned0=0, free=None, whole=True):
                side(-1)
                if free is None:
                    acc_free(blk, whole)
                for c in range(CPB):
                    chunk_ready(blk, c, turned, turned0 + c // 2 + 1)
                    for hc in range(2):
                        if free is not None and c == 0:
                            free(hc)
                        for t in range(NT):
                            mm = rows_mm(ps[:, bank + 2 * hc + t, :], x(c), t, c,
                                         slice(hc * 512, hc * 512 + 512), c == 0, c == CPB - 1)
                    mm.then_inc(split_used, 1)
                    side(c)

            def pairs(name, n, form, side=None, first_side=None, turned=None):
                b, start = base[name], 0
                if first_side is not None:
                    form(b, 0, turned=turned, side=first_side, whole=True)
                    form(b + 1, 1)
                    start = 1
                if start < n // 2:
                    with pe.Fori(start, n // 2) as i:
                        for par in range(2):
                            form(b + 2 * i + par, par, side=(lambda c: side(c, 2 * i + par)) if side else nothing)

            def turn_group(u, src, j, bank, rows, evicted=0):
                pe.wait_ge(S(f"rows{u}"), rows)
                if evicted:
                    pe.wait_ge(S(f"turned{u}"), evicted)
                for k2 in range(2):
                    for t in range(NT):
                        mm = pe.transpose(ps[:, bank, k2 * SEQ + t * P:k2 * SEQ + t * P + P],
                                          src[:, t, (2 * j + k2) * P:(2 * j + k2 + 1) * P], ident)
                mm.then_inc(S(f"turn{u}"), 1)

            def turn_ahead(u, src):
                def side(c):
                    for j in ((0, 1) if c < 0 else (c + 2,)):
                        if j < KT // 2:
                            turn_group(u, src, j, 4 + j % 4, j // 2 + 1, max(0, j - 3))
                return side

            pe.wait_ge(S("first_in"), 16)
            pe.wait_ge(S("gains_in"), 16 * 6)
            pe.wait_ge(S("lambdas_in"), 16 * 4)
            pe.transpose(ps[:, 0, 0:GAIN_ROWS], g_rows[0:GAIN_ROWS, 0, :], ident[0:GAIN_ROWS, 0:GAIN_ROWS])\
                .then_inc(S("gain_t"), 1)
            pe.wait_ge(S("gain_ok"), 1)

            pairs("qk", 4, cols_block, first_side=turn_ahead(0, resid), turned=S("turned0"))
            pairs("qkr", 4, cols_block)
            s1, qst, pT, on = temp[:, 0:512], temp[:, 512:768], temp[:, 1024:1536], temp[:, 1536:1792]

            def head_sum(h, bank):
                pe.wait_ge(S("a_sq"), h + 1)
                pe.matmul(ps[:, bank, :], ones, head_sq, start=True, stop=True).then_inc(S("a_ss"), 1)

            def head_norms(pos):
                if pos == 0:
                    pe.wait_ge(acc_freed, base["va"] + 1)
                if pos % 4 == 1:
                    head_sum(pos // 4, 4)
                if pos == 1:
                    pe.wait_ge(S("conv_in"), 48)
                    for n in range(2):
                        mm = pe.transpose(ps[:, 5 + n, 0:half_conv], g_rows[0:half_conv, 1 + n, :], ident[0:half_conv, 0:half_conv])
                    mm.then_inc(S("conv_t"), 1)
                    pe.wait_ge(S("lam_prod"), 1)
                    pe.matmul(ps[:, 7, 0:2], ones, lamprod, start=True, stop=True).then_inc(S("lam_sum"), 1)

            for n in range(2):
                rows_block(base["va"] + n, n, side=lambda c: head_norms(8 * n + c) if c >= 0 else None)

            def attention(c, h):
                if c == 0:
                    pe.wait_ge(S("a_q"), h + 1)
                    for t in range(NT):
                        mm = pe.matmul(ps[:, 5, t * SEQ:t * SEQ + SEQ], qst[:, t * P:t * P + P], tiles_a[:, bass.ds(8 + h, 1), :],
                                       start=True, stop=True)
                    mm.then_inc(S("a_score"), 1)
                if c == 2:
                    pe.wait_ge(S("a_exp"), h + 1)
                    for kt, t in ((0, 0), (0, 1), (1, 1)):
                        mm = pe.transpose(ps[:, 6, kt * SEQ + t * P:kt * SEQ + t * P + P],
                                          s1[:, t * SEQ + kt * P:t * SEQ + kt * P + P], ident)
                    mm.then_inc(S("a_turn"), 1)
                if c == 3:
                    pe.wait_ge(S("a_pT"), h + 1)
                    v = [va[:, kt, bass.ds(h * P, P)] for kt in range(NT)]
                    pe.matmul(ps[:, 7, 0:P], pT[:, 0:P], v[0], start=True, stop=True)
                    pe.matmul(ps[:, 7, P:2 * P], pT[:, P:2 * P], v[0], start=True, stop=False)
                    pe.matmul(ps[:, 7, P:2 * P], pT[:, SEQ + P:2 * SEQ], v[1], start=False, stop=True)\
                        .then_inc(S("a_o"), 1)
                if c == 4:
                    pe.wait_ge(S("a_on"), h + 1)
                    for t in range(NT):
                        mm = pe.transpose(ps[:, 4, t * P:t * P + P], on[:, t * P:t * P + P], ident)
                    mm.then_inc(S("a_oT"), 1)
                if c == 7:
                    pe.wait_ge(S("a_done"), h + 1)

            def attention_and_norm(c, h):
                attention(c, h)
                if c == 5:
                    head_sum(h + HOSTED, 6)

            pairs("vr", 4, rows_block, side=attention_and_norm)
            pairs("ga", 4, rows_block, side=lambda c, i: attention(c, 4 + i))

            kst, aT = temp[:, 0:512], temp[:, 512:1024]

            def retention(c, h):
                if c == 0:
                    pe.wait_ge(S("r_k"), h + 1)
                    for jt in range(NT):
                        for d in range(2):
                            mm = pe.matmul(ps[:, 4, jt * SEQ:jt * SEQ + SEQ], kst[:, d * SEQ + jt * P:d * SEQ + jt * P + P],
                                           tiles_b[:, bass.ds(2 * h + d, 1), :], start=(d == 0), stop=(d == 1))
                    mm.then_inc(S("r_score"), 1)
                if c == 2:
                    pe.wait_ge(S("r_a"), h + 1)
                    v = [rows_c[:, jt, bass.ds(h * 512, 512)] for jt in range(NT)]
                    pe.matmul(ps[:, 6, :], aT[:, 0:P], v[0], start=True, stop=True)
                    pe.matmul(ps[:, 7, :], aT[:, P:SEQ], v[0], start=True, stop=False)
                    pe.matmul(ps[:, 7, :], aT[:, SEQ + P:2 * SEQ], v[1], start=False, stop=True).then_inc(S("r_o"), 1)
                if c == 7:
                    pe.wait_ge(S("r_done"), h + 1)

            pairs("gb", 4, rows_block, side=retention)
            pairs("gr", 4, rows_block)

            def turn_ret(c):
                if 1 <= c <= 4:
                    for j in (2 * c - 2, 2 * c - 1):
                        turn_group(1, resid, j, 4 + j % 4, 1, max(0, j - 3))

            tall_block(base["oa"], 0, lambda c: oaT[:, c, :, :], side=turn_ret)
            pe.wait_ge(S("turned1"), KT // 2)
            acc_free(base["oa"] + 1)
            tall_block_late = base["oa"] + 1
            for c in range(CPB):
                chunk_ready(tall_block_late, c, None, 0)
                for hc in range(2):
                    for t in range(NT):
                        mm = rows_mm(ps[:, 4 + 2 * hc + t, :], oaT[:, c, :, :], t, c, slice(hc * 512, hc * 512 + 512),
                                     c == 0, c == CPB - 1)
                mm.then_inc(split_used, 1)

            for n in range(4):
                def turn_merged(c):
                    if c == 0 and n == 1:
                        pe.wait_ge(acc_freed, base["or"] + 1)
                    if n in (1, 2) and c in (1, 2):
                        j = 2 * (n - 1) + c - 1
                        turn_group(2, rows_d, j, 4 + j % 4, n)
                rows_block(base["or"] + n, n % 2, side=turn_merged)

            def turn_rest(c):
                if c in (0, 1):
                    for j in (2 * c + 4, 2 * c + 5):
                        turn_group(2, rows_d, j, 4 + j % 4, 3 + c, j - 3)

            def merged(kt):
                return oaT[:, kt, :, :] if kt < 8 else hT[:, kt, :, :]

            for n in range(4):
                rows_block(base["out"] + n, n % 2, turned=None if n else S("turned2"), side=nothing if n else turn_rest, x=merged)

            def feed_out(name, u):
                b = base[name]

                def one(i, blk, buf, start, stop):
                    pe.wait_ge(S(f"staged{u}"), i + 1)
                    for c in range(CPB):
                        if start and c == 0:
                            pe.wait_ge(acc_freed, b)
                        if start and c == 4:
                            pe.wait_ge(acc_freed, b + 1)
                        chunk_ready(blk, c, None, 0)
                        k = c % 4
                        for hc in range(2):
                            for t in range(NT):
                                mm = rows_mm(ps[:, 4 * (c // 4) + 2 * hc + t, :], staged[:, buf, k, :, :], t, c,
                                             slice(hc * 512, hc * 512 + 512), start and k == 0, stop and k == 3)
                        mm.then_inc(split_used, 1)

                one(0, b, 0, True, False)
                with pe.Fori(0, (FBLK - 3) // 2) as i:
                    one(2 * i + 1, b + 2 * i + 1, 1, False, False)
                    one(2 * i + 2, b + 2 * i + 2, 0, False, False)
                one(FBLK - 2, b + FBLK - 2, 1, False, False)
                one(FBLK - 1, b + FBLK - 1, 0, False, True)

            pairs("ff", 2 * FBLK, cols_block, first_side=turn_ahead(3, rows_d), turned=S("turned3"))
            feed_out("fo", 0)

            pairs("gqk", 2, cols_block, first_side=turn_ahead(4, rows_d), turned=S("turned4"))
            pairs("dqk", 4, cols_block)
            cols_block(base["al"], 0, tiles=1)
            gaT = temp[0:16, 0:SEQ]

            def low_rank(c):
                if c == 0:
                    pe.wait_ge(S("g_ga"), 1)
                    pe.wait_ge(S("alpha_in"), 32)
                    for t in range(NT):
                        pe.matmul(ps[:, 6 + t, :], gaT[:, t * P:t * P + P], area_g[0:16, 0:512], start=True, stop=False)
                        mm = pe.matmul(ps[:, 6 + t, :], ones[0:1, :], area_g[0:1, 512:1024], start=False, stop=True)
                    mm.then_inc(S("g_z"), 1)

            for n in range(2):
                rows_block(base["gv"] + n, 1 - n, side=low_rank if n else nothing)

            ke, qe = area_g[:, 0:LW], area_g[:, LW:2 * LW]
            sT, cross, la_h = temp[:, 0:512], temp[:, 512:768], temp[:, 768:1024]

            def linear_attention(c, h):
                if c in (0, 3):
                    t = c // 3
                    if t == 0:
                        pe.wait_ge(S("g_la"), h + 1)
                    else:
                        pe.wait_ge(S("g_sT"), 3 * h + 1)
                    la = la_h[:, t * P:t * P + P]
                    for n in range(2):
                        pe.matmul(ps[:, 4 + n, :], la, sums_m[:, n * 512:n * 512 + 512], start=True, stop=True)
                    pe.matmul(ps[:, 6, 0:P], la, sums_m[:, LW + t * P:LW + t * P + P], start=True, stop=True)\
                        .then_inc(S("g_sum"), 1)
                if c in (2, 5):
                    t = c // 3
                    pe.wait_ge(S("g_q"), 2 * h + t + 1)
                    pe.wait_ge(S("g_k"), 2 * h + t + 1)
                    for n in range(LEVELS):
                        mm = pe.matmul(ps[:, 4 + n // 4, n % 4 * P:n % 4 * P + P], ke[:, n * P:n * P + P],
                                       qe[:, n * P:n * P + P], start=True, stop=True)
                    mm.then_inc(S("g_score"), 1)
                    if t == 1:
                        pe.matmul(ps[:, 6, P:2 * P], cross[:, 0:P], cross[:, P:2 * P], start=True, stop=True)\
                            .then_inc(S("g_cross"), 1)
                if c == 7:
                    pe.wait_ge(S("g_sT"), 3 * h + 3)
                    v = [gv[:, jt, bass.ds(h * SEQ, SEQ)] for jt in range(NT)]
                    pe.matmul(ps[:, 7, 0:SEQ], sT[:, 0:P], v[0], start=True, stop=True)
                    pe.matmul(ps[:, 7, SEQ:], sT[:, P:SEQ], v[0], start=True, stop=False)
                    pe.matmul(ps[:, 7, SEQ:], sT[:, SEQ + P:], v[1], start=False, stop=True).then_inc(S("g_o"), 1)

            pe.wait_ge(S("second_in"), 16)
            with pe.Fori(0, 2) as i:
                for par in range(2):
                    rows_block(base["gg"] + 2 * i + par, 1 - par, side=lambda c: linear_attention(c, 2 * i + par))

            q_h, diff, dT = temp[:, 512:1024], temp[:, 0:512], temp[:, 1024:1536]

            def diff_attention(pos):
                if pos == -1:
                    for j, bank in enumerate((6, 4, 5)):
                        turn_group(5, rows_d, j, bank, j + 1)
                if pos == 3:
                    turn_group(5, rows_d, 3, 7, 4)
                h, step = divmod(pos - 4, 4)
                if step == 0 and 0 <= h < D_HEADS:
                    pe.wait_ge(S("d_p"), h + 1)
                    pe.wait_ge(S("turned5"), 4)
                    for kt, t in ((0, 0), (0, 1), (1, 1)):
                        mm = pe.transpose(ps[:, 6, kt * SEQ + t * P:kt * SEQ + t * P + P],
                                          diff[:, t * SEQ + kt * P:t * SEQ + kt * P + P], ident)
                    mm.then_inc(S("d_turn"), 1)
                if step == 1 and 0 <= h < D_HEADS:
                    pe.wait_ge(S("d_pT"), h + 1)
                    if h:
                        pe.wait_ge(S("rows5"), 4 + h)
                    v = [dv[:, kt, h * SEQ:(h + 1) * SEQ] for kt in range(NT)]
                    pe.matmul(ps[:, 7, 0:SEQ], dT[:, 0:P], v[0], start=True, stop=True)
                    pe.matmul(ps[:, 7, SEQ:], dT[:, P:SEQ], v[0], start=True, stop=False)
                    pe.matmul(ps[:, 7, SEQ:], dT[:, SEQ + P:], v[1], start=False, stop=True).then_inc(S("d_o"), 1)
                h, step = divmod(pos - 1, 4)
                if step == 0 and 0 <= h < D_HEADS:
                    pe.wait_ge(S("d_q"), h + 1)
                    pe.wait_ge(S("turned5"), 3 if h < 2 else 3 + h)
                    for c in range(2):
                        for t in range(NT):
                            mm = pe.matmul(ps[:, 4 + c, t * SEQ:t * SEQ + SEQ], q_h[:, c * SEQ + t * P:c * SEQ + t * P + P],
                                           tiles_a[:, 8 + 2 * h + c, :], start=True, stop=True)
                    mm.then_inc(S("d_score"), 1)
                h, step = divmod(pos - 8, 4)
                if step == 0 and 0 <= h < D_HEADS:
                    pe.wait_ge(S("d_top"), min(h + 2, D_HEADS))
                    turn_group(5, rows_d, 4 + h, 4, 5 + h)

            def last_kept(n):
                def wait(hc):
                    for kept in ("m_kept0", "m_kept1"):
                        pe.wait_ge(S(kept), 2 * n - 1 + hc)
                return wait

            for n in range(4):
                tall_block(base["o2"] + n, 4 if n == 3 else 0, lambda c: hT[:, 8 * (n // 2) + c, :, :],
                           side=lambda c: diff_attention(8 * n + c) if c >= 0 or n == 0 else None,
                           turned=S("turned5") if n in (0, 2) else None, turned0=4 * (n // 2),
                           free=last_kept(n) if n in (1, 2) else None, whole=(n == 0))

            pairs("ff2", 2 * FBLK, cols_block, first_side=turn_ahead(6, rows_d), turned=S("turned6"))
            feed_out("fo2", 1)

        @block.scalar
        def _(act):
            own = Chain(act, S("act_own"))

            def nothing(k):
                pass

            def split(blk, c):
                act.wait_ge(loaded[c % SLOTS], 16 * (2 * blk + c // SLOTS + 1))
                if not (isinstance(blk, int) and blk * CPB + c < SLOTS):
                    act.wait_ge(split_used, blk * CPB + c - SLOTS + 1)
                act.activation(whi[:, c % SLOTS, :], raw[:, c % SLOTS, :], ACT.Copy).then_inc(hi_ready, 1)

            def ahead(blk, side=nothing, more=True):
                side(-1)
                for k in range(CPB):
                    if k < SLOTS:
                        split(blk, k + SLOTS)
                    elif more:
                        split(blk + 1, k - SLOTS)
                    side(k)

            def block_done(blk):
                act.wait_ge(split_used, (blk + 1) * CPB)

            def low_sums(blk, par):
                block_done(blk)
                act.wait_ge(acc_freed, blk + 1)
                act.activation(lo_sum.rearrange("p (f t) -> p f t", f=4), ps[:, 4 * par:4 * par + 4, SEQ:], ACT.Copy)\
                    .then_inc(lo_copied, 1)

            def pairs(name, n, epilogue, side=None, first_side=None):
                b, start = base[name], 0
                if first_side is not None:
                    for par in range(2):
                        ahead(b + par, nothing if par else first_side)
                        epilogue(b + par, par, par)
                    start = 1
                if start < n // 2:
                    with act.Fori(start, n // 2) as i:
                        for par in range(2):
                            ahead(b + 2 * i + par, (lambda k: side(k, 2 * i + par)) if side else nothing)
                            epilogue(b + 2 * i + par, par, 2 * i + par)

            def turn_group(u, j, bank, dst, col0=None):
                act.wait_ge(S(f"turn{u}"), j + 1)
                src = ps[:, bank, :].rearrange("p (k t) -> p k t", k=2)
                if col0 is None:
                    ins = act.activation(dst[:, 2 * j:2 * j + 2, 0, :], src, ACT.Copy)
                else:
                    for k2 in range(2):
                        ins = act.activation(dst[:, 2 * j + k2, 0, :], src[:, k2, :], ACT.Copy,
                                             scale=gains[:, col0 + 2 * j + k2:col0 + 2 * j + k2 + 1])
                ins.then_inc(S(f"turn_hi{u}"), 1)

            def turn_ahead(u, col0):
                def side(k):
                    for j in ((0, 1, 2) if k < 0 else (k + 3,)):
                        if j < KT // 2:
                            turn_group(u, j, 4 + j % 4, hT, col0)
                return side

            def squares(u, src, q, width, ready):
                act.wait_ge(S(f"norm_in{u}"), ready)
                for t in range(NT):
                    ins = act.activation(rows_a[:, t, q * width:(q + 1) * width], src(t, q), ACT.Square,
                                         accum_out=parts[:, 4 * t + q:4 * t + q + 1])
                ins.then_inc(S(f"norm_part{u}"), 1)

            def root(u):
                act.wait_ge(S(f"norm_sum{u}"), 1)
                act.activation(sumsq, sumsq, ACT.Sqrt, bias=eps["model"]).then_inc(S(f"norm_sq{u}"), 1)

            def resid_cols(t, q):
                return resid[:, t, q * 512:q * 512 + 512]

            act.sem_inc(S("gate0"), 1)
            act.sem_inc(S("gate1"), 1)
            for name, at in (("norm_mix", 0), ("norm_ffn", 16), ("attn_pre_norm_2", 32), ("ffn_pre_norm_2", 48)):
                act.dma_start(g_rows[at:at + 16, 0, :], a[name].rearrange("l (k d) -> (l k) d", d=P)).then_inc(S("gains_in"), 16)
            for n, name in enumerate(("q_norm", "k_norm")):
                act.dma_start(g_rows[64 + n:65 + n, 0, :], a[name]).then_inc(S("gains_in"), 16)
            act.wait_ge(S("eps_ok"), 1)
            for t in range(NT):
                act.wait_ge(S(f"x_in{t}"), 16)
                ins = act.activation(rows_d[:, t, :], resid[:, t, :], ACT.Square, accum_out=sumsq[:, t:t + 1])
            own(ins)
            act.activation(sumsq, sumsq, ACT.Sqrt, bias=eps["model"]).then_inc(S("norm_sq0"), 1)
            for c in range(SLOTS):
                split(0, c)
            act.wait_ge(S("gain_ok"), 1)
            pairs("qk", 4, lambda blk, par, i: low_sums(blk, par), first_side=turn_ahead(0, GAIN["mix"]))
            pairs("qkr", 4, lambda blk, par, i: low_sums(blk, par))

            def keep_rows(dst):
                def epilogue(blk, par, i):
                    block_done(blk)
                    act.activation(dst[:, :, bass.ds(i * 512, 512)], ps[:, 2 * par:2 * par + 2, :], ACT.Copy)\
                        .then_inc(acc_freed, 1)
                return epilogue

            s1, pT = temp[:, 0:512], temp[:, 1024:1536]

            def head_root_of(h, bank, first=False):
                act.wait_ge(S("a_ss"), h + 1)
                if not first:
                    act.wait_ge(S("a_qn"), h)
                act.activation(head_root, ps[:, bank, :], ACT.Sqrt, bias=eps["head"]).then_inc(S("a_root"), 1)

            def head_norms(pos):
                if pos % 4 == 1:
                    head_root_of(pos // 4, 4, pos == 1)
                if pos == 15:
                    act.wait_ge(S("lam_sum"), 1)
                    act.activation(lam, ps[:, 7, 0:2], ACT.Exp).then_inc(S("lam_exp"), 1)

            for n in range(2):
                ahead(base["va"] + n, lambda k: head_norms(8 * n + k) if k >= 0 else None)
                keep_rows(va)(base["va"] + n, n, n)

            def attention(k, h):
                if k == 1:
                    act.wait_ge(S("a_top"), h + 1)
                    for t in range(NT):
                        ins = act.activation(s1[:, t * SEQ:t * SEQ + SEQ], s1[:, t * SEQ:t * SEQ + SEQ], ACT.Exp,
                                             bias=negtop[:, t:t + 1], scale=A_SCALE, accum_out=total[:, t:t + 1])
                    ins.then_inc(S("a_exp"), 1)
                if k == 2:
                    act.wait_ge(S("a_turn"), h + 1)
                    act.activation(pT[:, 0:SEQ], ps[:, 6, 0:SEQ], ACT.Copy)
                    act.activation(pT[:, SEQ + P:], ps[:, 6, SEQ + P:], ACT.Copy).then_inc(S("a_pT"), 1)
                if k == 4:
                    act.wait_ge(S("a_oT"), h + 1)
                    act.activation(oaT[:, bass.ds(h, 1), 0, :], ps[:, 4, 0:SEQ], ACT.Copy).then_inc(S("a_hi"), 1)

            def gate_rows(dst, func):
                def epilogue(blk, par, i):
                    block_done(blk)
                    act.activation(dst[:, :, bass.ds(i * 512, 512)], ps[:, 2 * par:2 * par + 2, :], func)\
                        .then_inc(acc_freed, 1)
                return epilogue

            def attention_and_norm(k, h):
                attention(k, h)
                if k == 5:
                    head_root_of(h + HOSTED, 6)

            pairs("vr", 4, keep_rows(rows_c), side=attention_and_norm)
            pairs("ga", 4, gate_rows(rows_d, ACT.Sigmoid), side=lambda k, i: attention(k, 4 + i))

            def retention(k, h):
                if k == 4:
                    act.wait_ge(S("r_var"), h + 1)
                    act.activation(rstd, mv.rearrange("p (t s) -> p t s", s=2)[:, :, 1], ACT.Sqrt, bias=eps["one"])\
                        .then_inc(S("r_root"), 1)

            pairs("gb", 4, gate_rows(rows_a, ACT.Sigmoid), side=retention)

            def silu_in_place(blk, par, i):
                block_done(blk)
                acc = ps[:, 2 * par:2 * par + 2, :]
                act.activation(acc, acc, ACT.Silu).then_inc(S("silu"), 1)

            pairs("gr", 4, silu_in_place)

            def turn_ret(k):
                if 1 <= k <= 4:
                    for j in (2 * k - 2, 2 * k - 1):
                        turn_group(1, j, 4 + j % 4, hT)

            for j in range(2):
                ahead(base["oa"] + j, nothing if j else turn_ret)
            for n in range(4):
                def turn_merged(k):
                    if n in (1, 2) and k in (1, 2):
                        j = 2 * (n - 1) + k - 1
                        turn_group(2, j, 4 + j % 4, oaT)
                ahead(base["or"] + n, turn_merged)

            def out_side(n):
                def side(k):
                    if n == 0 and k in (0, 1):
                        for j in (2 * k + 4, 2 * k + 5):
                            turn_group(2, j, 4 + j % 4, hT)
                    if n and k == 1:
                        squares(3, resid_cols, n - 1, 512, n)
                return side

            for n in range(4):
                ahead(base["out"] + n, out_side(n))
            squares(3, resid_cols, 3, 512, 4)
            root(3)

            def stage(u, i, buf):
                act.activation(staged[:, buf, :, 0, :], hidden[:, bass.ds(4 * i, 4), :], ACT.Copy).then_inc(S(f"stage_hi{u}"), 1)

            def first_stage(u):
                def side(k):
                    if k == 4:
                        act.wait_ge(S(f"hidden{u}"), 2)
                        stage(u, 0, 0)
                return side

            def feed_in(name, gate, col0, u, stage_u):
                b = base[name]

                def pair(i, side):
                    ahead(b + 2 * i, side)
                    low_sums(b + 2 * i, 0)
                    ahead(b + 2 * i + 1, lambda k: gate(k, i))
                    low_sums(b + 2 * i + 1, 1)

                pair(0, turn_ahead(u, col0))
                pair(1, first_stage(stage_u))
                with act.Fori(2, FBLK) as i:
                    pair(i, nothing)

            def silu_gate(k, i):
                if k == 1:
                    act.wait_ge(S("gate_sum"), i + 1)
                    act.wait_ge(S("hidden0"), i + 1)
                    act.activation(up_t, gate_t, ACT.Silu).then_inc(S("gate0"), 1)

            def feed_out(name, u, last, epilogue):
                b = base[name]

                def one(i, blk, buf, more=True):
                    def side(k):
                        if k == SLOTS - 1:
                            if more:
                                act.wait_ge(split_used, blk * CPB)
                                stage(u, i + 1, 1 - buf)
                            else:
                                epilogue(0)
                    ahead(blk, side, more or not last)

                def second_stage(k):
                    if k == SLOTS - 1:
                        act.wait_ge(S(f"hidden{u}"), FBLK + 1)
                        stage(u, 1, 1)

                ahead(b, second_stage)
                with act.Fori(0, (FBLK - 3) // 2) as i:
                    one(2 * i + 1, b + 2 * i + 1, 1)
                    one(2 * i + 2, b + 2 * i + 2, 0)
                one(FBLK - 2, b + FBLK - 2, 1)
                one(FBLK - 1, b + FBLK - 1, 0, False)
                epilogue(1)

            def fo_squares(half):
                for q in (2 * half, 2 * half + 1):
                    squares(4, resid_cols, q, 512, q + 1)

            feed_in("ff", silu_gate, GAIN["ffn"], 3, 0)
            feed_out("fo", 0, False, fo_squares)
            root(4)

            pairs("gqk", 2, lambda blk, par, i: low_sums(blk, par), first_side=turn_ahead(4, GAIN["pre2"]))
            pairs("dqk", 4, lambda blk, par, i: low_sums(blk, par))
            blk = base["al"]
            ahead(blk)
            block_done(blk)
            act.wait_ge(acc_freed, blk + 1)
            act.activation(lo_sum[0:16, 0:SEQ], ps[0:16, 0, SEQ:], ACT.Copy).then_inc(lo_copied, 1)

            z_abs = free_c[:, 0:1024]

            def low_rank(k):
                if k == 0:
                    act.wait_ge(S("g_z"), 1)
                    own(act.activation(z_abs.rearrange("p (t n) -> p t n", t=NT), ps[:, 6:8, :], ACT.Abs))
                if k == 1:
                    own(act.activation(z_abs, z_abs, ACT.Exp, scale=-1.0))
                if k == 2:
                    act.activation(z_abs, z_abs, ACT.Ln, bias=unit).then_inc(S("g_ln"), 1)

            for n in range(2):
                ahead(base["gv"] + n, low_rank if n else nothing)
                keep_rows(gv)(base["gv"] + n, 1 - n, n)

            decays = free_c[:, 0:9 * P]
            junk_g = rows_d[:, :, 1024:1024 + SEQ]

            def linear_attention(k, h):
                if k in (0, 3):
                    act.wait_ge(S("g_sum"), 2 * h + k // 3 + 1)
                    act.activation(decays[:, 0:LW].rearrange("p (n c) -> p n c", n=2), ps[:, 4:6, :], ACT.Exp, scale=1.0 / 16)
                    act.activation(decays[:, LW:], ps[:, 6, 0:P], ACT.Exp, scale=1.0 / 16).then_inc(S("g_exp"), 1)

            def norm_heads(done, u, eps_name, ps_rows, junk):
                act.wait_ge(done[0], done[1])
                for t in range(NT):
                    ins = act.activation(junk[:, t, :], ps_rows[:, t * SEQ:t * SEQ + SEQ], ACT.Square,
                                         accum_out=osum[:, t:t + 1])
                own(ins)
                act.activation(osum, osum, ACT.Sqrt, bias=eps[eps_name]).then_inc(S(u), 1)

            def norm_gla(h):
                norm_heads((S("g_o"), h + 1), "g_sq", "gla", ps[:, 7, :], junk_g)

            for section, rows in (("gg", gate_rows(rows_d, ACT.Silu)), ("dv", keep_rows(dv))):
                for n in range(2):
                    h = n + (2 if section == "dv" else 0)
                    def side(k):
                        if k >= 0:
                            linear_attention(k, h)
                        if k == 1 and h:
                            norm_gla(h - 1)
                    ahead(base[section] + n, side)
                    rows(base[section] + n, 1 - n, n)

            dT, s_both = temp[:, 1024:1536], area_g[:, 0:1024]
            junk_t = temp[:, 1536:2048].rearrange("p (t n) -> p t n", t=NT)

            def diff_attention(pos):
                for j, bank in (((0, 6), (1, 4), (2, 5)) if pos == -1 else ((3, 7),) if pos == 3 else ()):
                    turn_group(5, j, bank, hT)
                if pos == 0:
                    norm_gla(G_HEADS - 1)
                h, step = divmod(pos - 2, 4)
                if step == 0 and 0 <= h < D_HEADS:
                    act.wait_ge(S("d_top"), h + 1)
                    for n in range(4):
                        ins = act.activation(s_both[:, n * SEQ:n * SEQ + SEQ], s_both[:, n * SEQ:n * SEQ + SEQ], ACT.Exp,
                                             bias=negtop4[:, n:n + 1], scale=A_SCALE, accum_out=total4[:, n:n + 1])
                    ins.then_inc(S("d_exp"), 1)
                h, step = divmod(pos - 4, 4)
                if step == 0 and 0 <= h < D_HEADS:
                    act.wait_ge(S("d_turn"), h + 1)
                    act.activation(dT[:, 0:SEQ], ps[:, 6, 0:SEQ], ACT.Copy)
                    act.activation(dT[:, SEQ + P:], ps[:, 6, SEQ + P:], ACT.Copy).then_inc(S("d_pT"), 1)
                if step == 1 and 0 <= h < D_HEADS:
                    norm_heads((S("d_o"), h + 1), "d_sq", "diff", ps[:, 7, :], junk_t)
                h, step = divmod(pos - 8, 4)
                if step == 0 and 0 <= h < D_HEADS:
                    turn_group(5, 4 + h, 4, hT)

            def m_cols(t, q):
                return rows_m[:, t, q * CHUNK:(q + 1) * CHUNK]

            for n in range(4):
                def side(k):
                    if k >= 0 or n == 0:
                        diff_attention(8 * n + k)
                    if n == 3 and k == 1:
                        squares(7, m_cols, 0, CHUNK, 1)
                ahead(base["o2"] + n, side)
                if n < 2:
                    block_done(base["o2"] + n)
                    for hc in range(2):
                        act.activation(rows_m[:, 0, n * CHUNK + hc * 512:n * CHUNK + hc * 512 + 512], ps[:, 2 * hc, :], ACT.Copy)\
                            .then_inc(S("m_kept0"), 1)
            squares(7, m_cols, 1, CHUNK, 2)
            root(7)
            for q in range(4):
                squares(6, resid_cols, q, 512, q + 1)
            root(6)

            def gelu_gate(k, i):
                if k in (4, 5):
                    if k == 4:
                        act.wait_ge(S("conv_done"), i + 1)
                        act.wait_ge(S("hidden1"), i + 1)
                    for f in (2 * k - 8, 2 * k - 7):
                        ins = act.activation(up_t[:, f * SEQ:f * SEQ + SEQ], gate_t[:, f * SEQ:f * SEQ + SEQ],
                                             ACT.Gelu_apprx_tanh, bias=conv[:, bass.ds(3 * FT + 4 * i + f, 1)])
                    if k == 5:
                        ins.then_inc(S("gate1"), 1)

            def last_squares(half):
                act.wait_ge(split_used, (base["fo2"] + FBLK) * CPB - 4 + 4 * half)
                for q in (2 * half, 2 * half + 1):
                    for t in range(NT):
                        ins = act.activation(rows_d[:, t, q * 512:q * 512 + 512], ps[:, 2 * q + t, :], ACT.Square,
                                             accum_out=parts[:, 4 * t + q:4 * t + q + 1])
                    ins.then_inc(S("norm_part8"), 1)

            feed_in("ff2", gelu_gate, GAIN["ffn2"], 6, 1)
            feed_out("fo2", 1, True, last_squares)
            root(8)

        @block.vector
        def _(dve):
            own = Chain(dve, S("dve_own"))

            def nothing(k):
                pass

            def split(blk, c):
                dve.wait_ge(hi_ready, blk * CPB + c + 1)
                dve.tensor_tensor(wlo[:, c % SLOTS, :], raw[:, c % SLOTS, :], whi[:, c % SLOTS, :].bitcast(F32),
                                  ALU.subtract).then_inc(lo_ready, 1)

            def ahead(blk, side=nothing, more=True):
                side(-1)
                for k in range(CPB):
                    if k < SLOTS:
                        split(blk, k + SLOTS)
                    elif more:
                        split(blk + 1, k - SLOTS)
                    side(k)

            def block_done(blk):
                dve.wait_ge(split_used, (blk + 1) * CPB)

            def pairs(name, n, epilogue, side=None, first_side=None, per=0):
                b, start = base[name], 0
                if first_side is not None:
                    for par in range(2):
                        ahead(b + par, nothing if par else first_side)
                        epilogue(b + par, par, par)
                    start = 1
                if start < n // 2:
                    with dve.Fori(start, n // 2) as i:
                        own.begin(i - start, 2 * per)
                        for par in range(2):
                            ahead(b + 2 * i + par, (lambda k: side(k, 2 * i + par)) if side else nothing)
                            epilogue(b + 2 * i + par, par, 2 * i + par)
                    own.end(n // 2 - start)

            def add_low(blk, par, nth, dst):
                dve.wait_ge(lo_copied, nth + 1)
                return dve.tensor_tensor(dst, ps[:, 4 * par:4 * par + 4, 0:SEQ], lo_sum.rearrange("p (f t) -> p f t", f=4), ALU.add)

            def turn_group(u, j, bank, dst, col0=None):
                dve.wait_ge(S(f"turn_hi{u}"), j + 1)
                src = ps[:, bank, :].rearrange("p (k t) -> p k t", k=2)
                if col0 is None:
                    ins = dve.tensor_tensor(dst[:, 2 * j:2 * j + 2, 1, :], src, dst[:, 2 * j:2 * j + 2, 0, :].bitcast(F32), ALU.subtract)
                else:
                    for k2 in range(2):
                        kt = 2 * j + k2
                        ins = dve.scalar_tensor_tensor(dst[:, kt, 1, :], src[:, k2, :], gains[:, col0 + kt:col0 + kt + 1],
                                                       dst[:, kt, 0, :].bitcast(F32), ALU.mult, ALU.subtract)
                ins.then_inc(S(f"turned{u}"), 1)

            def turn_ahead(u, col0):
                def side(k):
                    for j in ((0, 1, 2) if k < 0 else (k + 3,)):
                        if j < KT // 2:
                            turn_group(u, j, 4 + j % 4, hT, col0)
                return side

            def row_scale(u, n=4):
                if u:
                    dve.wait_ge(S(f"norm_part{u}"), n)
                    dve.tensor_reduce(sumsq, parts.rearrange("p (t q) -> p t q", q=4)[:, :, 0:n], AX.X, ALU.add)\
                        .then_inc(S(f"norm_sum{u}"), 1)
                dve.wait_ge(S(f"norm_sq{u}"), 1)
                own(dve.reciprocal(rstd, sumsq))

            def norm_rows(u, dst):
                row_scale(u)
                for q in range(4):
                    cs = slice(q * 512, q * 512 + 512)
                    for t in range(NT):
                        ins = dve.tensor_scalar(dst[:, t, cs], resid[:, t, cs], rstd[:, t:t + 1], DM ** 0.5, ALU.mult, ALU.mult)
                    ins.then_inc(S(f"rows{u}"), 1)

            dve.sem_inc(acc_freed, 1)
            for n, width in (("head", P), ("model", DM), ("one", 1), ("diff", SEQ), ("gla", SEQ / A_SCALE ** 2)):
                dve.memset(eps[n], EPS * width)
            dve.memset(unit, 1.0).then_inc(S("eps_ok"), 1)
            for h in range(A_HEADS):
                dve.memset(slopes1[:, h:h + 1], -(2.0 ** -(h + 1)) / A_SCALE)
            for h in range(D_HEADS):
                ins = dve.memset(slopes2[:, h:h + 1], -(2.0 ** (-8.0 * (h + 1) / D_HEADS)) / A_SCALE)
            own(ins)
            dve.wait_ge(S("gain_t"), 1)
            own(dve.tensor_copy(gains[:, :], ps[:, 0, 0:GAIN_ROWS]))
            g_qk = gains[:, GAIN["q"]:GAIN["k"] + 1]
            dve.tensor_scalar(g_qk, g_qk, P ** 0.5, None, ALU.mult).then_inc(S("gain_ok"), 1)
            for c in range(SLOTS):
                split(0, c)
            norm_rows(0, resid)

            def keep_tiles(dst, nth0):
                def epilogue(blk, par, i):
                    add_low(blk, par, nth0 + i, dst[:, bass.ds(4 * i, 4), :]).then_inc(acc_freed, 1)
                return epilogue

            def no_epilogue(blk, par, i):
                pass

            s1, on = temp[:, 0:512], temp[:, 1536:1792]

            pairs("qk", 4, keep_tiles(tiles_a, 0), first_side=turn_ahead(0, GAIN["mix"]))
            pairs("qkr", 4, keep_tiles(tiles_b, 4))
            n_cols = 8

            def head_tiles(h):
                return [tiles_a[:, bass.ds(A_HEADS * n + h, 1), :] for n in range(2)]

            def head_squares(h):
                for n, x in enumerate(head_tiles(h)):
                    ins = dve.tensor_tensor(head_sq[:, n * SEQ:n * SEQ + SEQ].rearrange("p (n t) -> p n t", n=1), x, x, ALU.mult)
                ins.then_inc(S("a_sq"), 1)

            def head_scale(h):
                dve.wait_ge(S("a_root"), h + 1)
                own(dve.reciprocal(head_root, head_root))
                for n, x in enumerate(head_tiles(h)):
                    root = head_root[:, n * SEQ:n * SEQ + SEQ].rearrange("p (n t) -> p n t", n=1)
                    ins = dve.scalar_tensor_tensor(x, x, gains[:, GAIN["q"] + n:GAIN["q"] + n + 1], root, ALU.mult, ALU.mult)
                ins.then_inc(S("a_qn"), 1)

            def head_norms(pos):
                if pos % 4 == 0:
                    head_squares(pos // 4)
                if pos % 4 == 2:
                    head_scale(pos // 4)
                if pos == 2:
                    dve.wait_ge(S("conv_t"), 1)
                    own(dve.tensor_copy(conv[:, :].rearrange("p (n f) -> p n f", n=2), ps[:, 5:7, 0:half_conv]))

            for n in range(2):
                lq, lk = GAIN["lq1"] + 2 * n, GAIN["lk1"] + 2 * n
                ins = dve.tensor_tensor(lamprod[:, n:n + 1], gains[:, lq:lq + 1], gains[:, lk:lk + 1], ALU.mult)
            ins.then_inc(S("lam_prod"), 1)
            dve.wait_ge(acc_freed, base["va"] + 1)
            for n in range(2):
                ahead(base["va"] + n, lambda k: head_norms(8 * n + k) if k >= 0 else None)
            dve.wait_ge(S("lam_exp"), 1)
            own(dve.tensor_tensor(neglam, lam[:, 1:2], lam[:, 0:1], ALU.subtract))
            own(dve.tensor_scalar(neglam, neglam, -LAMBDA_INIT, None, ALU.add))

            def attention(k, h):
                if k == 0:
                    dve.wait_ge(S("a_score"), h + 1)
                    own(dve.scalar_tensor_tensor(s1, dist, slopes1[:, bass.ds(h, 1)], ps[:, 5, :], ALU.mult, ALU.add))
                    own(dve.tensor_reduce(top, s1.rearrange("p (t k) -> p t k", t=NT), AX.X, ALU.max))
                    dve.tensor_scalar(negtop, top, -A_SCALE, None, ALU.mult).then_inc(S("a_top"), 1)
                if k == 3:
                    dve.wait_ge(S("a_exp"), h + 1)
                    own(dve.reciprocal(recip, total))
                    dve.wait_ge(S("a_o"), h + 1)
                    for t in range(NT):
                        ins = dve.tensor_scalar(on[:, t * P:t * P + P], ps[:, 7, t * P:t * P + P], recip[:, t:t + 1], None, ALU.mult)
                    ins.then_inc(S("a_on"), 1)
                if k == 4:
                    dve.wait_ge(S("a_hi"), h + 1)
                    dve.tensor_tensor(oaT[:, bass.ds(h, 1), 1, :], ps[:, 4, 0:SEQ], oaT[:, bass.ds(h, 1), 0, :].bitcast(F32),
                                      ALU.subtract).then_inc(S("a_done"), 1)

            def attention_and_norm(k, h):
                attention(k, h)
                if k == 4:
                    head_squares(h + HOSTED)
                if k == 6:
                    head_scale(h + HOSTED)

            pairs("vr", 4, no_epilogue, side=attention_and_norm, per=4)
            pairs("ga", 4, no_epilogue, side=lambda k, i: attention(k, 4 + i), per=3)

            aT = temp[:, 512:1024]

            def retention(k, h):
                if k == 0:
                    dve.wait_ge(S("r_score"), h + 1)
                    dve.tensor_tensor(aT, ps[:, 4, :], decay[:, bass.ds(h * 512, 512)], ALU.mult).then_inc(S("r_a"), 1)
                if k == 3:
                    dve.wait_ge(S("r_o"), h + 1)
                    for t in range(NT):
                        ins = dve.bn_stats(bn[:, 6 * t:6 * t + 6], ps[:, 6 + t, :])
                    own(ins)
                    dve.memset(spare, 0.0)
                    for t in range(NT):
                        ins = dve.bn_aggr(mv[:, 2 * t:2 * t + 2], bn[:, 6 * t:6 * t + 6])
                    ins.then_inc(S("r_var"), 1)
                if k == 4:
                    dve.wait_ge(S("r_root"), h + 1)
                    own(dve.reciprocal(rstd, rstd))
                    for t in range(NT):
                        ins = dve.tensor_scalar(resid[:, t, bass.ds(h * 512, 512)], ps[:, 6 + t, :], mv[:, 2 * t:2 * t + 1],
                                                rstd[:, t:t + 1], ALU.subtract, ALU.mult)
                    ins.then_inc(S("r_done"), 1)

            pairs("gb", 4, no_epilogue, side=retention, per=2)

            def times_silu(blk, par, i):
                dve.wait_ge(S("silu"), i + 1)
                o = resid[:, :, bass.ds(i * 512, 512)]
                dve.tensor_tensor(o, o, ps[:, 2 * par:2 * par + 2, :], ALU.mult).then_inc(acc_freed, 1)

            dve.wait_ge(S("r_done"), R_HEADS)
            pairs("gr", 4, times_silu)
            dve.wait_ge(acc_freed, base["oa"] + 1)
            dve.sem_inc(S("rows1"), 1)

            def turn_ret(k):
                if 1 <= k <= 4:
                    for j in (2 * k - 2, 2 * k - 1):
                        turn_group(1, j, 4 + j % 4, hT)

            for j in range(2):
                blk = base["oa"] + j
                ahead(blk, nothing if j else turn_ret)
                block_done(blk)
                for t in range(NT):
                    m = rows_d[:, t, j * CHUNK:(j + 1) * CHUNK].rearrange("p (f n) -> p f n", f=2)
                    acc = ps[:, 4 * j:4 * j + 4, :].rearrange("p (f t) n -> p f t n", t=NT)[:, :, t, :]
                    ins = dve.tensor_tensor(m, m, acc, ALU.mult)
                ins.then_inc(acc_freed, 1)

            dve.wait_ge(acc_freed, base["or"] + 1)
            for n in range(4):
                def turn_merged(k):
                    if n in (1, 2) and k in (1, 2):
                        j = 2 * (n - 1) + k - 1
                        turn_group(2, j, 4 + j % 4, oaT)
                blk, par = base["or"] + n, n % 2
                ahead(blk, turn_merged)
                block_done(blk)
                cs = slice(n * 512, n * 512 + 512)
                own(dve.tensor_tensor(rows_a[:, :, cs], rows_a[:, :, cs], ps[:, 2 * par:2 * par + 2, :], ALU.mult))
                own(dve.tensor_tensor(rows_d[:, :, cs], rows_d[:, :, cs], rows_a[:, :, cs], ALU.add))
                dve.sem_inc(acc_freed, 1)
                dve.sem_inc(S("rows2"), 1)

            def turn_rest(k):
                if k in (0, 1):
                    for j in (2 * k + 4, 2 * k + 5):
                        turn_group(2, j, 4 + j % 4, hT)

            for n in range(4):
                blk, par = base["out"] + n, n % 2
                ahead(blk, nothing if n else turn_rest)
                block_done(blk)
                dve.wait_ge(S("x_again"), 16)
                r = resid[:, :, n * 512:n * 512 + 512]
                own(dve.tensor_tensor(r, r, ps[:, 2 * par:2 * par + 2, :], ALU.add))
                dve.sem_inc(acc_freed, 1)
                dve.sem_inc(S("norm_in3"), 1)
            norm_rows(3, rows_d)

            gate4 = gate_t.rearrange("p (f t) -> p f t", f=4)
            prod_t = area_d[:, 3072:4096].rearrange("p (f t) -> p f t", f=4)

            def stage(u, i, buf):
                dve.wait_ge(S(f"stage_hi{u}"), i + 1)
                dve.tensor_tensor(staged[:, buf, :, 1, :], hidden[:, bass.ds(4 * i, 4), :],
                                  staged[:, buf, :, 0, :].bitcast(F32), ALU.subtract).then_inc(S(f"staged{u}"), 1)

            def feed_in(name, u, col0, turned, gate_sum, per, side2, n_cols):
                b = base[name]

                def pair(i, side):
                    ahead(b + 2 * i, side)
                    gate_sum(b + 2 * i, i, n_cols + 2 * i)
                    ahead(b + 2 * i + 1, lambda k: side2(k, i))
                    dve.wait_ge(S(f"hidden{u}"), i + 1)
                    add_low(b + 2 * i + 1, 1, n_cols + 2 * i + 1, prod_t).then_inc(acc_freed, 1)

                pair(0, turn_ahead(turned, col0))
                pair(1, lambda k: stage(u, 0, 0) if k == 4 else None)
                with dve.Fori(2, FBLK) as i:
                    own.begin(i - 2, per)
                    pair(i, nothing)
                own.end(FBLK - 2)

            def silu_sum(blk, i, nth):
                dve.wait_ge(S("gate0"), i + 1)
                own(add_low(blk, 0, nth, gate4))
                dve.sem_inc(acc_freed, 1)
                dve.sem_inc(S("gate_sum"), 1)

            feed_in("ff", 0, GAIN["ffn"], 3, silu_sum, 1, lambda k, i: None, n_cols)
            n_cols += 2 * FBLK

            def feed_out(name, u, last, epilogue):
                b = base[name]

                def one(i, blk, buf, more=True):
                    def side(k):
                        if k == SLOTS - 1:
                            if more:
                                stage(u, i + 1, 1 - buf)
                            else:
                                epilogue(0)
                    ahead(blk, side, more or not last)

                one(0, b, 0)
                with dve.Fori(0, (FBLK - 3) // 2) as i:
                    one(2 * i + 1, b + 2 * i + 1, 1)
                    one(2 * i + 2, b + 2 * i + 2, 0)
                one(FBLK - 2, b + FBLK - 2, 1)
                one(FBLK - 1, b + FBLK - 1, 0, False)
                epilogue(1)

            def add_resid(half):
                dve.wait_ge(split_used, (base["fo"] + FBLK) * CPB - 4 + 4 * half)
                for q in (2 * half, 2 * half + 1):
                    for t in range(NT):
                        r = resid[:, t, q * 512:q * 512 + 512]
                        ins = dve.tensor_tensor(r, r, ps[:, 2 * q + t, :], ALU.add)
                    own(ins)
                    dve.sem_inc(S("norm_in4"), 1)

            feed_out("fo", 0, False, add_resid)
            dve.sem_inc(acc_freed, FBLK)
            norm_rows(4, rows_d)

            pairs("gqk", 2, keep_tiles(tiles_b, n_cols), first_side=turn_ahead(4, GAIN["pre2"]))
            pairs("dqk", 4, keep_tiles(tiles_a, n_cols + 2))
            n_cols += 6
            ahead(base["al"])
            dve.wait_ge(lo_copied, n_cols + 1)
            own(dve.tensor_tensor(temp[0:16, 0:SEQ], ps[0:16, 0, 0:SEQ], lo_sum[0:16, 0:SEQ], ALU.add))
            dve.sem_inc(acc_freed, 1)
            dve.sem_inc(S("g_ga"), 1)
            n_cols += 1
            log_a = temp[:, 1024:2048]

            def low_rank(k):
                if k == 3:
                    dve.wait_ge(S("g_ln"), 1)
                    dve.scalar_tensor_tensor(log_a.rearrange("p (t n) -> p t n", t=NT), ps[:, 6:8, :], 0.0,
                                             free_c[:, 0:1024].rearrange("p (t n) -> p t n", t=NT),
                                             ALU.min, ALU.subtract).then_inc(S("g_log"), 1)

            for n in range(2):
                ahead(base["gv"] + n, low_rank if n else nothing)

            decays = free_c[:, 0:9 * P]
            qe = area_g[:, LW:2 * LW]
            sT, cross = temp[:, 0:512], temp[:, 512:768]
            lev = decays[:, 0:LW].rearrange("p (n c) -> p n c", c=P)
            gain_g, gain_d = free_c[:, 1280:1536], free_c[:, 1536:1792]
            head_rows = free_c[:, 1792:2048]
            dve.wait_ge(S("second_in"), 16)
            dve.wait_ge(S("norms_in"), 32)
            for n in (gain_g, gain_d):
                dve.tensor_scalar(n, n, SEQ ** 0.5 * (1.0 - LAMBDA_INIT if n is gain_d else 1.0), None, ALU.mult)
            own(dve.memset(sT, 0.0))

            def linear_attention(k, h):
                if k in (0, 3):
                    t = k // 3
                    dve.wait_ge(S("g_exp"), 2 * h + t + 1)
                    key = tiles_b[:, bass.ds(4 + h, 1), t * P:t * P + P]
                    q = tiles_b[:, bass.ds(h, 1), t * P:t * P + P]
                    dve.tensor_tensor(qe.rearrange("p (n c) -> p n c", c=P), lev, q.to_broadcast([P, LEVELS, P]), ALU.mult)
                    ins = dve.tensor_tensor(cross[:, t * P:t * P + P].rearrange("p (n c) -> p n c", n=1),
                                            decays[:, LW:].rearrange("p (n c) -> p n c", n=1), (key, q)[t], ALU.mult)
                    ins.then_inc(S("g_q"), 1)
                if k in (2, 5):
                    t = k // 3
                    dve.wait_ge(S("g_score"), 2 * h + t + 1)
                    own(dve.tensor_tensor(decays[:, 0:LW].rearrange("p (n c) -> p n c", n=2), ps[:, 4:6, :],
                                          masks_m.rearrange("p (n c) -> p n c", n=2), ALU.mult))
                    ins = dve.tensor_reduce(sT[:, t * SEQ + t * P:t * SEQ + t * P + P],
                                            decays[:, 0:LW].rearrange("p (n c) -> p c n", c=P), AX.X, ALU.add)
                    ins.then_inc(S("g_sT"), 1)
                    if t == 1:
                        dve.wait_ge(S("g_cross"), h + 1)
                        dve.tensor_copy(sT[:, P:SEQ], ps[:, 6, P:2 * P]).then_inc(S("g_sT"), 1)

            def head_out(h):
                dve.wait_ge(S("g_sq"), h + 1)
                own(dve.reciprocal(orstd, osum))
                for t in range(NT):
                    own(dve.scalar_tensor_tensor(head_rows, ps[:, 7, t * SEQ:t * SEQ + SEQ], orstd[:, t:t + 1], gain_g,
                                                 ALU.mult, ALU.mult))
                    o = rows_d[:, t, h * SEQ:(h + 1) * SEQ]
                    own(dve.tensor_tensor(o, o, head_rows, ALU.mult))
                dve.sem_inc(S("rows5"), 1)

            for h in range(G_HEADS):
                blk = base["gg"] + h

                def side(k):
                    if k >= 0:
                        linear_attention(k, h)
                    if k == 1 and h:
                        head_out(h - 1)
                ahead(blk, side)

            diff, s_both = temp[:, 0:512], area_g[:, 0:1024]

            def diff_attention(pos):
                for j, bank in (((0, 6), (1, 4), (2, 5)) if pos == -1 else ((3, 7),) if pos == 3 else ()):
                    turn_group(5, j, bank, hT)
                if pos == 0:
                    head_out(G_HEADS - 1)
                h, step = divmod(pos - 1, 4)
                if step == 0 and 0 <= h < D_HEADS:
                    dve.wait_ge(S("d_score"), h + 1)
                    for c in range(2):
                        ins = dve.scalar_tensor_tensor(s_both[:, c * 512:c * 512 + 512], dist, slopes2[:, h:h + 1], ps[:, 4 + c, :],
                                                       ALU.mult, ALU.add)
                    own(ins)
                    own(dve.tensor_reduce(top4, s_both.rearrange("p (n k) -> p n k", n=4), AX.X, ALU.max))
                    dve.tensor_scalar(negtop4, top4, -A_SCALE, None, ALU.mult).then_inc(S("d_top"), 1)
                if step == 1 and 0 <= h < D_HEADS:
                    dve.wait_ge(S("d_exp"), h + 1)
                    own(dve.reciprocal(recip4, total4))
                    own(dve.tensor_scalar(recip4[:, 2:4], recip4[:, 2:4], neglam, None, ALU.mult))
                    for t in range(NT):
                        ins = dve.tensor_scalar(diff[:, t * SEQ:t * SEQ + SEQ], s_both[:, t * SEQ:t * SEQ + SEQ],
                                                recip4[:, t:t + 1], None, ALU.mult)
                    own(ins)
                    for t in range(NT):
                        ins = dve.scalar_tensor_tensor(diff[:, t * SEQ:t * SEQ + SEQ], s_both[:, 512 + t * SEQ:512 + t * SEQ + SEQ],
                                                       recip4[:, 2 + t:3 + t], diff[:, t * SEQ:t * SEQ + SEQ], ALU.mult, ALU.add)
                    ins.then_inc(S("d_p"), 1)
                h, step = divmod(pos - 6, 4)
                if step == 0 and 0 <= h < D_HEADS:
                    dve.wait_ge(S("d_sq"), h + 1)
                    own(dve.reciprocal(orstd, osum))
                    for t in range(NT):
                        ins = dve.scalar_tensor_tensor(rows_d[:, t, 1024 + h * SEQ:1024 + (h + 1) * SEQ],
                                                       ps[:, 7, t * SEQ:t * SEQ + SEQ], orstd[:, t:t + 1], gain_d, ALU.mult, ALU.mult)
                    ins.then_inc(S("rows5"), 1)
                if step == 2 and 0 <= h < D_HEADS:
                    turn_group(5, 4 + h, 4, hT)

            for n in range(4):
                blk, bank, j = base["o2"] + n, 4 if n == 3 else 0, n % 2
                ahead(blk, lambda k: diff_attention(8 * n + k) if k >= 0 or n == 0 else None)
                block_done(blk)
                for hc in range(2):
                    cs = slice(j * CHUNK + hc * 512, j * CHUNK + hc * 512 + 512)
                    if n >= 2:
                        m = rows_m[:, :, cs]
                        ins = dve.tensor_tensor(m, m, ps[:, bank + 2 * hc:bank + 2 * hc + 2, :], ALU.add)
                    else:
                        dve.tensor_copy(rows_m[:, 1, cs], ps[:, bank + 2 * hc + 1, :]).then_inc(S("m_kept1"), 1)
                if n < 2:
                    dve.wait_ge(S("m_kept0"), 2 * n + 2)
                else:
                    own(ins)
                    dve.sem_inc(S("norm_in7"), 1)
                dve.sem_inc(acc_freed, 1)

            def scale_rows():
                own(dve.tensor_scalar(rstd, rstd, DM ** 0.5, None, ALU.mult))

            row_scale(7, 2)
            scale_rows()
            dve.wait_ge(S("post_in"), 16)
            for q in range(4):
                cs = slice(q * 512, q * 512 + 512)
                for t in range(NT):
                    ins = dve.scalar_tensor_tensor(rows_m[:, t, cs], rows_m[:, t, cs], rstd[:, t:t + 1], area_g[:, cs], ALU.mult, ALU.mult)
                own(ins)
                own(dve.tensor_tensor(resid[:, :, cs], resid[:, :, cs], rows_m[:, :, cs], ALU.add))
                dve.sem_inc(S("norm_in6"), 1)
            own(dve.memset(conv_in, 0.0))
            norm_rows(6, rows_d)

            def conv_sum(blk, i, nth):
                own(add_low(blk, 0, nth, conv_in[:, :, 2:]))
                dve.sem_inc(acc_freed, 1)

            def convolve(tap, i):
                if not 0 <= tap < 3:
                    return
                if tap == 0:
                    dve.wait_ge(S("gate1"), i + 1)
                for f in range(4):
                    src = conv_in[:, f, tap:tap + SEQ]
                    w = conv[:, bass.ds(tap * FT + 4 * i + f, 1)]
                    dst = gate_t[:, f * SEQ:f * SEQ + SEQ]
                    if tap == 0:
                        ins = dve.tensor_scalar(dst, src, w, None, ALU.mult)
                    else:
                        ins = dve.scalar_tensor_tensor(dst, src, w, dst, ALU.mult, ALU.add)
                if tap < 2:
                    own(ins)
                else:
                    ins.then_inc(S("conv_done"), 1)

            def no_adds(half):
                pass

            feed_in("ff2", 1, GAIN["ffn2"], 6, conv_sum, 3, convolve, n_cols)
            feed_out("fo2", 1, True, no_adds)
            row_scale(8)
            scale_rows()
            dve.wait_ge(S("post_in2"), 16)
            for q in range(4):
                cs = slice(q * 512, q * 512 + 512)
                for t in range(NT):
                    ins = dve.scalar_tensor_tensor(rows_a[:, t, cs], ps[:, 2 * q + t, :], rstd[:, t:t + 1], area_g[:, cs], ALU.mult, ALU.mult)
                own(ins)
                dve.tensor_tensor(resid[:, :, cs], resid[:, :, cs], rows_a[:, :, cs], ALU.add).then_inc(S("y_ready"), 1)

        @block.gpsimd
        def _(pool):
            pool.sem_inc(S("hidden0"), 1)
            pool.sem_inc(S("hidden1"), 1)
            for n, name in enumerate(("lambda_q1_2", "lambda_k1_2", "lambda_q2_2", "lambda_k2_2")):
                pool.dma_start(g_rows[66 + n:67 + n, 0, :], a[name]).then_inc(S("lambdas_in"), 16)
            taps = a["conv_w_2"].rearrange("l w (f d) -> (l w f) d", d=P)
            pool.dma_start(g_rows[0:half_conv, 1, :], taps[0:half_conv, :]).then_inc(S("conv_in"), 16)
            pool.dma_start(g_rows[0:half_conv // 2, 2, :], taps[half_conv:, :]).then_inc(S("conv_in"), 16)
            pool.dma_start(g_rows[half_conv // 2:half_conv, 2, :], a["conv_b_2"].rearrange("l (f d) -> (l f) d", d=P))\
                .then_inc(S("conv_in"), 16)
            pool.dma_start(masks[:, 0:R_HEADS * NT * SEQ], c_decay).then_inc(S("decay_in"), 16)

            q_st = temp[:, 512:768].rearrange("p (n t) -> p n t", n=1)
            pool.wait_ge(S("a_qn"), 1)
            pool.tensor_copy(q_st, tiles_a[:, 0:1, :]).then_inc(S("a_q"), 1)
            with pool.Fori(1, A_HEADS) as h:
                pool.wait_ge(S("a_qn"), h + 1)
                pool.wait_ge(S("a_score"), h)
                pool.tensor_copy(q_st, tiles_a[:, bass.ds(h, 1), :]).then_inc(S("a_q"), 1)

            kst = temp[:, 0:512].rearrange("p (d t) -> p d t", d=2)
            pool.wait_ge(S("a_done"), A_HEADS)
            pool.wait_ge(S("decay_in"), 16)
            pool.tensor_copy(kst, tiles_b[:, 8:10, :]).then_inc(S("r_k"), 1)
            with pool.Fori(1, R_HEADS) as h:
                pool.wait_ge(S("r_score"), h)
                pool.tensor_copy(kst, tiles_b[:, bass.ds(8 + 2 * h, 2), :]).then_inc(S("r_k"), 1)
            pool.wait_ge(S("r_done"), R_HEADS)
            pool.dma_start(masks[:, :], c_second).then_inc(S("second_in"), 16)
            pool.wait_ge(S("turned1"), KT // 2)
            pool.dma_start(resid[:, :, :], x_rows).then_inc(S("x_again"), 16)

            prod = area_d[:, 3072:4096].rearrange("p (f t) -> p f t", f=4)
            up4 = up_t.rearrange("p (f t) -> p f t", f=4)

            def hidden_of(u, name):
                with pool.Fori(0, FBLK) as i:
                    pool.wait_ge(S(f"gate{u}"), i + 2)
                    pool.wait_ge(acc_freed, base[name] + 2 * i + 3)
                    pool.tensor_tensor(hidden[:, bass.ds(4 * i, 4), :], up4, prod, ALU.mult).then_inc(S(f"hidden{u}"), 1)

            hidden_of(0, "ff")
            pool.dma_start(area_g[0:16, 0:512], a["w_alpha_up_2"].rearrange("l k n -> (l k) n")).then_inc(S("alpha_in"), 16)
            pool.dma_start(area_g[0:1, 512:1024], a["b_alpha_2"]).then_inc(S("alpha_in"), 16)
            pool.wait_ge(S("staged0"), FBLK)
            for n, name in enumerate(("gla_norm_2", "diff_norm_2")):
                pool.dma_start(free_c[:, 1280 + n * SEQ:1280 + (n + 1) * SEQ], a[name].to_broadcast([P, SEQ])).then_inc(S("norms_in"), 16)
            la = temp[:, 1024:2048].rearrange("p (t n) -> p t n", t=NT)
            lev = free_c[:, 0:LW].rearrange("p (n c) -> p n c", c=P)
            ke = area_g[:, 0:LW].rearrange("p (n c) -> p n c", c=P)
            pool.wait_ge(S("g_log"), 1)

            def linear_attention(h):
                pool.tensor_copy(temp[:, 768:1024].rearrange("p (t n) -> p t n", t=NT), la[:, :, bass.ds(h * P, P)])\
                    .then_inc(S("g_la"), 1)
                for t in range(NT):
                    pool.wait_ge(S("g_exp"), 2 * h + t + 1)
                    pool.tensor_tensor(ke, lev, tiles_b[:, bass.ds(4 + h, 1), t * P:t * P + P].to_broadcast([P, LEVELS, P]), ALU.mult)\
                        .then_inc(S("g_k"), 1)

            linear_attention(0)
            with pool.Fori(1, G_HEADS) as h:
                pool.wait_ge(S("g_sum"), 2 * h)
                linear_attention(h)
            pool.wait_ge(S("g_cross"), G_HEADS)
            q_d = temp[:, 512:1024].rearrange("p (n t) -> p n t", n=2)
            for h in range(D_HEADS):
                if h:
                    pool.wait_ge(S("d_score"), h)
                pool.tensor_copy(q_d, tiles_a[:, 2 * h:2 * h + 2, :]).then_inc(S("d_q"), 1)
            pool.wait_ge(S("d_p"), D_HEADS)
            pool.dma_start(area_g[:, :], a["attn_post_norm_2"].to_broadcast([P, DM])).then_inc(S("post_in"), 16)
            pool.wait_ge(S("norm_in6"), 4)
            pool.dma_start(area_g[:, :], a["ffn_post_norm_2"].to_broadcast([P, DM])).then_inc(S("post_in2"), 16)
            hidden_of(1, "ff2")


_INS = ["x", "w_in", "w_o_attn", "w_o_ret", "w_out", "q_norm", "k_norm", "norm_mix", "norm_ffn", "w_ffn_in", "w_ffn_out",
        "attn_pre_norm_2", "w_in_2", "w_alpha_up_2", "b_alpha_2", "gla_norm_2", "lambda_q1_2", "lambda_k1_2",
        "lambda_q2_2", "lambda_k2_2", "diff_norm_2", "w_o_2", "attn_post_norm_2", "ffn_pre_norm_2", "w_ffn_in_2",
        "conv_w_2", "conv_b_2", "w_ffn_out_2", "ffn_post_norm_2"]


def kernel(**inputs):
    import concourse.bacc as bacc
    from concourse.bass_utils import run_bass_kernel_spmd

    nc = bacc.Bacc("TRN2", target_bir_lowering=False, num_devices=1)
    arrays, aps = {}, {}
    for name in _INS:
        arrays[name] = np.ascontiguousarray(inputs[name])
        aps[name] = nc.dram_tensor(name, arrays[name].shape, F32, kind="ExternalInput").ap()
    consts = []
    for name, value in zip(("shape_first", "shape_decay", "shape_second"), shape_constants()):
        arrays[name] = np.ascontiguousarray(value)
        consts.append(nc.dram_tensor(name, value.shape, F32, kind="ExternalInput").ap())
    out = nc.dram_tensor("y", (1, SEQ, DM), F32, kind="ExternalOutput").ap()
    two_blocks(nc, aps, out, *consts)
    r = run_bass_kernel_spmd(nc, [arrays], core_ids=[0])
    return r.results[0]["y"]
```

```python
from contextlib import ExitStack

import numpy as np
import concourse.bass as bass
from concourse import mybir

F32 = mybir.dt.float32
F32R = mybir.dt.float32r
ALU = mybir.AluOpType
ACT = mybir.ActivationFunctionType
AX = mybir.AxisListType

P = 128
SEQ = 256
NT = SEQ // P
DM = 2048
KT = DM // P
EPS = 1e-6
CHUNK = 1024
CPB = 8
SLOTS = 4
FF = 5632
FT = FF // P
FBLK = FF // 512
A_HEADS = 8
LATE = (0, 3, 4, 6)
HOSTED = 4
R_HEADS = 4
G_HEADS = 4
D_HEADS = 4
A_SCALE = 128 ** -0.5
LAMBDA_INIT = 0.2
MASKED = 1e30
LEVELS = 8
LW = LEVELS * P

GAIN = {"mix": 0, "ffn": 16, "pre2": 32, "ffn2": 48, "q": 64, "k": 65, "lq1": 66, "lk1": 67, "lq2": 68, "lk2": 69}
GAIN_ROWS = 70
CONV_ROWS = 4 * FT


def shape_constants():
    i = np.arange(P)
    ident = np.eye(P)
    ones = np.ones((P, P))
    q = np.arange(SEQ).reshape(NT, P).T[:, :, None]
    rel = q - np.arange(SEQ)[None, None, :]
    dist = np.where(rel >= 0, rel, MASKED).reshape(P, NT * SEQ)
    log_g = np.log(1.0 - 2.0 ** (-5.0 - np.arange(R_HEADS)))
    j = np.arange(SEQ).reshape(NT, P).T[:, None, :, None]
    gap = np.arange(SEQ)[None, None, None, :] - j
    decay = np.where(gap >= 0, np.exp(log_g[None, :, None, None] * np.maximum(gap, 0)), 0.0) * 256 ** -0.5
    sums, masks = [], []
    for s in (64, 32, 16, 8, 4, 2, 1):
        t, u = i[None, :], i[:, None]
        right = (t // s) % 2 == 1
        seam = np.where(right, t // s * s, (t // s + 1) * s)
        sums.append(np.where(right, (u >= seam) & (u <= t), (u > t) & (u < seam)))
        masks.append((u // (2 * s) == t // (2 * s)) & ((u // s) % 2 == 0) & right)
    sums.append(np.zeros((P, P)))
    masks.append(np.eye(P))
    sums.append(i[:, None] > i[None, :])
    sums.append(i[:, None] <= i[None, :])
    first = np.concatenate([ident, ones, dist], 1)
    second = np.concatenate([m.astype(np.float64) for m in sums + masks], 1)
    return (first.astype(np.float32), decay.reshape(P, -1).astype(np.float32), second.astype(np.float32))


class Chain:

    def __init__(self, eng, sem):
        self.eng, self.sem, self.base, self.k, self.at = eng, sem, 0, 0, None

    def __call__(self, ins):
        self.k += 1
        ins.then_inc(self.sem, 1)
        value = self.base + self.k
        if self.at is not None:
            i, per = self.at
            value = i * per + value
        self.eng.wait_ge(self.sem, value)

    def straight(self):
        self.base, self.k, self.at = self.base + self.k, 0, None

    def begin(self, i, per):
        self.straight()
        self.at = (i, per)

    def end(self, n):
        assert self.k == self.at[1], (self.k, self.at)
        self.base, self.k, self.at = self.base + n * self.k, 0, None


def two_blocks(nc, a, out, c_first, c_decay, c_second):
    with ExitStack() as ctx:
        def sb(name, shape, dt=F32):
            return ctx.enter_context(nc.sbuf_tensor(name, shape, dt))

        sems = {}

        def S(name):
            if name not in sems:
                sems[name] = ctx.enter_context(nc.semaphore(name))
            return sems[name]

        raw = sb("raw", [P, SLOTS, CHUNK])
        whi = sb("whi", [P, SLOTS, CHUNK], F32R)
        wlo = sb("wlo", [P, SLOTS, CHUNK], F32R)
        hT = sb("hT", [P, KT, 2, SEQ], F32R)
        big = sb("big", [P, 48 * SEQ])
        area_d = sb("area_d", [P, NT * DM])
        split_e = sb("split_e", [P, 16, SEQ], F32R)
        resid = sb("resid", [P, NT, DM])
        area_g = sb("area_g", [P, 2048])
        temp = sb("temp", [P, 2048])
        first = sb("first", [P, 2 * P + NT * SEQ])
        masks = sb("masks", [P, 10 * P + LW])
        gains = sb("gains", [P, GAIN_ROWS])
        conv = sb("conv", [P, CONV_ROWS])
        small = sb("small", [P, 96])

        ident, ones = first[:, 0:P], first[:, P:2 * P]
        dist = first[:, 2 * P:]
        decay = masks[:, 0:R_HEADS * NT * SEQ]
        sums_m, masks_m = masks[:, 0:10 * P], masks[:, 10 * P:]

        area = [big[:, n * 16 * SEQ:(n + 1) * 16 * SEQ] for n in range(3)]
        tiles_a = area[0].rearrange("p (n t) -> p n t", t=SEQ)
        rows_a = area[0].rearrange("p (t n) -> p t n", t=NT)
        tiles_b = area[1].rearrange("p (n t) -> p n t", t=SEQ)
        gv = area[1][:, 2048:].rearrange("p (t n) -> p t n", t=NT)
        rows_m = area[1].rearrange("p (t n) -> p t n", t=NT)
        rows_c = area[2].rearrange("p (t n) -> p t n", t=NT)
        dv = area[2][:, 0:2048].rearrange("p (t n) -> p t n", t=NT)
        free_c = area[2][:, 2048:]
        hidden = big[:, 0:FT * SEQ].rearrange("p (n t) -> p n t", t=SEQ)
        rows_d = area_d[:, :].rearrange("p (t n) -> p t n", t=NT)
        va = area_g[:, :].rearrange("p (t n) -> p t n", t=NT)
        head_sq, head_root = area_d[:, 1024:1536], area_d[:, 1536:2048]
        lo_sum = area_d[:, 0:1024]
        gate_t = area_d[:, 1024:2048]
        up_t = area_d[:, 2048:3072]
        scale_row = big[:, FT * SEQ:(FT + 1) * SEQ]
        scale_diag = temp[:, 1536:1536 + SEQ]
        conv_in = temp[:, 0:4 * (2 + SEQ)].rearrange("p (f t) -> p f t", f=4)
        oaT = split_e[:, :, :].rearrange("p (h s) t -> p h s t", s=2)
        staged = split_e[:, :, :].rearrange("p (b k s) t -> p b k s t", b=2, s=2)

        ps = ctx.enter_context(nc.psum_tensor("ps", [P, 8, 512], F32))

        col = {}

        def keep(name, n):
            at = sum(w for _, w in col.values())
            col[name] = (at, n)
            return small[:, at:at + n]

        sumsq = keep("sumsq", 2)
        rstd = keep("rstd", 2)
        late = keep("late", 2)
        slopes1 = keep("slopes1", A_HEADS)
        slopes2 = keep("slopes2", D_HEADS)
        top = keep("top", 2)
        negtop = keep("negtop", 2)
        total = keep("total", 2)
        recip = keep("recip", 2)
        bn = keep("bn", 12)
        mv = keep("mv", 4)
        lam = keep("lam", 2)
        neglam = keep("neglam", 1)
        lamprod = keep("lamprod", 2)
        unit = keep("unit", 1)
        parts = keep("parts", 8)
        top4 = keep("top4", 4)
        negtop4 = keep("negtop4", 4)
        total4 = keep("total4", 4)
        recip4 = keep("recip4", 4)
        osum = keep("osum", 2)
        orstd = keep("orstd", 2)
        spare = keep("spare", 1)
        eps = {n: keep(f"eps_{n}", 1) for n in ("head", "model", "one", "gla", "diff")}

        order = [("qk", 4), ("qkr", 4), ("va", 2), ("vr", 4), ("ga", 4), ("gb", 4), ("gr", 4), ("oa", 2), ("or", 4),
                 ("out", 4), ("ff", 2 * FBLK), ("fo", FBLK),
                 ("gqk", 2), ("dqk", 4), ("al", 1), ("gv", 2), ("gg", 2), ("dv", 2), ("o2", 4),
                 ("ff2", 2 * FBLK), ("fo2", FBLK)]
        base, n_blocks = {}, 0
        for name, n in order:
            base[name] = n_blocks
            n_blocks += n

        loaded = [S(f"loaded{s}") for s in range(SLOTS)]
        hi_ready, lo_ready, split_used = S("hi_ready"), S("lo_ready"), S("split_used")
        acc_freed = S("acc_freed")
        lo_copied = S("lo_copied")

        def wcols(w):
            return a[w].rearrange("l (k p) n -> p (l k) n", p=P)

        x_rows = a["x"].rearrange("b (t p) n -> p (b t) n", p=P)
        half_conv = CONV_ROWS // 2
        g_rows = area_g[:, 0:3 * P].rearrange("p (n d) -> p n d", d=P)

        block = ctx.enter_context(nc.Block())

        @block.sync
        def _(sp):
            def chunk_in(blk, c, src):
                if not (isinstance(blk, int) and blk * CPB + c < SLOTS):
                    sp.wait_ge(lo_ready, blk * CPB + c - SLOTS + 1)
                dst = raw[:, c % SLOTS, :]
                if len(src.shape) == 3:
                    dst = dst.rearrange("p (k n) -> p k n", k=2)[:, :, 0:src.shape[2]]
                sp.dma_start(dst, src).then_inc(loaded[c % SLOTS], 16)

            def wide(blk, w, col0, n=512, cs=range(CPB)):
                for c in cs:
                    chunk_in(blk, c, wcols(w)[:, 2 * c:2 * c + 2, bass.ds(col0, n)])

            def run(name, n, w, col0):
                with sp.Fori(0, n) as i:
                    wide(base[name] + i, w, col0 + i * 512)

            def tall(blk, w, kt0, col0):
                for c in range(CPB):
                    chunk_in(blk, c, wcols(w)[:, kt0 + c, col0:col0 + CHUNK])

            def feed_in(name, w):
                with sp.Fori(0, FBLK) as i:
                    wide(base[name] + 2 * i, w, i * 512)
                    wide(base[name] + 2 * i + 1, w, FF + i * 512)

            def feed_out(name, w):
                with sp.Fori(0, FBLK) as i:
                    for c in range(CPB):
                        rows = a[w].rearrange("l k n -> (l k) n")[bass.ds(i * 512 + c % 4 * P, P), :]
                        chunk_in(base[name] + i, c, rows[:, c // 4 * CHUNK:(c // 4 + 1) * CHUNK])

            sp.dma_start(first[:, 0:2 * P], c_first[:, 0:2 * P]).then_inc(S("first_in"), 16)
            for t in range(NT):
                sp.dma_start(resid[:, t, :], x_rows[:, t, :]).then_inc(S("x_in"), 16)
            wide(0, "w_in", 0, cs=(0,))
            sp.wait_ge(S("gains_in"), 16 * 6)
            wide(0, "w_in", 0, cs=range(1, CPB))
            with sp.Fori(1, 4) as i:
                wide(i, "w_in", i * 512)
            run("qkr", 4, "w_in", 3072)
            run("va", 2, "w_in", 2048)
            run("vr", 4, "w_in", 5120)
            with sp.Fori(0, 8) as i:
                wide(base["ga"] + i, "w_in", 9216 + i * 512)
            run("gr", 4, "w_in", 7168)
            for j in range(2):
                tall(base["oa"] + j, "w_o_attn", 0, j * CHUNK)
            run("or", 4, "w_o_ret", 0)
            run("out", 4, "w_out", 0)
            feed_in("ff", "w_ffn_in")
            feed_out("fo", "w_ffn_out")
            run("gqk", 2, "w_in_2", 0)
            run("dqk", 4, "w_in_2", 3088)
            wide(base["al"], "w_in_2", 3072, P)
            run("gv", 2, "w_in_2", 1024)
            run("gg", 2, "w_in_2", 2048)
            run("dv", 2, "w_in_2", 5136)
            for n in range(4):
                tall(base["o2"] + n, "w_o_2", 8 * (n // 2), n % 2 * CHUNK)
            feed_in("ff2", "w_ffn_in_2")
            feed_out("fo2", "w_ffn_out_2")
            y_rows = out.rearrange("b (t p) n -> p (b t) n", p=P)
            for q in range(4):
                sp.wait_ge(S("y_ready"), q + 1)
                sp.dma_start(y_rows[:, :, q * 512:q * 512 + 512], resid[:, :, q * 512:q * 512 + 512]).then_inc(S("stored"), 16)
            sp.wait_ge(S("stored"), 64)

        @block.tensor
        def _(pe):
            def nothing(c):
                pass

            def acc_free(blk, all_of_them=False):
                if isinstance(blk, int) and blk == 0:
                    return
                pe.wait_ge(acc_freed, blk + 1 if all_of_them else blk)

            def chunk_ready(blk, c, turned, upto):
                if turned is not None:
                    pe.wait_ge(turned, upto)
                pe.wait_ge(lo_ready, blk * CPB + c + 1)

            def cols_block(blk, par, turned=None, side=nothing, whole=False, tiles=4):
                if whole is not None:
                    acc_free(blk, whole)
                side(-1)
                for c in range(CPB):
                    chunk_ready(blk, c, turned, c + 1)
                    for k2 in range(2):
                        kt = 2 * c + k2
                        for ft in range(tiles):
                            acc = ps[:, 4 * par + ft, :]
                            f = slice(k2 * 512 + ft * P, k2 * 512 + ft * P + P)
                            pe.matmul(acc, whi[:, c % SLOTS, f], hT[:, kt, :, :], start=(kt == 0), stop=False)
                            mm = pe.matmul(acc[:, 0:SEQ], wlo[:, c % SLOTS, f], hT[:, kt, 0, :], start=False,
                                           stop=(kt == KT - 1))
                    mm.then_inc(split_used, 1)
                    side(c)

            def rows_mm(acc, x, t, c, f, start, stop):
                hi, lo = x[:, 0, t * P:t * P + P], x[:, 1, t * P:t * P + P]
                pe.matmul(acc, hi, whi[:, c % SLOTS, f], start=start, stop=False)
                pe.matmul(acc, hi, wlo[:, c % SLOTS, f], start=False, stop=False)
                return pe.matmul(acc, lo, whi[:, c % SLOTS, f], start=False, stop=stop)

            def rows_block(blk, par, turned=None, side=nothing, whole=False, x=lambda kt: hT[:, kt, :, :]):
                acc_free(blk, whole)
                side(-1)
                for c in range(CPB):
                    chunk_ready(blk, c, turned, c + 1)
                    for k2 in range(2):
                        kt = 2 * c + k2
                        for t in range(NT):
                            mm = rows_mm(ps[:, 2 * par + t, :], x(kt), t, c,
                                         slice(k2 * 512, k2 * 512 + 512), kt == 0, kt == KT - 1)
                    mm.then_inc(split_used, 1)
                    side(c)

            def tall_block(blk, bank, x, side=nothing, turned=None, turned0=0, free=None, whole=True):
                side(-1)
                if free is None:
                    acc_free(blk, whole)
                for c in range(CPB):
                    chunk_ready(blk, c, turned, turned0 + c // 2 + 1)
                    for hc in range(2):
                        if free is not None and c == 0:
                            free(hc)
                        for t in range(NT):
                            mm = rows_mm(ps[:, bank + 2 * hc + t, :], x(c), t, c,
                                         slice(hc * 512, hc * 512 + 512), c == 0, c == CPB - 1)
                    mm.then_inc(split_used, 1)
                    side(c)

            def pairs(name, n, form, side=None, first_side=None, turned=None, whole=True):
                b, start = base[name], 0
                if first_side is not None:
                    form(b, 0, turned=turned, side=first_side, whole=whole)
                    form(b + 1, 1)
                    start = 1
                if start < n // 2:
                    with pe.Fori(start, n // 2) as i:
                        for par in range(2):
                            form(b + 2 * i + par, par, side=(lambda c: side(c, 2 * i + par)) if side else nothing)

            def turn_group(u, src, j, bank, rows, evicted=0):
                pe.wait_ge(S(f"{'norm_in' if u in LATE else 'rows'}{u}"), rows)
                if evicted:
                    pe.wait_ge(S(f"turned{u}"), evicted)
                for k2 in range(2):
                    for t in range(NT):
                        mm = pe.transpose(ps[:, bank, k2 * SEQ + t * P:k2 * SEQ + t * P + P],
                                          src[:, t, (2 * j + k2) * P:(2 * j + k2 + 1) * P], ident)
                mm.then_inc(S(f"turn{u}"), 1)

            def turn_ahead(u, src, done=0):
                def side(c):
                    for j in ((0, 1) if c < 0 else (c + 2,)):
                        if done <= j < KT // 2:
                            turn_group(u, src, j, 4 + j % 4, j // 2 + 1, max(0, j - 3))
                    if u in LATE and c == CPB - 1:
                        pe.wait_ge(S(f"diag{u}"), 1)
                        pe.matmul(ps[:, 4, 0:SEQ], ones, scale_diag, start=True, stop=True).then_inc(S(f"scale{u}"), 1)
                        pe.wait_ge(S(f"scaled{u}"), 1)
                return side

            pe.wait_ge(S("first_in"), 16)
            pe.wait_ge(S("gains_in"), 16 * 6)
            pe.wait_ge(S("lambdas_in"), 16 * 4)
            pe.transpose(ps[:, 0, 0:GAIN_ROWS], g_rows[0:GAIN_ROWS, 0, :], ident[0:GAIN_ROWS, 0:GAIN_ROWS])\
                .then_inc(S("gain_t"), 1)
            pe.wait_ge(S("gain_ok"), 1)

            pairs("qk", 4, cols_block, first_side=turn_ahead(0, resid), turned=S("turned0"))
            pairs("qkr", 4, cols_block)
            s1, qst, pT, on = temp[:, 0:512], temp[:, 512:768], temp[:, 1024:1536], temp[:, 1536:1792]

            def head_sum(h, bank):
                pe.wait_ge(S("a_sq"), h + 1)
                pe.matmul(ps[:, bank, :], ones, head_sq, start=True, stop=True).then_inc(S("a_ss"), 1)

            def head_norms(pos):
                if pos == 0:
                    pe.wait_ge(acc_freed, base["va"] + 1)
                if pos % 4 == 1:
                    head_sum(pos // 4, 4)
                if pos == 1:
                    pe.wait_ge(S("conv_in"), 48)
                    for n in range(2):
                        mm = pe.transpose(ps[:, 5 + n, 0:half_conv], g_rows[0:half_conv, 1 + n, :], ident[0:half_conv, 0:half_conv])
                    mm.then_inc(S("conv_t"), 1)
                    pe.wait_ge(S("lam_prod"), 1)
                    pe.matmul(ps[:, 7, 0:2], ones, lamprod, start=True, stop=True).then_inc(S("lam_sum"), 1)

            for n in range(2):
                rows_block(base["va"] + n, n, side=lambda c: head_norms(8 * n + c) if c >= 0 else None)

            def attention(c, h):
                if c == 0:
                    pe.wait_ge(S("a_q"), h + 1)
                    for t in range(NT):
                        mm = pe.matmul(ps[:, 5, t * SEQ:t * SEQ + SEQ], qst[:, t * P:t * P + P], tiles_a[:, bass.ds(8 + h, 1), :],
                                       start=True, stop=True)
                    mm.then_inc(S("a_score"), 1)
                if c == 2:
                    pe.wait_ge(S("a_exp"), h + 1)
                    for kt, t in ((0, 0), (0, 1), (1, 1)):
                        mm = pe.transpose(ps[:, 6, kt * SEQ + t * P:kt * SEQ + t * P + P],
                                          s1[:, t * SEQ + kt * P:t * SEQ + kt * P + P], ident)
                    mm.then_inc(S("a_turn"), 1)
                if c == 3:
                    pe.wait_ge(S("a_pT"), h + 1)
                    v = [va[:, kt, bass.ds(h * P, P)] for kt in range(NT)]
                    pe.matmul(ps[:, 7, 0:P], pT[:, 0:P], v[0], start=True, stop=True)
                    pe.matmul(ps[:, 7, P:2 * P], pT[:, P:2 * P], v[0], start=True, stop=False)
                    pe.matmul(ps[:, 7, P:2 * P], pT[:, SEQ + P:2 * SEQ], v[1], start=False, stop=True)\
                        .then_inc(S("a_o"), 1)
                if c == 4:
                    pe.wait_ge(S("a_on"), h + 1)
                    for t in range(NT):
                        mm = pe.transpose(ps[:, 4, t * P:t * P + P], on[:, t * P:t * P + P], ident)
                    mm.then_inc(S("a_oT"), 1)
                if c == 7:
                    pe.wait_ge(S("a_done"), h + 1)

            def attention_and_norm(c, h):
                attention(c, h)
                if c == 5:
                    head_sum(h + HOSTED, 6)

            pairs("vr", 4, rows_block, side=attention_and_norm)
            pairs("ga", 4, rows_block, side=lambda c, i: attention(c, 4 + i))

            kst, aT = temp[:, 0:512], temp[:, 512:1024]

            def retention(c, h):
                if c == 0:
                    pe.wait_ge(S("r_k"), h + 1)
                    for jt in range(NT):
                        for d in range(2):
                            mm = pe.matmul(ps[:, 4, jt * SEQ:jt * SEQ + SEQ], kst[:, d * SEQ + jt * P:d * SEQ + jt * P + P],
                                           tiles_b[:, bass.ds(2 * h + d, 1), :], start=(d == 0), stop=(d == 1))
                    mm.then_inc(S("r_score"), 1)
                if c == 2:
                    pe.wait_ge(S("r_a"), h + 1)
                    v = [rows_c[:, jt, bass.ds(h * 512, 512)] for jt in range(NT)]
                    pe.matmul(ps[:, 6, :], aT[:, 0:P], v[0], start=True, stop=True)
                    pe.matmul(ps[:, 7, :], aT[:, P:SEQ], v[0], start=True, stop=False)
                    pe.matmul(ps[:, 7, :], aT[:, SEQ + P:2 * SEQ], v[1], start=False, stop=True).then_inc(S("r_o"), 1)
                if c == 7:
                    pe.wait_ge(S("r_done"), h + 1)

            pairs("gb", 4, rows_block, side=retention)
            pairs("gr", 4, rows_block)

            def turn_ret(c):
                if 1 <= c <= 4:
                    for j in (2 * c - 2, 2 * c - 1):
                        turn_group(1, resid, j, 4 + j % 4, 1, max(0, j - 3))

            tall_block(base["oa"], 0, lambda c: oaT[:, c, :, :], side=turn_ret)
            pe.wait_ge(S("turned1"), KT // 2)
            tall_block(base["oa"] + 1, 4, lambda c: oaT[:, c, :, :], whole=False)

            for n in range(4):
                def turn_merged(c):
                    if c == 0 and n == 1:
                        pe.wait_ge(acc_freed, base["or"] + 1)
                    if n in (1, 2) and c in (1, 2):
                        j = 2 * (n - 1) + c - 1
                        turn_group(2, rows_d, j, 4 + j % 4, n)
                rows_block(base["or"] + n, n % 2, side=turn_merged)

            def turn_rest(c):
                if c in (0, 1):
                    for j in (2 * c + 4, 2 * c + 5):
                        turn_group(2, rows_d, j, 4 + j % 4, 3 + c, j - 3)

            def merged(kt):
                return oaT[:, kt, :, :] if kt < 8 else hT[:, kt, :, :]

            for n in range(4):
                def out_side(c):
                    if n == 0:
                        turn_rest(c)
                    if n >= 2 and c == 1:
                        for j in (2 * n - 4, 2 * n - 3):
                            turn_group(3, resid, j, 4 + j, n - 1)
                rows_block(base["out"] + n, n % 2, turned=None if n else S("turned2"), side=out_side, x=merged)

            def feed_out(name, u, last_side=nothing):
                b = base[name]

                def one(i, blk, buf, start, stop):
                    pe.wait_ge(S(f"staged{u}"), i + 1)
                    for c in range(CPB):
                        if start and c == 0:
                            pe.wait_ge(acc_freed, b)
                        if start and c == 4:
                            pe.wait_ge(acc_freed, b + 1)
                        chunk_ready(blk, c, None, 0)
                        k = c % 4
                        for hc in range(2):
                            for t in range(NT):
                                mm = rows_mm(ps[:, 4 * (c // 4) + 2 * hc + t, :], staged[:, buf, k, :, :], t, c,
                                             slice(hc * 512, hc * 512 + 512), start and k == 0, stop and k == 3)
                        mm.then_inc(split_used, 1)
                        if stop:
                            last_side(c)

                one(0, b, 0, True, False)
                with pe.Fori(0, (FBLK - 3) // 2) as i:
                    one(2 * i + 1, b + 2 * i + 1, 1, False, False)
                    one(2 * i + 2, b + 2 * i + 2, 0, False, False)
                one(FBLK - 2, b + FBLK - 2, 1, False, False)
                one(FBLK - 1, b + FBLK - 1, 0, False, True)

            pairs("ff", 2 * FBLK, cols_block, first_side=turn_ahead(3, resid, 4), turned=S("turned3"))

            def turn_first(c):
                if c in (4, 5):
                    for j in (2 * c - 8, 2 * c - 7):
                        turn_group(4, resid, j, j, c - 3)

            feed_out("fo", 0, turn_first)

            pe.wait_ge(S("turned4"), KT // 4)
            pairs("gqk", 2, cols_block, first_side=turn_ahead(4, resid, 4), turned=S("turned4"), whole=None)
            pairs("dqk", 4, cols_block)
            cols_block(base["al"], 0, tiles=1)
            gaT = temp[0:16, 0:SEQ]

            def low_rank(c):
                if c == 0:
                    pe.wait_ge(S("g_ga"), 1)
                    pe.wait_ge(S("alpha_in"), 32)
                    for t in range(NT):
                        pe.matmul(ps[:, 6 + t, :], gaT[:, t * P:t * P + P], area_g[0:16, 0:512], start=True, stop=False)
                        mm = pe.matmul(ps[:, 6 + t, :], ones[0:1, :], area_g[0:1, 512:1024], start=False, stop=True)
                    mm.then_inc(S("g_z"), 1)

            for n in range(2):
                rows_block(base["gv"] + n, 1 - n, side=low_rank if n else nothing)

            ke, qe = area_g[:, 0:LW], area_g[:, LW:2 * LW]
            sT, cross, la_h = temp[:, 0:512], temp[:, 512:768], temp[:, 768:1024]

            def linear_attention(c, h):
                if c in (0, 3):
                    t = c // 3
                    if t == 0:
                        pe.wait_ge(S("g_la"), h + 1)
                    else:
                        pe.wait_ge(S("g_sT"), 3 * h + 1)
                    la = la_h[:, t * P:t * P + P]
                    for n in range(2):
                        pe.matmul(ps[:, 4 + n, :], la, sums_m[:, n * 512:n * 512 + 512], start=True, stop=True)
                    pe.matmul(ps[:, 6, 0:P], la, sums_m[:, LW + t * P:LW + t * P + P], start=True, stop=True)\
                        .then_inc(S("g_sum"), 1)
                if c in (2, 5):
                    t = c // 3
                    pe.wait_ge(S("g_q"), 2 * h + t + 1)
                    pe.wait_ge(S("g_k"), 2 * h + t + 1)
                    for n in range(LEVELS):
                        mm = pe.matmul(ps[:, 4 + n // 4, n % 4 * P:n % 4 * P + P], ke[:, n * P:n * P + P],
                                       qe[:, n * P:n * P + P], start=True, stop=True)
                    mm.then_inc(S("g_score"), 1)
                    if t == 1:
                        pe.matmul(ps[:, 6, P:2 * P], cross[:, 0:P], cross[:, P:2 * P], start=True, stop=True)\
                            .then_inc(S("g_cross"), 1)
                if c == 7:
                    pe.wait_ge(S("g_sT"), 3 * h + 3)
                    v = [gv[:, jt, bass.ds(h * SEQ, SEQ)] for jt in range(NT)]
                    pe.matmul(ps[:, 7, 0:SEQ], sT[:, 0:P], v[0], start=True, stop=True)
                    pe.matmul(ps[:, 7, SEQ:], sT[:, P:SEQ], v[0], start=True, stop=False)
                    pe.matmul(ps[:, 7, SEQ:], sT[:, SEQ + P:], v[1], start=False, stop=True).then_inc(S("g_o"), 1)

            pe.wait_ge(S("second_in"), 16)
            with pe.Fori(0, 2) as i:
                for par in range(2):
                    rows_block(base["gg"] + 2 * i + par, 1 - par, side=lambda c: linear_attention(c, 2 * i + par))

            q_h, diff, dT = temp[:, 512:1024], temp[:, 0:512], temp[:, 1024:1536]

            def at(pos, first):
                h, off = divmod(pos - first, 4)
                return (h,) if off == 0 and 0 <= h < D_HEADS else ()

            def diff_attention(pos):
                if pos == -1:
                    for j, bank in enumerate((6, 4, 5)):
                        turn_group(5, rows_d, j, bank, j + 1)
                if pos == 3:
                    turn_group(5, rows_d, 3, 7, 4)
                for h in at(pos, 4):
                    pe.wait_ge(S("d_p"), h + 1)
                    pe.wait_ge(S("turned5"), max(3, 3 + h))
                    for kt, t in ((0, 0), (0, 1), (1, 1)):
                        mm = pe.transpose(ps[:, 6, kt * SEQ + t * P:kt * SEQ + t * P + P],
                                          diff[:, t * SEQ + kt * P:t * SEQ + kt * P + P], ident)
                    mm.then_inc(S("d_turn"), 1)
                for h in at(pos, 0):
                    pe.wait_ge(S("d_q"), h + 1)
                    pe.wait_ge(S("turned5"), 3)
                    for c in range(2):
                        for t in range(NT):
                            mm = pe.matmul(ps[:, 4 + c, t * SEQ:t * SEQ + SEQ], q_h[:, c * SEQ + t * P:c * SEQ + t * P + P],
                                           tiles_a[:, 8 + 2 * h + c, :], start=True, stop=True)
                    mm.then_inc(S("d_score"), 1)
                for h in at(pos, 5):
                    pe.wait_ge(S("d_pT"), h + 1)
                    pe.wait_ge(S("turned5"), 4)
                    pe.wait_ge(S("rows5"), 4 + h)
                    v = [dv[:, kt, h * SEQ:(h + 1) * SEQ] for kt in range(NT)]
                    pe.matmul(ps[:, 7, 0:SEQ], dT[:, 0:P], v[0], start=True, stop=True)
                    pe.matmul(ps[:, 7, SEQ:], dT[:, P:SEQ], v[0], start=True, stop=False)
                    pe.matmul(ps[:, 7, SEQ:], dT[:, SEQ + P:], v[1], start=False, stop=True).then_inc(S("d_o"), 1)
                for h in at(pos, 9):
                    turn_group(5, rows_d, 4 + h, 6, 5 + h)

            def last_kept(n):
                def wait(hc):
                    for kept in ("m_kept0", "m_kept1"):
                        pe.wait_ge(S(kept), 2 * n - 1 + hc)
                return wait

            for n in range(4):
                tall_block(base["o2"] + n, 4 if n == 3 else 0, lambda c: hT[:, 8 * (n // 2) + c, :, :],
                           side=lambda c: diff_attention(8 * n + c) if c >= 0 or n == 0 else None,
                           turned=S("turned5") if n in (0, 2) else None, turned0=4 * (n // 2),
                           free=last_kept(n) if n in (1, 2) else None, whole=(n == 0))

            pairs("ff2", 2 * FBLK, cols_block, first_side=turn_ahead(6, resid), turned=S("turned6"))
            feed_out("fo2", 1)

        @block.scalar
        def _(act):
            own = Chain(act, S("act_own"))

            def nothing(k):
                pass

            def split(blk, c):
                act.wait_ge(loaded[c % SLOTS], 16 * (2 * blk + c // SLOTS + 1))
                if not (isinstance(blk, int) and blk * CPB + c < SLOTS):
                    act.wait_ge(split_used, blk * CPB + c - SLOTS + 1)
                act.activation(whi[:, c % SLOTS, :], raw[:, c % SLOTS, :], ACT.Copy).then_inc(hi_ready, 1)

            def ahead(blk, side=nothing, more=True, hold=False):
                side(-1)
                for k in range(CPB):
                    if k < SLOTS:
                        split(blk, k + SLOTS)
                    elif more and not (hold and k == CPB - 1):
                        split(blk + 1, k - SLOTS)
                    side(k)

            def held(blk):
                split(blk + 1, SLOTS - 1)

            def block_done(blk):
                act.wait_ge(split_used, (blk + 1) * CPB)

            def low_sums(blk, par):
                block_done(blk)
                act.wait_ge(acc_freed, blk + 1)
                act.activation(lo_sum.rearrange("p (f t) -> p f t", f=4), ps[:, 4 * par:4 * par + 4, SEQ:], ACT.Copy)\
                    .then_inc(lo_copied, 1)

            def pairs(name, n, epilogue, side=None, first_side=None):
                b, start = base[name], 0
                if first_side is not None:
                    for par in range(2):
                        ahead(b + par, nothing if par else first_side)
                        epilogue(b + par, par, par)
                    start = 1
                if start < n // 2:
                    with act.Fori(start, n // 2) as i:
                        for par in range(2):
                            ahead(b + 2 * i + par, (lambda k: side(k, 2 * i + par)) if side else nothing)
                            epilogue(b + 2 * i + par, par, 2 * i + par)

            def turn_group(u, j, bank, dst, col0=None):
                act.wait_ge(S(f"turn{u}"), j + 1)
                src = ps[:, bank, :].rearrange("p (k t) -> p k t", k=2)
                if col0 is None:
                    ins = act.activation(dst[:, 2 * j:2 * j + 2, 0, :], src, ACT.Copy)
                else:
                    for k2 in range(2):
                        ins = act.activation(dst[:, 2 * j + k2, 0, :], src[:, k2, :], ACT.Copy,
                                             scale=gains[:, col0 + 2 * j + k2:col0 + 2 * j + k2 + 1])
                ins.then_inc(S(f"turn_hi{u}"), 1)

            def turn_ahead(u, col0, done=0, todo=()):
                def side(k):
                    for j in ((0, 1, 2) if k < 0 else (k + 3,)):
                        if done <= j < KT // 2:
                            turn_group(u, j, 4 + j % 4, hT, col0)
                    if u in LATE:
                        q = k - 1
                        if q in todo:
                            squares(u, resid_cols, q, 512, q + 1)
                        if k == 5:
                            root(u)
                return side

            def squares(u, src, q, width, ready):
                act.wait_ge(S(f"norm_in{u}"), ready)
                for t in range(NT):
                    ins = act.activation(rows_a[:, t, q * width:(q + 1) * width], src(t, q), ACT.Square,
                                         accum_out=parts[:, 4 * t + q:4 * t + q + 1])
                ins.then_inc(S(f"norm_part{u}"), 1)

            def root(u):
                act.wait_ge(S(f"norm_sum{u}"), 1)
                act.activation(sumsq, sumsq, ACT.Sqrt, bias=eps["model"]).then_inc(S(f"norm_sq{u}"), 1)

            def resid_cols(t, q):
                return resid[:, t, q * 512:q * 512 + 512]

            act.sem_inc(S("gate0"), 1)
            act.sem_inc(S("gate1"), 1)
            for name, at in (("norm_mix", 0), ("norm_ffn", 16), ("attn_pre_norm_2", 32), ("ffn_pre_norm_2", 48)):
                act.dma_start(g_rows[at:at + 16, 0, :], a[name].rearrange("l (k d) -> (l k) d", d=P)).then_inc(S("gains_in"), 16)
            for n, name in enumerate(("q_norm", "k_norm")):
                act.dma_start(g_rows[64 + n:65 + n, 0, :], a[name]).then_inc(S("gains_in"), 16)
            split(0, 0)
            act.wait_ge(S("gain_ok"), 1)
            for j in range(2):
                turn_group(0, j, 4 + j, hT, GAIN["mix"])
            for c in range(1, SLOTS):
                split(0, c)
            act.wait_ge(S("eps_ok"), 1)
            pairs("qk", 4, lambda blk, par, i: low_sums(blk, par), first_side=turn_ahead(0, GAIN["mix"], 2, range(4)))
            pairs("qkr", 4, lambda blk, par, i: low_sums(blk, par))

            def late_rows(dst, func):
                def epilogue(blk, par, i):
                    block_done(blk)
                    for t in range(NT):
                        ins = act.activation(dst[:, t, bass.ds(i * 512, 512)], ps[:, 2 * par + t, :], func, scale=late[:, t:t + 1])
                    ins.then_inc(acc_freed, 1)
                return epilogue

            s1, pT = temp[:, 0:512], temp[:, 1024:1536]

            def head_root_of(h, bank, first=False):
                act.wait_ge(S("a_ss"), h + 1)
                if not first:
                    act.wait_ge(S("a_qn"), h)
                act.activation(head_root, ps[:, bank, :], ACT.Sqrt, bias=eps["head"]).then_inc(S("a_root"), 1)

            def head_norms(pos):
                if pos % 4 == 1:
                    head_root_of(pos // 4, 4, pos == 1)
                if pos == 15:
                    act.wait_ge(S("lam_sum"), 1)
                    act.activation(lam, ps[:, 7, 0:2], ACT.Exp).then_inc(S("lam_exp"), 1)

            for n in range(2):
                ahead(base["va"] + n, lambda k: head_norms(8 * n + k) if k >= 0 else None)
                late_rows(va, ACT.Copy)(base["va"] + n, n, n)

            def attention(k, h):
                if k == 1:
                    act.wait_ge(S("a_top"), h + 1)
                    for t in range(NT):
                        ins = act.activation(s1[:, t * SEQ:t * SEQ + SEQ], s1[:, t * SEQ:t * SEQ + SEQ], ACT.Exp,
                                             bias=negtop[:, t:t + 1], scale=A_SCALE, accum_out=total[:, t:t + 1])
                    ins.then_inc(S("a_exp"), 1)
                if k == 2:
                    act.wait_ge(S("a_turn"), h + 1)
                    act.activation(pT[:, 0:SEQ], ps[:, 6, 0:SEQ], ACT.Copy)
                    act.activation(pT[:, SEQ + P:], ps[:, 6, SEQ + P:], ACT.Copy).then_inc(S("a_pT"), 1)
                if k == 4:
                    act.wait_ge(S("a_oT"), h + 1)
                    act.activation(oaT[:, bass.ds(h, 1), 0, :], ps[:, 4, 0:SEQ], ACT.Copy).then_inc(S("a_hi"), 1)

            def attention_and_norm(k, h):
                attention(k, h)
                if k == 5:
                    head_root_of(h + HOSTED, 6)

            pairs("vr", 4, late_rows(rows_c, ACT.Copy), side=attention_and_norm)
            pairs("ga", 4, late_rows(rows_d, ACT.Sigmoid), side=lambda k, i: attention(k, 4 + i))

            def retention(k, h):
                if k == 4:
                    act.wait_ge(S("r_var"), h + 1)
                    act.activation(rstd, mv.rearrange("p (t s) -> p t s", s=2)[:, :, 1], ACT.Sqrt, bias=eps["one"])\
                        .then_inc(S("r_root"), 1)

            pairs("gb", 4, late_rows(rows_a, ACT.Sigmoid), side=retention)

            def silu_in_place(blk, par, i):
                block_done(blk)
                for t in range(NT):
                    acc = ps[:, 2 * par + t, :]
                    ins = act.activation(acc, acc, ACT.Silu, scale=late[:, t:t + 1])
                ins.then_inc(S("silu"), 1)

            pairs("gr", 4, silu_in_place)

            def turn_ret(k):
                if 1 <= k <= 4:
                    for j in (2 * k - 2, 2 * k - 1):
                        turn_group(1, j, 4 + j % 4, hT)

            for j in range(2):
                ahead(base["oa"] + j, nothing if j else turn_ret)
            for n in range(4):
                def turn_merged(k):
                    if n in (1, 2) and k in (1, 2):
                        j = 2 * (n - 1) + k - 1
                        turn_group(2, j, 4 + j % 4, oaT)
                ahead(base["or"] + n, turn_merged)

            def out_side(n):
                def side(k):
                    if n == 0 and k in (0, 1):
                        for j in (2 * k + 4, 2 * k + 5):
                            turn_group(2, j, 4 + j % 4, hT)
                    if n >= 2 and k == 1:
                        for j in (2 * n - 4, 2 * n - 3):
                            turn_group(3, j, 4 + j, hT, GAIN["ffn"])
                    if n and k == 2:
                        squares(3, resid_cols, n - 1, 512, n)
                return side

            for n in range(4):
                ahead(base["out"] + n, out_side(n))

            def stage(u, i, buf):
                act.activation(staged[:, buf, :, 0, :], hidden[:, bass.ds(4 * i, 4), :], ACT.Copy).then_inc(S(f"stage_hi{u}"), 1)

            def first_stage(u):
                def side(k):
                    if k == 4:
                        act.wait_ge(S(f"hidden{u}"), 2)
                        stage(u, 0, 0)
                return side

            def feed_in(name, gate, first_side, stage_u):
                b = base[name]

                def pair(i, side):
                    ahead(b + 2 * i, side)
                    low_sums(b + 2 * i, 0)
                    ahead(b + 2 * i + 1, lambda k: gate(k, i))
                    low_sums(b + 2 * i + 1, 1)

                pair(0, first_side)
                pair(1, first_stage(stage_u))
                with act.Fori(2, FBLK) as i:
                    pair(i, nothing)

            def silu_gate(k, i):
                if k == 1:
                    act.wait_ge(S("gate_sum"), i + 1)
                    act.wait_ge(S("hidden0"), i + 1)
                    act.activation(up_t, gate_t, ACT.Silu).then_inc(S("gate0"), 1)

            def feed_out(name, u, last, last_side):
                b = base[name]

                def one(i, blk, buf):
                    def side(k):
                        if k == SLOTS - 1:
                            act.wait_ge(split_used, blk * CPB)
                            stage(u, i + 1, 1 - buf)
                    ahead(blk, side)

                def second_stage(k):
                    if k == SLOTS - 1:
                        act.wait_ge(S(f"hidden{u}"), FBLK + 1)
                        stage(u, 1, 1)

                ahead(b, second_stage)
                with act.Fori(0, (FBLK - 3) // 2) as i:
                    one(2 * i + 1, b + 2 * i + 1, 1)
                    one(2 * i + 2, b + 2 * i + 2, 0)
                one(FBLK - 2, b + FBLK - 2, 1)
                ahead(b + FBLK - 1, last_side, not last)

            def turn_first(k):
                if k in (4, 5):
                    for j in (2 * k - 8, 2 * k - 7):
                        turn_group(4, j, j, hT, GAIN["pre2"])
                    squares(4, resid_cols, k - 4, 512, k - 3)

            feed_in("ff", silu_gate, turn_ahead(3, GAIN["ffn"], 4, (3,)), 0)
            feed_out("fo", 0, False, turn_first)

            pairs("gqk", 2, lambda blk, par, i: low_sums(blk, par), first_side=turn_ahead(4, GAIN["pre2"], 4, (2, 3)))
            pairs("dqk", 4, lambda blk, par, i: low_sums(blk, par))
            blk = base["al"]
            ahead(blk)
            block_done(blk)
            act.wait_ge(acc_freed, blk + 1)
            act.activation(lo_sum[0:16, 0:SEQ], ps[0:16, 0, SEQ:], ACT.Copy).then_inc(lo_copied, 1)

            z_abs = free_c[:, 0:1024]

            def low_rank(k):
                if k == 0:
                    act.wait_ge(S("g_z"), 1)
                    own(act.activation(z_abs.rearrange("p (t n) -> p t n", t=NT), ps[:, 6:8, :], ACT.Abs))
                if k == 1:
                    own(act.activation(z_abs, z_abs, ACT.Exp, scale=-1.0))
                if k == 2:
                    act.activation(z_abs, z_abs, ACT.Ln, bias=unit).then_inc(S("g_ln"), 1)

            for n in range(2):
                ahead(base["gv"] + n, low_rank if n else nothing)
                late_rows(gv, ACT.Copy)(base["gv"] + n, 1 - n, n)

            decays = free_c[:, 0:9 * P]
            junk_g = rows_d[:, :, 1024:1024 + SEQ]

            def linear_attention(k, h):
                if k in (0, 3):
                    act.wait_ge(S("g_sum"), 2 * h + k // 3 + 1)
                    act.activation(decays[:, 0:LW].rearrange("p (n c) -> p n c", n=2), ps[:, 4:6, :], ACT.Exp, scale=1.0 / 16)
                    act.activation(decays[:, LW:], ps[:, 6, 0:P], ACT.Exp, scale=1.0 / 16).then_inc(S("g_exp"), 1)

            def norm_heads(done, u, eps_name, ps_rows, junk):
                act.wait_ge(done[0], done[1])
                for t in range(NT):
                    ins = act.activation(junk[:, t, :], ps_rows[:, t * SEQ:t * SEQ + SEQ], ACT.Square,
                                         accum_out=osum[:, t:t + 1])
                own(ins)
                act.activation(osum, osum, ACT.Sqrt, bias=eps[eps_name]).then_inc(S(u), 1)

            def norm_gla(h):
                norm_heads((S("g_o"), h + 1), "g_sq", "gla", ps[:, 7, :], junk_g)

            for section, rows in (("gg", late_rows(rows_d, ACT.Silu)), ("dv", late_rows(dv, ACT.Copy))):
                for n in range(2):
                    h = n + (2 if section == "dv" else 0)
                    def side(k):
                        if k >= 0:
                            linear_attention(k, h)
                        if k == 4 and h:
                            norm_gla(h - 1)
                    ahead(base[section] + n, side)
                    rows(base[section] + n, 1 - n, n)

            dT, s_both = temp[:, 1024:1536], area_g[:, 0:1024]
            junk_t = temp[:, 1536:2048].rearrange("p (t n) -> p t n", t=NT)

            def at(pos, first):
                h, off = divmod(pos - first, 4)
                return (h,) if off == 0 and 0 <= h < D_HEADS else ()

            def diff_attention(pos):
                if pos == -1:
                    for j, bank in enumerate((6, 4, 5)):
                        turn_group(5, j, bank, hT)
                    norm_gla(G_HEADS - 1)
                if pos == 3:
                    turn_group(5, 3, 7, hT)
                for h in at(pos, 4):
                    act.wait_ge(S("d_turn"), h + 1)
                    act.activation(dT[:, 0:SEQ], ps[:, 6, 0:SEQ], ACT.Copy)
                    act.activation(dT[:, SEQ + P:], ps[:, 6, SEQ + P:], ACT.Copy).then_inc(S("d_pT"), 1)
                for h in at(pos, 0):
                    act.wait_ge(S("d_top"), h + 1)
                    for n in range(4):
                        ins = act.activation(s_both[:, n * SEQ:n * SEQ + SEQ], s_both[:, n * SEQ:n * SEQ + SEQ], ACT.Exp,
                                             bias=negtop4[:, n:n + 1], scale=A_SCALE, accum_out=total4[:, n:n + 1])
                    ins.then_inc(S("d_exp"), 1)
                for h in at(pos, 5):
                    norm_heads((S("d_o"), h + 1), "d_sq", "diff", ps[:, 7, :], junk_t)
                for h in at(pos, 9):
                    turn_group(5, 4 + h, 6, hT)

            def m_cols(t, q):
                return rows_m[:, t, q * 512:q * 512 + 512]

            for n in range(4):
                def side(k):
                    if k >= 0 or n == 0:
                        diff_attention(8 * n + k)
                    if n == 3 and k in (1, 2):
                        squares(7, m_cols, k - 1, 512, k)
                ahead(base["o2"] + n, side, hold=(n < 2))
                if n < 2:
                    block_done(base["o2"] + n)
                    for hc in range(2):
                        act.activation(rows_m[:, 0, n * CHUNK + hc * 512:n * CHUNK + hc * 512 + 512], ps[:, 2 * hc, :], ACT.Copy)\
                            .then_inc(S("m_kept0"), 1)
                    held(base["o2"] + n)
            for q in (2, 3):
                squares(7, m_cols, q, 512, q + 1)
            root(7)

            def gelu_gate(k, i):
                if k in (4, 5):
                    if k == 4:
                        act.wait_ge(S("conv_done"), i + 1)
                        act.wait_ge(S("hidden1"), i + 1)
                    for f in (2 * k - 8, 2 * k - 7):
                        ins = act.activation(up_t[:, f * SEQ:f * SEQ + SEQ], gate_t[:, f * SEQ:f * SEQ + SEQ],
                                             ACT.Gelu_apprx_tanh, bias=conv[:, bass.ds(3 * FT + 4 * i + f, 1)])
                    if k == 5:
                        ins.then_inc(S("gate1"), 1)

            def last_squares(half):
                act.wait_ge(split_used, (base["fo2"] + FBLK) * CPB - 4 + 4 * half)
                for q in (2 * half, 2 * half + 1):
                    for t in range(NT):
                        ins = act.activation(rows_d[:, t, q * 512:q * 512 + 512], ps[:, 2 * q + t, :], ACT.Square,
                                             accum_out=parts[:, 4 * t + q:4 * t + q + 1])
                    ins.then_inc(S("norm_part8"), 1)

            feed_in("ff2", gelu_gate, turn_ahead(6, GAIN["ffn2"], 0, range(4)), 1)
            feed_out("fo2", 1, True, lambda k: last_squares(0) if k == SLOTS - 1 else None)
            last_squares(1)
            root(8)

        @block.vector
        def _(dve):
            own = Chain(dve, S("dve_own"))

            def nothing(k):
                pass

            def split(blk, c):
                dve.wait_ge(hi_ready, blk * CPB + c + 1)
                dve.tensor_tensor(wlo[:, c % SLOTS, :], raw[:, c % SLOTS, :], whi[:, c % SLOTS, :].bitcast(F32),
                                  ALU.subtract).then_inc(lo_ready, 1)

            def ahead(blk, side=nothing, more=True, hold=False):
                side(-1)
                for k in range(CPB):
                    if k < SLOTS:
                        split(blk, k + SLOTS)
                    elif more and not (hold and k == CPB - 1):
                        split(blk + 1, k - SLOTS)
                    side(k)

            def held(blk):
                split(blk + 1, SLOTS - 1)

            def block_done(blk):
                dve.wait_ge(split_used, (blk + 1) * CPB)

            def pairs(name, n, epilogue, side=None, first_side=None, per=0):
                b, start = base[name], 0
                if first_side is not None:
                    for par in range(2):
                        ahead(b + par, nothing if par else first_side)
                        epilogue(b + par, par, par)
                    start = 1
                if start < n // 2:
                    with dve.Fori(start, n // 2) as i:
                        own.begin(i - start, 2 * per)
                        for par in range(2):
                            ahead(b + 2 * i + par, (lambda k: side(k, 2 * i + par)) if side else nothing)
                            epilogue(b + 2 * i + par, par, 2 * i + par)
                    own.end(n // 2 - start)

            def add_low(blk, par, nth, dst):
                dve.wait_ge(lo_copied, nth + 1)
                return dve.tensor_tensor(dst, ps[:, 4 * par:4 * par + 4, 0:SEQ], lo_sum.rearrange("p (f t) -> p f t", f=4), ALU.add)

            def turn_group(u, j, bank, dst, col0=None):
                dve.wait_ge(S(f"turn_hi{u}"), j + 1)
                src = ps[:, bank, :].rearrange("p (k t) -> p k t", k=2)
                if col0 is None:
                    ins = dve.tensor_tensor(dst[:, 2 * j:2 * j + 2, 1, :], src, dst[:, 2 * j:2 * j + 2, 0, :].bitcast(F32), ALU.subtract)
                else:
                    for k2 in range(2):
                        kt = 2 * j + k2
                        ins = dve.scalar_tensor_tensor(dst[:, kt, 1, :], src[:, k2, :], gains[:, col0 + kt:col0 + kt + 1],
                                                       dst[:, kt, 0, :].bitcast(F32), ALU.mult, ALU.subtract)
                ins.then_inc(S(f"turned{u}"), 1)

            def turn_ahead(u, col0, done=0, first=nothing):
                def side(k):
                    for j in ((0, 1, 2) if k < 0 else (k + 3,)):
                        first(j)
                        if done <= j < KT // 2:
                            turn_group(u, j, 4 + j % 4, hT, col0)
                    if u in LATE:
                        late_scale(u, k)
                return side

            def late_scale(u, k):
                if k == 5:
                    row_scale(u)
                    own(dve.tensor_scalar(late, rstd, DM ** 0.5, None, ALU.mult))
                    for t in range(NT):
                        ins = dve.tensor_scalar(scale_diag[:, t * P:t * P + P], ident, late[:, t:t + 1], None, ALU.mult)
                    ins.then_inc(S(f"diag{u}"), 1)
                if k == CPB - 1:
                    dve.wait_ge(S(f"scale{u}"), 1)
                    own(dve.tensor_copy(scale_row, ps[:, 4, 0:SEQ]))
                    dve.sem_inc(S(f"scaled{u}"), 1)

            def scaled(x):
                return dve.tensor_tensor(x, x, scale_row.rearrange("p (f t) -> p f t", f=1).to_broadcast([P, 4, SEQ]), ALU.mult)

            def row_scale(u, meanwhile=None):
                dve.wait_ge(S(f"norm_part{u}"), 4)
                dve.tensor_reduce(sumsq, parts.rearrange("p (t q) -> p t q", q=4), AX.X, ALU.add).then_inc(S(f"norm_sum{u}"), 1)
                if meanwhile is not None:
                    meanwhile()
                dve.wait_ge(S(f"norm_sq{u}"), 1)
                own(dve.reciprocal(rstd, sumsq))

            dve.sem_inc(acc_freed, 1)
            for n, width in (("head", P), ("model", DM), ("one", 1), ("diff", SEQ), ("gla", SEQ / A_SCALE ** 2)):
                dve.memset(eps[n], EPS * width)
            dve.memset(unit, 1.0).then_inc(S("eps_ok"), 1)
            for h in range(A_HEADS):
                dve.memset(slopes1[:, h:h + 1], -(2.0 ** -(h + 1)) / A_SCALE)
            for h in range(D_HEADS):
                ins = dve.memset(slopes2[:, h:h + 1], -(2.0 ** (-8.0 * (h + 1) / D_HEADS)) / A_SCALE)
            own(ins)
            dve.wait_ge(S("gain_t"), 1)
            own(dve.tensor_copy(gains[:, :], ps[:, 0, 0:GAIN_ROWS]))
            g_qk = gains[:, GAIN["q"]:GAIN["k"] + 1]
            dve.tensor_scalar(g_qk, g_qk, P ** 0.5, None, ALU.mult).then_inc(S("gain_ok"), 1)
            dve.wait_ge(S("x_in"), 16 * NT)
            dve.sem_inc(S("norm_in0"), 4)
            split(0, 0)
            for j in range(2):
                turn_group(0, j, 4 + j, hT, GAIN["mix"])
            for c in range(1, SLOTS):
                split(0, c)

            def keep_tiles(dst, nth0):
                def epilogue(blk, par, i):
                    tiles = dst[:, bass.ds(4 * i, 4), :]
                    own(add_low(blk, par, nth0 + i, tiles))
                    scaled(tiles).then_inc(acc_freed, 1)
                return epilogue

            def no_epilogue(blk, par, i):
                pass

            s1, on = temp[:, 0:512], temp[:, 1536:1792]

            pairs("qk", 4, keep_tiles(tiles_a, 0), first_side=turn_ahead(0, GAIN["mix"], 2), per=1)
            pairs("qkr", 4, keep_tiles(tiles_b, 4), per=1)
            n_cols = 8

            def head_tiles(h):
                return [tiles_a[:, bass.ds(A_HEADS * n + h, 1), :] for n in range(2)]

            def head_squares(h):
                for n, x in enumerate(head_tiles(h)):
                    ins = dve.tensor_tensor(head_sq[:, n * SEQ:n * SEQ + SEQ].rearrange("p (n t) -> p n t", n=1), x, x, ALU.mult)
                ins.then_inc(S("a_sq"), 1)

            def head_scale(h):
                dve.wait_ge(S("a_root"), h + 1)
                own(dve.reciprocal(head_root, head_root))
                for n, x in enumerate(head_tiles(h)):
                    root = head_root[:, n * SEQ:n * SEQ + SEQ].rearrange("p (n t) -> p n t", n=1)
                    ins = dve.scalar_tensor_tensor(x, x, gains[:, GAIN["q"] + n:GAIN["q"] + n + 1], root, ALU.mult, ALU.mult)
                ins.then_inc(S("a_qn"), 1)

            def head_norms(pos):
                if pos == 0:
                    head_squares(0)
                if pos % 4 == 2:
                    h = pos // 4
                    dve.wait_ge(S("a_root"), h + 1)
                    if h + 1 < HOSTED:
                        head_squares(h + 1)
                    head_scale(h)
                if pos == 2:
                    dve.wait_ge(S("conv_t"), 1)
                    own(dve.tensor_copy(conv[:, :].rearrange("p (n f) -> p n f", n=2), ps[:, 5:7, 0:half_conv]))

            for n in range(2):
                lq, lk = GAIN["lq1"] + 2 * n, GAIN["lk1"] + 2 * n
                ins = dve.tensor_tensor(lamprod[:, n:n + 1], gains[:, lq:lq + 1], gains[:, lk:lk + 1], ALU.mult)
            ins.then_inc(S("lam_prod"), 1)
            dve.wait_ge(acc_freed, base["va"] + 1)
            for n in range(2):
                ahead(base["va"] + n, lambda k: head_norms(8 * n + k) if k >= 0 else None)
            dve.wait_ge(S("dist_in"), 16)
            dve.wait_ge(S("lam_exp"), 1)
            own(dve.tensor_tensor(neglam, lam[:, 1:2], lam[:, 0:1], ALU.subtract))
            own(dve.tensor_scalar(neglam, neglam, -LAMBDA_INIT, None, ALU.add))

            def attention(k, h):
                if k == 0:
                    dve.wait_ge(S("a_score"), h + 1)
                    own(dve.scalar_tensor_tensor(s1, dist, slopes1[:, bass.ds(h, 1)], ps[:, 5, :], ALU.mult, ALU.add))
                    own(dve.tensor_reduce(top, s1.rearrange("p (t k) -> p t k", t=NT), AX.X, ALU.max))
                    dve.tensor_scalar(negtop, top, -A_SCALE, None, ALU.mult).then_inc(S("a_top"), 1)
                if k == 3:
                    dve.wait_ge(S("a_exp"), h + 1)
                    own(dve.reciprocal(recip, total))
                    dve.wait_ge(S("a_o"), h + 1)
                    for t in range(NT):
                        ins = dve.tensor_scalar(on[:, t * P:t * P + P], ps[:, 7, t * P:t * P + P], recip[:, t:t + 1], None, ALU.mult)
                    ins.then_inc(S("a_on"), 1)
                if k == 4:
                    dve.wait_ge(S("a_hi"), h + 1)
                    dve.tensor_tensor(oaT[:, bass.ds(h, 1), 1, :], ps[:, 4, 0:SEQ], oaT[:, bass.ds(h, 1), 0, :].bitcast(F32),
                                      ALU.subtract).then_inc(S("a_done"), 1)

            def attention_and_norm(k, h):
                attention(k, h)
                if k == 4:
                    head_squares(h + HOSTED)
                if k == 6:
                    head_scale(h + HOSTED)

            pairs("vr", 4, no_epilogue, side=attention_and_norm, per=4)
            pairs("ga", 4, no_epilogue, side=lambda k, i: attention(k, 4 + i), per=3)

            aT = temp[:, 512:1024]

            def retention(k, h):
                if k == 0:
                    dve.wait_ge(S("r_score"), h + 1)
                    dve.tensor_tensor(aT, ps[:, 4, :], decay[:, bass.ds(h * 512, 512)], ALU.mult).then_inc(S("r_a"), 1)
                if k == 3:
                    dve.wait_ge(S("r_o"), h + 1)
                    for t in range(NT):
                        ins = dve.bn_stats(bn[:, 6 * t:6 * t + 6], ps[:, 6 + t, :])
                    own(ins)
                    dve.memset(spare, 0.0)
                    for t in range(NT):
                        ins = dve.bn_aggr(mv[:, 2 * t:2 * t + 2], bn[:, 6 * t:6 * t + 6])
                    ins.then_inc(S("r_var"), 1)
                if k == 4:
                    dve.wait_ge(S("r_root"), h + 1)
                    own(dve.reciprocal(rstd, rstd))
                    for t in range(NT):
                        ins = dve.tensor_scalar(resid[:, t, bass.ds(h * 512, 512)], ps[:, 6 + t, :], mv[:, 2 * t:2 * t + 1],
                                                rstd[:, t:t + 1], ALU.subtract, ALU.mult)
                    ins.then_inc(S("r_done"), 1)

            pairs("gb", 4, no_epilogue, side=retention, per=2)

            def times_silu(blk, par, i):
                dve.wait_ge(S("silu"), i + 1)
                o = resid[:, :, bass.ds(i * 512, 512)]
                dve.tensor_tensor(o, o, ps[:, 2 * par:2 * par + 2, :], ALU.mult).then_inc(acc_freed, 1)

            dve.wait_ge(S("r_done"), R_HEADS)
            pairs("gr", 4, times_silu)
            dve.wait_ge(acc_freed, base["oa"] + 1)
            dve.sem_inc(S("rows1"), 1)

            def turn_ret(k):
                if 1 <= k <= 4:
                    for j in (2 * k - 2, 2 * k - 1):
                        turn_group(1, j, 4 + j % 4, hT)

            for j in range(2):
                blk = base["oa"] + j
                ahead(blk, nothing if j else turn_ret)
                block_done(blk)
                for t in range(NT):
                    m = rows_d[:, t, j * CHUNK:(j + 1) * CHUNK].rearrange("p (f n) -> p f n", f=2)
                    acc = ps[:, 4 * j:4 * j + 4, :].rearrange("p (f t) n -> p f t n", t=NT)[:, :, t, :]
                    ins = dve.tensor_tensor(m, m, acc, ALU.mult)
                ins.then_inc(acc_freed, 1)

            dve.wait_ge(acc_freed, base["or"] + 1)
            for n in range(4):
                def turn_merged(k):
                    if n in (1, 2) and k in (1, 2):
                        j = 2 * (n - 1) + k - 1
                        turn_group(2, j, 4 + j % 4, oaT)
                blk, par = base["or"] + n, n % 2
                ahead(blk, turn_merged)
                block_done(blk)
                cs = slice(n * 512, n * 512 + 512)
                own(dve.tensor_tensor(rows_a[:, :, cs], rows_a[:, :, cs], ps[:, 2 * par:2 * par + 2, :], ALU.mult))
                own(dve.tensor_tensor(rows_d[:, :, cs], rows_d[:, :, cs], rows_a[:, :, cs], ALU.add))
                dve.sem_inc(acc_freed, 1)
                dve.sem_inc(S("rows2"), 1)

            def turn_rest(k):
                if k in (0, 1):
                    for j in (2 * k + 4, 2 * k + 5):
                        turn_group(2, j, 4 + j % 4, hT)

            for n in range(4):
                blk, par = base["out"] + n, n % 2

                def out_side(k):
                    if n == 0:
                        turn_rest(k)
                    if n >= 2 and k == 1:
                        for j in (2 * n - 4, 2 * n - 3):
                            turn_group(3, j, 4 + j, hT, GAIN["ffn"])
                ahead(blk, out_side, hold=(n == 3))
                block_done(blk)
                dve.wait_ge(S("x_again"), 16)
                r = resid[:, :, n * 512:n * 512 + 512]
                own(dve.tensor_tensor(r, r, ps[:, 2 * par:2 * par + 2, :], ALU.add))
                dve.sem_inc(acc_freed, 1)
                dve.sem_inc(S("norm_in3"), 1)
            held(base["out"] + 3)

            gate4 = gate_t.rearrange("p (f t) -> p f t", f=4)
            prod_t = area_d[:, 3072:4096].rearrange("p (f t) -> p f t", f=4)

            def stage(u, i, buf):
                dve.wait_ge(S(f"stage_hi{u}"), i + 1)
                dve.tensor_tensor(staged[:, buf, :, 1, :], hidden[:, bass.ds(4 * i, 4), :],
                                  staged[:, buf, :, 0, :].bitcast(F32), ALU.subtract).then_inc(S(f"staged{u}"), 1)

            def feed_in(name, u, first_side, gate_sum, per, side2, n_cols):
                b = base[name]

                def pair(i, side):
                    ahead(b + 2 * i, side)
                    gate_sum(b + 2 * i, i, n_cols + 2 * i)
                    ahead(b + 2 * i + 1, lambda k: side2(k, i))
                    dve.wait_ge(S(f"hidden{u}"), i + 1)
                    own(add_low(b + 2 * i + 1, 1, n_cols + 2 * i + 1, prod_t))
                    scaled(prod_t).then_inc(acc_freed, 1)

                pair(0, first_side)
                pair(1, lambda k: stage(u, 0, 0) if k == 4 else None)
                with dve.Fori(2, FBLK) as i:
                    own.begin(i - 2, per)
                    pair(i, nothing)
                own.end(FBLK - 2)

            def silu_sum(blk, i, nth):
                dve.wait_ge(S("gate0"), i + 1)
                own(add_low(blk, 0, nth, gate4))
                dve.sem_inc(acc_freed, 1)
                own(scaled(gate4))
                dve.sem_inc(S("gate_sum"), 1)

            feed_in("ff", 0, turn_ahead(3, GAIN["ffn"], 4), silu_sum, 3, lambda k, i: None, n_cols)
            n_cols += 2 * FBLK

            def feed_out(name, u, last, last_side):
                b = base[name]

                def one(i, blk, buf):
                    ahead(blk, lambda k: stage(u, i + 1, 1 - buf) if k == SLOTS - 1 else None)

                one(0, b, 0)
                with dve.Fori(0, (FBLK - 3) // 2) as i:
                    one(2 * i + 1, b + 2 * i + 1, 1)
                    one(2 * i + 2, b + 2 * i + 2, 0)
                one(FBLK - 2, b + FBLK - 2, 1)
                ahead(b + FBLK - 1, last_side, not last, hold=True)

            def add_resid(half):
                dve.wait_ge(split_used, (base["fo"] + FBLK) * CPB - 4 + 4 * half)
                for q in (2 * half, 2 * half + 1):
                    for t in range(NT):
                        r = resid[:, t, q * 512:q * 512 + 512]
                        ins = dve.tensor_tensor(r, r, ps[:, 2 * q + t, :], ALU.add)
                    own(ins)
                    dve.sem_inc(S("norm_in4"), 1)

            def turn_first(k):
                if k == SLOTS - 1:
                    add_resid(0)
                if k in (4, 5):
                    for j in (2 * k - 8, 2 * k - 7):
                        turn_group(4, j, j, hT, GAIN["pre2"])

            feed_out("fo", 0, False, turn_first)
            add_resid(1)
            dve.sem_inc(acc_freed, FBLK)
            held(base["fo"] + FBLK - 1)

            pairs("gqk", 2, keep_tiles(tiles_b, n_cols), first_side=turn_ahead(4, GAIN["pre2"], 4), per=1)
            pairs("dqk", 4, keep_tiles(tiles_a, n_cols + 2), per=1)
            n_cols += 6
            ahead(base["al"])
            dve.wait_ge(lo_copied, n_cols + 1)
            own(dve.tensor_tensor(temp[0:16, 0:SEQ], ps[0:16, 0, 0:SEQ], lo_sum[0:16, 0:SEQ], ALU.add))
            own(dve.tensor_tensor(temp[0:16, 0:SEQ], temp[0:16, 0:SEQ], scale_row[0:16, :], ALU.mult))
            dve.sem_inc(acc_freed, 1)
            dve.sem_inc(S("g_ga"), 1)
            n_cols += 1
            log_a = temp[:, 1024:2048]

            def low_rank(k):
                if k == 3:
                    dve.wait_ge(S("g_ln"), 1)
                    dve.scalar_tensor_tensor(log_a.rearrange("p (t n) -> p t n", t=NT), ps[:, 6:8, :], 0.0,
                                             free_c[:, 0:1024].rearrange("p (t n) -> p t n", t=NT),
                                             ALU.min, ALU.subtract).then_inc(S("g_log"), 1)

            for n in range(2):
                ahead(base["gv"] + n, low_rank if n else nothing)

            decays = free_c[:, 0:9 * P]
            qe = area_g[:, LW:2 * LW]
            sT, cross = temp[:, 0:512], temp[:, 512:768]
            lev = decays[:, 0:LW].rearrange("p (n c) -> p n c", c=P)
            gain_g, gain_d = free_c[:, 1280:1536], free_c[:, 1536:1792]
            head_rows = free_c[:, 1792:2048]
            dve.wait_ge(S("second_in"), 16)
            dve.wait_ge(S("norms_in"), 32)
            for n in (gain_g, gain_d):
                dve.tensor_scalar(n, n, SEQ ** 0.5 * (1.0 - LAMBDA_INIT if n is gain_d else 1.0), None, ALU.mult)
            own(dve.memset(sT, 0.0))

            def linear_attention(k, h):
                if k in (0, 3):
                    t = k // 3
                    dve.wait_ge(S("g_exp"), 2 * h + t + 1)
                    key = tiles_b[:, bass.ds(4 + h, 1), t * P:t * P + P]
                    q = tiles_b[:, bass.ds(h, 1), t * P:t * P + P]
                    dve.tensor_tensor(qe.rearrange("p (n c) -> p n c", c=P), lev, q.to_broadcast([P, LEVELS, P]), ALU.mult)
                    ins = dve.tensor_tensor(cross[:, t * P:t * P + P].rearrange("p (n c) -> p n c", n=1),
                                            decays[:, LW:].rearrange("p (n c) -> p n c", n=1), (key, q)[t], ALU.mult)
                    ins.then_inc(S("g_q"), 1)
                if k in (2, 5):
                    t = k // 3
                    dve.wait_ge(S("g_score"), 2 * h + t + 1)
                    own(dve.tensor_tensor(decays[:, 0:LW].rearrange("p (n c) -> p n c", n=2), ps[:, 4:6, :],
                                          masks_m.rearrange("p (n c) -> p n c", n=2), ALU.mult))
                    ins = dve.tensor_reduce(sT[:, t * SEQ + t * P:t * SEQ + t * P + P],
                                            decays[:, 0:LW].rearrange("p (n c) -> p c n", c=P), AX.X, ALU.add)
                    ins.then_inc(S("g_sT"), 1)
                    if t == 1:
                        dve.wait_ge(S("g_cross"), h + 1)
                        dve.tensor_copy(sT[:, P:SEQ], ps[:, 6, P:2 * P]).then_inc(S("g_sT"), 1)

            def head_out(h):
                dve.wait_ge(S("g_sq"), h + 1)
                own(dve.reciprocal(orstd, osum))
                for t in range(NT):
                    own(dve.scalar_tensor_tensor(head_rows, ps[:, 7, t * SEQ:t * SEQ + SEQ], orstd[:, t:t + 1], gain_g,
                                                 ALU.mult, ALU.mult))
                    o = rows_d[:, t, h * SEQ:(h + 1) * SEQ]
                    own(dve.tensor_tensor(o, o, head_rows, ALU.mult))
                dve.sem_inc(S("rows5"), 1)

            for h in range(G_HEADS):
                blk = base["gg"] + h

                def side(k):
                    if k >= 0:
                        linear_attention(k, h)
                    if k == 4 and h:
                        head_out(h - 1)
                ahead(blk, side)

            diff, s_both = temp[:, 0:512], area_g[:, 0:1024]

            def at(pos, first):
                h, off = divmod(pos - first, 4)
                return (h,) if off == 0 and 0 <= h < D_HEADS else ()

            def diff_attention(pos):
                if pos == -1:
                    for j, bank in enumerate((6, 4, 5)):
                        turn_group(5, j, bank, hT)
                    head_out(G_HEADS - 1)
                if pos == 3:
                    turn_group(5, 3, 7, hT)
                for h in at(pos, 8):
                    dve.wait_ge(S("d_sq"), h + 1)
                    own(dve.reciprocal(orstd, osum))
                    for t in range(NT):
                        ins = dve.scalar_tensor_tensor(rows_d[:, t, 1024 + h * SEQ:1024 + (h + 1) * SEQ],
                                                       ps[:, 7, t * SEQ:t * SEQ + SEQ], orstd[:, t:t + 1], gain_d, ALU.mult, ALU.mult)
                    ins.then_inc(S("rows5"), 1)
                for h in at(pos, 9):
                    turn_group(5, 4 + h, 6, hT)
                for h in at(pos, 0):
                    dve.wait_ge(S("d_score"), h + 1)
                    for c in range(2):
                        ins = dve.scalar_tensor_tensor(s_both[:, c * 512:c * 512 + 512], dist, slopes2[:, h:h + 1], ps[:, 4 + c, :],
                                                       ALU.mult, ALU.add)
                    own(ins)
                    own(dve.tensor_reduce(top4, s_both.rearrange("p (n k) -> p n k", n=4), AX.X, ALU.max))
                    dve.tensor_scalar(negtop4, top4, -A_SCALE, None, ALU.mult).then_inc(S("d_top"), 1)
                for h in at(pos, 1):
                    dve.wait_ge(S("d_exp"), h + 1)
                    own(dve.reciprocal(recip4, total4))
                    own(dve.tensor_scalar(recip4[:, 2:4], recip4[:, 2:4], neglam, None, ALU.mult))
                    for t in range(NT):
                        ins = dve.tensor_scalar(diff[:, t * SEQ:t * SEQ + SEQ], s_both[:, t * SEQ:t * SEQ + SEQ],
                                                recip4[:, t:t + 1], None, ALU.mult)
                    own(ins)
                    for t in range(NT):
                        ins = dve.scalar_tensor_tensor(diff[:, t * SEQ:t * SEQ + SEQ], s_both[:, 512 + t * SEQ:512 + t * SEQ + SEQ],
                                                       recip4[:, 2 + t:3 + t], diff[:, t * SEQ:t * SEQ + SEQ], ALU.mult, ALU.add)
                    ins.then_inc(S("d_p"), 1)

            def row_gain(q):
                return area_g[:, q * 512:q * 512 + 512].rearrange("p (t n) -> p t n", t=1).to_broadcast([P, NT, 512])

            def m_gain(q):
                dve.wait_ge(S("norm_part7"), q + 1)
                m = rows_m[:, :, q * 512:q * 512 + 512]
                own(dve.tensor_tensor(m, m, row_gain(q), ALU.mult))

            def o2_side(n):
                def side(k):
                    if k >= 0 or n == 0:
                        diff_attention(8 * n + k)
                    if n == 3 and k in (4, 5):
                        if k == 4:
                            dve.wait_ge(S("post_in"), 16)
                        m_gain(k - 4)
                return side

            for n in range(4):
                blk, bank, j = base["o2"] + n, 4 if n == 3 else 0, n % 2
                ahead(blk, o2_side(n), hold=(n != 2))
                block_done(blk)
                for hc in range(2):
                    cs = slice(j * CHUNK + hc * 512, j * CHUNK + hc * 512 + 512)
                    if n >= 2:
                        m = rows_m[:, :, cs]
                        dve.tensor_tensor(m, m, ps[:, bank + 2 * hc:bank + 2 * hc + 2, :], ALU.add).then_inc(S("norm_in7"), 1)
                    else:
                        dve.tensor_copy(rows_m[:, 1, cs], ps[:, bank + 2 * hc + 1, :]).then_inc(S("m_kept1"), 1)
                if n < 2:
                    dve.wait_ge(S("m_kept0"), 2 * n + 2)
                else:
                    dve.wait_ge(S("norm_in7"), 2 * n - 2)
                dve.sem_inc(acc_freed, 1)
                if n != 2:
                    held(blk)

            def scale_rows():
                own(dve.tensor_scalar(rstd, rstd, DM ** 0.5, None, ALU.mult))

            own(dve.memset(conv_in[:, :, 0:2], 0.0))
            row_scale(7)
            scale_rows()

            def post_norm(j):
                before = {0: 0, 2: 1, 3: 2, 4: 3}
                if j not in before:
                    return
                q = before[j]
                if q >= 2:
                    m_gain(q)
                cs = slice(q * 512, q * 512 + 512)
                for t in range(NT):
                    ins = dve.scalar_tensor_tensor(resid[:, t, cs], rows_m[:, t, cs], rstd[:, t:t + 1], resid[:, t, cs], ALU.mult, ALU.add)
                ins.then_inc(S("norm_in6"), 1)

            def conv_sum(blk, i, nth):
                own(add_low(blk, 0, nth, conv_in[:, :, 2:]))
                dve.sem_inc(acc_freed, 1)
                own(scaled(conv_in[:, :, 2:]))

            def convolve(tap, i):
                if not 0 <= tap < 3:
                    return
                if tap == 0:
                    dve.wait_ge(S("gate1"), i + 1)
                for f in range(4):
                    src = conv_in[:, f, tap:tap + SEQ]
                    w = conv[:, bass.ds(tap * FT + 4 * i + f, 1)]
                    dst = gate_t[:, f * SEQ:f * SEQ + SEQ]
                    if tap == 0:
                        ins = dve.tensor_scalar(dst, src, w, None, ALU.mult)
                    else:
                        ins = dve.scalar_tensor_tensor(dst, src, w, dst, ALU.mult, ALU.add)
                if tap < 2:
                    own(ins)
                else:
                    ins.then_inc(S("conv_done"), 1)

            feed_in("ff2", 1, turn_ahead(6, GAIN["ffn2"], 0, post_norm), conv_sum, 5, convolve, n_cols)

            def out_gain(q):
                dve.wait_ge(S("norm_part8"), q + 1)
                own(dve.tensor_tensor(rows_a[:, :, q * 512:q * 512 + 512], ps[:, 2 * q:2 * q + 2, :], row_gain(q), ALU.mult))

            def out_gains(k):
                if k == 4:
                    dve.wait_ge(S("post_in2"), 16)
                    out_gain(0)
                    out_gain(1)

            feed_out("fo2", 1, True, out_gains)
            row_scale(8, lambda: out_gain(2))
            scale_rows()
            for q in range(4):
                if q == 3:
                    out_gain(q)
                cs = slice(q * 512, q * 512 + 512)
                for t in range(NT):
                    ins = dve.scalar_tensor_tensor(resid[:, t, cs], rows_a[:, t, cs], rstd[:, t:t + 1], resid[:, t, cs], ALU.mult, ALU.add)
                ins.then_inc(S("y_ready"), 1)

        @block.gpsimd
        def _(pool):
            pool.sem_inc(S("hidden0"), 1)
            pool.sem_inc(S("hidden1"), 1)
            for n, name in enumerate(("lambda_q1_2", "lambda_k1_2", "lambda_q2_2", "lambda_k2_2")):
                pool.dma_start(g_rows[66 + n:67 + n, 0, :], a[name]).then_inc(S("lambdas_in"), 16)
            taps = a["conv_w_2"].rearrange("l w (f d) -> (l w f) d", d=P)
            pool.dma_start(g_rows[0:half_conv, 1, :], taps[0:half_conv, :]).then_inc(S("conv_in"), 16)
            pool.dma_start(g_rows[0:half_conv // 2, 2, :], taps[half_conv:, :]).then_inc(S("conv_in"), 16)
            pool.dma_start(g_rows[half_conv // 2:half_conv, 2, :], a["conv_b_2"].rearrange("l (f d) -> (l f) d", d=P))\
                .then_inc(S("conv_in"), 16)
            pool.dma_start(dist, c_first[:, 2 * P:]).then_inc(S("dist_in"), 16)
            pool.dma_start(masks[:, 0:R_HEADS * NT * SEQ], c_decay).then_inc(S("decay_in"), 16)

            q_st = temp[:, 512:768].rearrange("p (n t) -> p n t", n=1)
            pool.wait_ge(S("a_qn"), 1)
            pool.tensor_copy(q_st, tiles_a[:, 0:1, :]).then_inc(S("a_q"), 1)
            with pool.Fori(1, A_HEADS) as h:
                pool.wait_ge(S("a_qn"), h + 1)
                pool.wait_ge(S("a_score"), h)
                pool.tensor_copy(q_st, tiles_a[:, bass.ds(h, 1), :]).then_inc(S("a_q"), 1)

            kst = temp[:, 0:512].rearrange("p (d t) -> p d t", d=2)
            pool.wait_ge(S("a_done"), A_HEADS)
            pool.wait_ge(S("decay_in"), 16)
            pool.tensor_copy(kst, tiles_b[:, 8:10, :]).then_inc(S("r_k"), 1)
            with pool.Fori(1, R_HEADS) as h:
                pool.wait_ge(S("r_score"), h)
                pool.tensor_copy(kst, tiles_b[:, bass.ds(8 + 2 * h, 2), :]).then_inc(S("r_k"), 1)
            pool.wait_ge(S("r_done"), R_HEADS)
            pool.dma_start(masks[:, :], c_second).then_inc(S("second_in"), 16)
            pool.wait_ge(S("turned1"), KT // 2)
            pool.dma_start(resid[:, :, :], x_rows).then_inc(S("x_again"), 16)

            prod = area_d[:, 3072:4096].rearrange("p (f t) -> p f t", f=4)
            up4 = up_t.rearrange("p (f t) -> p f t", f=4)

            def hidden_of(u, name):
                with pool.Fori(0, FBLK) as i:
                    pool.wait_ge(S(f"gate{u}"), i + 2)
                    pool.wait_ge(acc_freed, base[name] + 2 * i + 3)
                    pool.tensor_tensor(hidden[:, bass.ds(4 * i, 4), :], up4, prod, ALU.mult).then_inc(S(f"hidden{u}"), 1)

            hidden_of(0, "ff")
            pool.dma_start(area_g[0:16, 0:512], a["w_alpha_up_2"].rearrange("l k n -> (l k) n")).then_inc(S("alpha_in"), 16)
            pool.dma_start(area_g[0:1, 512:1024], a["b_alpha_2"]).then_inc(S("alpha_in"), 16)
            pool.wait_ge(S("staged0"), FBLK)
            for n, name in enumerate(("gla_norm_2", "diff_norm_2")):
                pool.dma_start(free_c[:, 1280 + n * SEQ:1280 + (n + 1) * SEQ], a[name].to_broadcast([P, SEQ])).then_inc(S("norms_in"), 16)
            la = temp[:, 1024:2048].rearrange("p (t n) -> p t n", t=NT)
            lev = free_c[:, 0:LW].rearrange("p (n c) -> p n c", c=P)
            ke = area_g[:, 0:LW].rearrange("p (n c) -> p n c", c=P)
            pool.wait_ge(S("g_log"), 1)

            def linear_attention(h):
                pool.tensor_copy(temp[:, 768:1024].rearrange("p (t n) -> p t n", t=NT), la[:, :, bass.ds(h * P, P)])\
                    .then_inc(S("g_la"), 1)
                for t in range(NT):
                    pool.wait_ge(S("g_exp"), 2 * h + t + 1)
                    pool.tensor_tensor(ke, lev, tiles_b[:, bass.ds(4 + h, 1), t * P:t * P + P].to_broadcast([P, LEVELS, P]), ALU.mult)\
                        .then_inc(S("g_k"), 1)

            linear_attention(0)
            with pool.Fori(1, G_HEADS) as h:
                pool.wait_ge(S("g_sum"), 2 * h)
                linear_attention(h)
            pool.wait_ge(S("g_cross"), G_HEADS)
            q_d = temp[:, 512:1024].rearrange("p (n t) -> p n t", n=2)
            for h in range(D_HEADS):
                if h:
                    pool.wait_ge(S("d_score"), h)
                pool.tensor_copy(q_d, tiles_a[:, 2 * h:2 * h + 2, :]).then_inc(S("d_q"), 1)
            pool.wait_ge(S("d_p"), D_HEADS)
            pool.dma_start(area_g[:, :], a["attn_post_norm_2"].to_broadcast([P, DM])).then_inc(S("post_in"), 16)
            pool.wait_ge(S("norm_in6"), 4)
            pool.dma_start(area_g[:, :], a["ffn_post_norm_2"].to_broadcast([P, DM])).then_inc(S("post_in2"), 16)
            hidden_of(1, "ff2")


_INS = ["x", "w_in", "w_o_attn", "w_o_ret", "w_out", "q_norm", "k_norm", "norm_mix", "norm_ffn", "w_ffn_in", "w_ffn_out",
        "attn_pre_norm_2", "w_in_2", "w_alpha_up_2", "b_alpha_2", "gla_norm_2", "lambda_q1_2", "lambda_k1_2",
        "lambda_q2_2", "lambda_k2_2", "diff_norm_2", "w_o_2", "attn_post_norm_2", "ffn_pre_norm_2", "w_ffn_in_2",
        "conv_w_2", "conv_b_2", "w_ffn_out_2", "ffn_post_norm_2"]


def kernel(**inputs):
    import concourse.bacc as bacc
    from concourse.bass_utils import run_bass_kernel_spmd

    nc = bacc.Bacc("TRN2", target_bir_lowering=False, num_devices=1)
    arrays, aps = {}, {}
    for name in _INS:
        arrays[name] = np.ascontiguousarray(inputs[name])
        aps[name] = nc.dram_tensor(name, arrays[name].shape, F32, kind="ExternalInput").ap()
    consts = []
    for name, value in zip(("shape_first", "shape_decay", "shape_second"), shape_constants()):
        arrays[name] = np.ascontiguousarray(value)
        consts.append(nc.dram_tensor(name, value.shape, F32, kind="ExternalInput").ap())
    out = nc.dram_tensor("y", (1, SEQ, DM), F32, kind="ExternalOutput").ap()
    two_blocks(nc, aps, out, *consts)
    r = run_bass_kernel_spmd(nc, [arrays], core_ids=[0])
    return r.results[0]["y"]
```
